# Optimizing a Trainium2 kernel written in Bass

```python
import jax, jax.numpy as jnp
from jax import lax
import numpy as np

D_MODEL = 1024
BATCH = 1
SEQ = 1024
DEPTH = 2

GRID_W = 64
CTX_LEN = 256
N_EVEN = (DEPTH + 1) // 2
N_ODD = DEPTH // 2
N_MOD = 6
EPS = 1e-6

POOL_WINDOWS = (2, 4, 8, 16)
N_POOL = 4
POOL_GROUP = 3 * D_MODEL // 16
POOL_WIDTH = N_POOL * POOL_GROUP
FOURIER_WIDTH = D_MODEL // 4
AB_WIDTH = POOL_WIDTH + FOURIER_WIDTH

HEAD_DIM = 64
N_Q_HEADS = D_MODEL // 128
N_KV_HEADS = N_Q_HEADS // 4
GQA_GROUP = N_Q_HEADS // N_KV_HEADS
WINDOW = 128
BLOCK = 128
ROPE_THETA = 10000.0
RWKV_HEADS = D_MODEL // 128
RWKV_WIDTH = RWKV_HEADS * HEAD_DIM
DECAY_LORA = 64
AAA_LORA = 64
GATE_LORA = 128
GN_EPS = 64e-5
ATT_WIDTH = N_Q_HEADS * HEAD_DIM
KV_WIDTH = N_KV_HEADS * HEAD_DIM
CD_SIZES = (ATT_WIDTH, KV_WIDTH, KV_WIDTH, 3 * RWKV_WIDTH, DECAY_LORA, AAA_LORA, GATE_LORA)
CD_WIDTH = 2560
CD_OUT = ATT_WIDTH + RWKV_WIDTH

D_FF = 2816

kernel_name = 'hybrid_pool_fourier_swa_rwkv7_dit'

def _rmsnorm(x, g):
    xf = x.astype(jnp.float32)
    y = xf * lax.rsqrt(jnp.mean(xf * xf, axis=-1, keepdims=True) + EPS)
    return (y * g.astype(jnp.float32)).astype(x.dtype)

def _modulate(x, shift, scale):
    return x * (1 + scale) + shift

def _dwconv3(x, w):
    xp = jnp.pad(x, ((0, 0), (1, 1), (0, 0)))
    return xp[:, :-2] * w[0] + xp[:, 1:-1] * w[1] + xp[:, 2:] * w[2]

def _split_sizes(t, sizes):
    out, start = [], 0
    for s in sizes:
        out.append(t[..., start:start + s])
        start += s
    return out

def _pool_minus_self(x, window):
    T = x.shape[1]
    left = window // 2
    right = window - 1 - left
    xf = x.astype(jnp.float32)
    cs = jnp.pad(jnp.cumsum(xf, axis=1), ((0, 0), (1, 0), (0, 0)))
    t = jnp.arange(T)
    lo = jnp.maximum(t - left, 0)
    hi = jnp.minimum(t + right + 1, T)
    mean = (cs[:, hi] - cs[:, lo]) / (hi - lo).astype(jnp.float32)[None, :, None]
    return (mean - xf).astype(x.dtype)

def _ab_mixer(u, w_in, pool_w, pool_scale, fourier_w, w_out):
    B, T, _ = u.shape
    z = u @ w_in
    za, zb = z[..., :POOL_WIDTH], z[..., POOL_WIDTH:]
    groups = jnp.split(za, N_POOL, axis=-1)
    pooled = jnp.stack([_pool_minus_self(g, w) for g, w in zip(groups, POOL_WINDOWS)], axis=2)
    ya = jnp.einsum('btgc,gcd->btgd', pooled, pool_w).reshape(B, T, POOL_WIDTH) * pool_scale
    spec = jnp.fft.fft2(zb.astype(jnp.float32), axes=(1, 2), norm='ortho').real
    yb = spec.astype(z.dtype) @ fourier_w
    return jnp.concatenate([ya, yb], axis=-1) @ w_out

def _axial_rope(x, pos_row, pos_col):
    half = HEAD_DIM // 2
    inv = ROPE_THETA ** (-jnp.arange(0, half, 2, dtype=jnp.float32) / half)
    xf = x.astype(jnp.float32)

    def rot(xs, pos):
        ang = pos.astype(jnp.float32)[:, None] * inv[None, :]
        cos = jnp.cos(ang)[None, :, None, :]
        sin = jnp.sin(ang)[None, :, None, :]
        x1, x2 = xs[..., :half // 2], xs[..., half // 2:]
        return jnp.concatenate([x1 * cos - x2 * sin, x2 * cos + x1 * sin], axis=-1)

    out = jnp.concatenate([rot(xf[..., :half], pos_row), rot(xf[..., half:], pos_col)], axis=-1)
    return out.astype(x.dtype)

def _sink_attend(q, ks, vs, masks, sink):
    B, Q, HK, G, _ = q.shape
    scale = HEAD_DIM ** -0.5
    logits = []
    for kt, m in zip(ks, masks):
        s = jnp.einsum('bqhgd,bkhd->bhgqk', q, kt).astype(jnp.float32) * scale
        if m is not None:
            s = jnp.where(m, s, -jnp.inf)
        logits.append(s)
    logits.append(jnp.broadcast_to(sink.reshape(HK, G, 1, 1).astype(jnp.float32), (B, HK, G, Q, 1)))
    p = jax.nn.softmax(jnp.concatenate(logits, axis=-1), axis=-1)
    outs, off = [], 0
    for vt in vs:
        K = vt.shape[1]
        outs.append(jnp.einsum('bhgqk,bkhd->bqhgd', p[..., off:off + K].astype(vt.dtype), vt))
        off += K
    out = outs[0]
    for o in outs[1:]:
        out = out + o
    return out

def _window_attention(q, k, v, kc, vc, sink):
    B, T = q.shape[:2]
    nb = T // BLOCK
    pad = ((0, 0), (BLOCK, BLOCK), (0, 0), (0, 0))
    kp, vp = jnp.pad(k, pad), jnp.pad(v, pad)
    qg = q.reshape(B, T, N_KV_HEADS, GQA_GROUP, HEAD_DIM)
    offs_q = jnp.arange(BLOCK)
    offs_k = jnp.arange(3 * BLOCK)

    def one_block(i):
        start = i * BLOCK
        q_i = lax.dynamic_slice_in_dim(qg, start, BLOCK, axis=1)
        k_i = lax.dynamic_slice_in_dim(kp, start, 3 * BLOCK, axis=1)
        v_i = lax.dynamic_slice_in_dim(vp, start, 3 * BLOCK, axis=1)
        qpos = start + offs_q
        kpos = start - BLOCK + offs_k
        m = (jnp.abs(kpos[None, :] - qpos[:, None]) <= WINDOW) & (kpos >= 0)[None, :] & (kpos < T)[None, :]
        return _sink_attend(q_i, [k_i, kc], [v_i, vc], [m, None], sink)

    o = lax.map(one_block, jnp.arange(nb))
    return jnp.moveaxis(o, 0, 1).reshape(B, T, ATT_WIDTH)

def _rwkv_prepare(rkv, wl, al, conv_w, w0, w2, a0, a2, k_k, k_a):
    B, T, _ = rkv.shape
    f32 = jnp.float32
    heads = lambda t: t.reshape(B, T, RWKV_HEADS, HEAD_DIM)
    r, k, v = jnp.split(_dwconv3(rkv, conv_w).astype(f32), 3, axis=-1)
    kk = heads(k * k_k)
    kk = kk * lax.rsqrt(jnp.sum(kk * kk, axis=-1, keepdims=True) + EPS)
    dirs = []
    for d in range(2):
        w_log = -jax.nn.softplus(-(w0[d] + jnp.tanh(wl.astype(f32)) @ w2[d])) - 0.5
        decay = jnp.exp(-jnp.exp(w_log))
        a = jax.nn.sigmoid(a0[d] + al.astype(f32) @ a2[d])
        kmod = k * (1 + (a - 1) * k_a)
        dirs.append((heads(decay), heads(a), heads(kmod)))
    return heads(r), heads(v), kk, dirs

def _rwkv_scan(S0, decay, kk, a, k, v, r, reverse):
    to_time = lambda t: None if t is None else jnp.moveaxis(t, 1, 0)

    def step(S, xs):
        w_t, kk_t, a_t, k_t, v_t, r_t = xs
        sa = jnp.einsum('bhvk,bhk->bhv', S, kk_t)
        S = S * w_t[:, :, None, :] - sa[..., None] * (kk_t * a_t)[:, :, None, :] + v_t[..., None] * k_t[:, :, None, :]
        y = None if r_t is None else jnp.einsum('bhvk,bhk->bhv', S, r_t)
        return S, y

    xs = tuple(to_time(t) for t in (decay, kk, a, k, v, r))
    S, ys = lax.scan(step, S0, xs, reverse=reverse)
    return S, (None if ys is None else jnp.moveaxis(ys, 0, 1))

def _rwkv_out(y, r, v, dirs, gl, r_k, lnx_w, lnx_b, g_up, dtype):
    B, T = y.shape[:2]
    mu = jnp.mean(y, axis=-1, keepdims=True)
    var = jnp.mean(jnp.square(y - mu), axis=-1, keepdims=True)
    yn = ((y - mu) * lax.rsqrt(var + GN_EPS)).reshape(B, T, RWKV_WIDTH) * lnx_w + lnx_b
    bonus = (jnp.sum(r * dirs[0][2] * r_k, axis=-1, keepdims=True)
             + jnp.sum(r * dirs[1][2] * r_k, axis=-1, keepdims=True)) * v
    gate = jax.nn.sigmoid(gl) @ g_up
    return ((yn + bonus.reshape(B, T, RWKV_WIDTH)) * gate).astype(dtype)

def _cd_mixer(u, uc, pos_row, pos_col, ctx_out, w_in, q_norm, k_norm, sink, conv_w,
              w0, w2, a0, a2, k_k, k_a, r_k, lnx_w, lnx_b, g_up, w_out):
    B, T, _ = u.shape
    C = uc.shape[1]
    q, k, v, rkv, wl, al, gl = _split_sizes(u @ w_in, CD_SIZES)
    q_c, k_c, v_c, rkv_c, wl_c, al_c, gl_c = _split_sizes(uc @ w_in, CD_SIZES)
    q = _axial_rope(_rmsnorm(q.reshape(B, T, N_Q_HEADS, HEAD_DIM), q_norm), pos_row, pos_col)
    k = _axial_rope(_rmsnorm(k.reshape(B, T, N_KV_HEADS, HEAD_DIM), k_norm), pos_row, pos_col)
    v = v.reshape(B, T, N_KV_HEADS, HEAD_DIM)
    k_c = _rmsnorm(k_c.reshape(B, C, N_KV_HEADS, HEAD_DIM), k_norm)
    v_c = v_c.reshape(B, C, N_KV_HEADS, HEAD_DIM)
    att = _window_attention(q, k, v, k_c, v_c, sink)
    rw = (conv_w, w0, w2, a0, a2, k_k, k_a)
    rr_c, rv_c, rkk_c, dirs_c = _rwkv_prepare(rkv_c, wl_c, al_c, *rw)
    rr, rv, rkk, dirs = _rwkv_prepare(rkv, wl, al, *rw)
    S0 = jnp.zeros((B, RWKV_HEADS, HEAD_DIM, HEAD_DIM), jnp.float32)
    ys, ys_c = [], []
    for d, rev in enumerate((False, True)):
        dec_c, a_c, km_c = dirs_c[d]
        S_ctx, yc_d = _rwkv_scan(S0, dec_c, rkk_c, a_c, km_c, rv_c, rr_c if ctx_out else None, rev)
        dec, a, km = dirs[d]
        _, y_d = _rwkv_scan(S_ctx, dec, rkk, a, km, rv, rr, rev)
        ys.append(y_d)
        ys_c.append(yc_d)
    mix = _rwkv_out(ys[0] + ys[1], rr, rv, dirs, gl, r_k, lnx_w, lnx_b, g_up, u.dtype)
    out = jnp.concatenate([att, mix], axis=-1) @ w_out
    if not ctx_out:
        return out, None
    q_c = _rmsnorm(q_c.reshape(B, C, N_KV_HEADS, GQA_GROUP, HEAD_DIM), q_norm)
    att_c = _sink_attend(q_c, [k_c], [v_c], [None], sink).reshape(B, C, ATT_WIDTH)
    mix_c = _rwkv_out(ys_c[0] + ys_c[1], rr_c, rv_c, dirs_c, gl_c, r_k, lnx_w, lnx_b, g_up, uc.dtype)
    out_c = jnp.concatenate([att_c, mix_c], axis=-1) @ w_out
    return out, out_c

def _conv_ffn(u, w_up, conv_w, w_down):
    gate, val = jnp.split(_dwconv3(u @ w_up, conv_w), 2, axis=-1)
    return (jax.nn.silu(gate) * val) @ w_down

def setup_inputs(seed: int = 0) -> dict:
    key = jax.random.key(seed)
    keys = iter(jax.random.split(key, 48))

    def nrm(shape, std):
        return jax.random.normal(next(keys), shape, jnp.float32) * std

    D = D_MODEL
    return {
        'x': nrm((BATCH, SEQ, D), 1.0),
        'c': nrm((BATCH, D), 1.0),
        'ctx': nrm((BATCH, CTX_LEN, D), 1.0),
        'c_ctx': nrm((D,), 1.0),
        'ada_w': nrm((DEPTH, D, N_MOD * D), 0.5 * D ** -0.5),
        'ada_b': nrm((DEPTH, N_MOD * D), 0.02),
        'norm1': 1.0 + nrm((DEPTH, D), 0.05),
        'norm2': 1.0 + nrm((DEPTH, D), 0.05),
        'ffn_up': nrm((DEPTH, D, 2 * D_FF), D ** -0.5),
        'ffn_conv': nrm((DEPTH, 3, 2 * D_FF), 3 ** -0.5),
        'ffn_down': nrm((DEPTH, D_FF, D), D_FF ** -0.5),
        'ab_w_in': nrm((N_EVEN, D, AB_WIDTH), D ** -0.5),
        'pool_w': nrm((N_EVEN, N_POOL, POOL_GROUP, POOL_GROUP), POOL_GROUP ** -0.5),
        'pool_scale': 1.0 + nrm((N_EVEN, POOL_WIDTH), 0.1),
        'fourier_w': nrm((N_EVEN, FOURIER_WIDTH, FOURIER_WIDTH), FOURIER_WIDTH ** -0.5),
        'ab_w_out': nrm((N_EVEN, AB_WIDTH, D), AB_WIDTH ** -0.5),
        'cd_w_in': nrm((N_ODD, D, CD_WIDTH), D ** -0.5),
        'q_norm': 1.0 + nrm((N_ODD, HEAD_DIM), 0.05),
        'k_norm': 1.0 + nrm((N_ODD, HEAD_DIM), 0.05),
        'attn_sink': nrm((N_ODD, N_Q_HEADS), 0.5),
        'rwkv_conv': nrm((N_ODD, 3, 3 * RWKV_WIDTH), 3 ** -0.5),
        'rwkv_w0': jax.random.uniform(next(keys), (N_ODD, 2, RWKV_WIDTH), jnp.float32, -6.0, 0.0),
        'rwkv_w2': nrm((N_ODD, 2, DECAY_LORA, RWKV_WIDTH), 0.5 * DECAY_LORA ** -0.5),
        'rwkv_a0': nrm((N_ODD, 2, RWKV_WIDTH), 0.5),
        'rwkv_a2': nrm((N_ODD, 2, AAA_LORA, RWKV_WIDTH), 0.5 * AAA_LORA ** -0.5),
        'rwkv_k_k': 0.85 + nrm((N_ODD, RWKV_WIDTH), 0.05),
        'rwkv_k_a': 1.0 + nrm((N_ODD, RWKV_WIDTH), 0.05),
        'rwkv_r_k': nrm((N_ODD, RWKV_HEADS, HEAD_DIM), 0.1),
        'rwkv_lnx_w': 1.0 + nrm((N_ODD, RWKV_WIDTH), 0.05),
        'rwkv_lnx_b': nrm((N_ODD, RWKV_WIDTH), 0.02),
        'rwkv_g_up': nrm((N_ODD, GATE_LORA, RWKV_WIDTH), GATE_LORA ** -0.5),
        'cd_w_out': nrm((N_ODD, CD_OUT, D), CD_OUT ** -0.5),
    }

def reference(x, c, ctx, c_ctx, ada_w, ada_b, norm1, norm2, ffn_up, ffn_conv, ffn_down,
              ab_w_in, pool_w, pool_scale, fourier_w, ab_w_out,
              cd_w_in, q_norm, k_norm, attn_sink, rwkv_conv, rwkv_w0, rwkv_w2, rwkv_a0, rwkv_a2,
              rwkv_k_k, rwkv_k_a, rwkv_r_k, rwkv_lnx_w, rwkv_lnx_b, rwkv_g_up, cd_w_out):
    L = x.shape[1]
    rows = L // GRID_W
    pos_row = jnp.repeat(jnp.arange(rows, dtype=jnp.int32), GRID_W)
    pos_col = jnp.broadcast_to(jnp.arange(GRID_W, dtype=jnp.int32)[None, :], (rows, GRID_W)).reshape(-1)
    h, hc = x, ctx
    for layer in range(DEPTH):
        last = layer == DEPTH - 1
        even = layer % 2 == 0
        j = layer // 2
        mod = jax.nn.silu(c) @ ada_w[layer] + ada_b[layer]
        sh1, sc1, gt1, sh2, sc2, gt2 = jnp.split(mod[:, None, :], N_MOD, axis=-1)
        u = _modulate(_rmsnorm(h, norm1[layer]), sh1, sc1)
        if (not last) or (not even):
            mod_c = jax.nn.silu(c_ctx) @ ada_w[layer] + ada_b[layer]
            csh1, csc1, cgt1, csh2, csc2, cgt2 = jnp.split(mod_c, N_MOD, axis=-1)
            uc = _modulate(_rmsnorm(hc, norm1[layer]), csh1, csc1)
        if even:
            ab = (ab_w_in[j], pool_w[j], pool_scale[j], fourier_w[j], ab_w_out[j])
            y = _ab_mixer(u, *ab)
            yc = None if last else _ab_mixer(uc, *ab)
        else:
            y, yc = _cd_mixer(u, uc, pos_row, pos_col, not last, cd_w_in[j], q_norm[j], k_norm[j],
                              attn_sink[j], rwkv_conv[j], rwkv_w0[j], rwkv_w2[j], rwkv_a0[j], rwkv_a2[j],
                              rwkv_k_k[j], rwkv_k_a[j], rwkv_r_k[j], rwkv_lnx_w[j], rwkv_lnx_b[j],
                              rwkv_g_up[j], cd_w_out[j])
        ffn = (ffn_up[layer], ffn_conv[layer], ffn_down[layer])
        h = h + gt1 * y
        h = h + gt2 * _conv_ffn(_modulate(_rmsnorm(h, norm2[layer]), sh2, sc2), *ffn)
        if not last:
            hc = hc + cgt1 * yc
            hc = hc + cgt2 * _conv_ffn(_modulate(_rmsnorm(hc, norm2[layer]), csh2, csc2), *ffn)
    return h


_drawn_inputs = setup_inputs


def setup_inputs(seed=0):
    import zlib

    import numpy as np

    out = dict(_drawn_inputs(seed))
    spreads = {}
    factors = {'norm1': 2.848,
     'q_norm': 173.114,
     'k_norm': 162.452,
     'attn_sink': 8.0,
     'rwkv_w2': 8.0,
     'rwkv_k_k': 200.0,
     'rwkv_k_a': 6.625,
     'rwkv_lnx_w': 64.0,
     'rwkv_lnx_b': 200.0}
    for name, (base, spread) in spreads.items():
        noise = np.random.default_rng([zlib.crc32(name.encode()), seed]).standard_normal(out[name].shape)
        drawn = base * np.exp(spread * noise) if base else spread * noise
        out[name] = __import__('jax').numpy.asarray(drawn.astype(out[name].dtype))
    for name, factor in factors.items():
        out[name] = (out[name] * factor).astype(out[name].dtype)
    return out
```

```python
import numpy as np
import concourse.bass as bass
from concourse import mybir

ALU = mybir.AluOpType
ACT = mybir.ActivationFunctionType
AX = mybir.AxisListType
F32 = mybir.dt.float32
F32R = mybir.dt.float32r

P = 128
D = 1024
KT = D // P
SEQ = 1024
CTX = 256
NT = SEQ + CTX
COLS = [(0, 512), (512, 512), (1024, 256)]
SEGS = [(0, SEQ), (SEQ, CTX)]
FF = 2816
FT = FF // P
GROUPS = FT // 2
EPS = 1e-6
GRID_W = 64
ZT = 2560 // P
ZA_AT = [8, 8 + SEQ + 16]
PW = ZA_AT[1] + CTX + 8


def za_col(at):
    return at + (ZA_AT[0] if at < SEQ else ZA_AT[1] - SEQ)


class Chain:

    def __init__(self, eng, sem, base=0):
        self.eng, self.sem, self.n, self.base = eng, sem, 0, base

    def link(self, ins):
        ins.then_inc(self.sem, 1)
        self.n += 1
        self.eng.wait_ge(self.sem, self.n + self.base)


class Kernel:
    def __init__(self, nc, a, out):
        self.nc, self.a, self.out = nc, a, out
        self.base = -(-nc.sbuf_base // 32) * 32
        self.top = 0
        self.sems = []
        place = self.place
        self.h = place("h", [P, KT, NT], F32)
        self.w_at = self.top
        self.raw = place("w_raw", [P, 2, KT * P], F32)
        self.whi = place("w_hi", [P, 3, KT * P], F32R)
        self.wlo = place("w_lo", [P, 3, KT * P], F32R)
        self.u_at = self.top
        self.uhi = place("u_hi", [P, KT, NT], F32R)
        self.ulo = place("u_lo", [P, KT, NT], F32R)
        self.s_at = self.top
        self.act_hi = place("act_hi", [P, 2, 2, NT], F32R)
        self.act_lo = place("act_lo", [P, 2, 2, NT], F32R)
        self.t_at = self.top
        self.top += 2 * NT * 4
        self.s_end = self.top
        self.mod = place("mod", [P, 2, 48, 2], F32)
        self.gs = place("gs", [P, 4, KT, 2], F32)
        self.small = place("small", [P, SMALL_N], F32)
        self.ones = place("ones", [P, P], F32)
        self.eye = place("eye", [P, P], F32)
        self.eye2 = place("eye2", [P, P // 2], F32)
        self.epsc = place("epsc", [P, 2], F32)
        self.zero = place("zero", [P, 2], F32)
        self.ps = nc.psum_tensor("ps", [P, 2, 4, 512], F32).__enter__()

    def place(self, name, shape, dt, at=None):
        size = -(-4 * int(np.prod(shape[1:])) // 32) * 32
        if at is None:
            at = self.top
            self.top += size
        return self.nc.alloc_sbuf_tensor_at(name, shape, dt, offset=self.base + at)

    def sem(self, name):
        sem = self.nc.alloc_semaphore(name)
        self.sems.append(sem)
        return sem

    def phase_over(self):
        self.nc.clear_and_free_semaphores(self.sems)
        self.nc.all_engine_barrier(sem_only=True)
        self.sems = []

    def S(self, name):
        o, n = SMALL[name]
        return self.small[:, o:o + n]

    def part(self, layer, part, k, cond):
        return self.mod[:, layer, part * KT + k, cond:cond + 1]


_SMALL = [("cond", 16), ("ada_b", 96), ("norm", 32), ("conv", 2 * 3 * 44), ("pool_scale", 6),
          ("edge", 4 * 16), ("qn", 1), ("kn", 1), ("rconv", 3 * 12), ("sink", 8)]
SMALL, _o = {}, 0
for _n, _c in _SMALL:
    SMALL[_n] = (_o, _c)
    _o += _c
SMALL_N = _o


class Weights:

    def __init__(self, K, name, dram, nblk):
        self.K, self.dram, self.nblk = K, dram, nblk
        self.loaded = [K.sem(f"{name}_w_loaded{s}") for s in range(2)]
        self.hi_done = K.sem(f"{name}_w_hi_done")
        self.split = K.sem(f"{name}_w_split")

    def load(self, sp):
        def pair(i, first):
            for s in range(2):
                if not first:
                    sp.wait_ge(self.split, 2 * i + s - 1)
                sp.dma_start(self.K.raw[:, s, :], self.dram[2 * i + s]).then_inc(self.loaded[s], 16)
        pair(0, True)
        with sp.Fori(1, self.nblk // 2) as i:
            pair(i, False)

    def divide_one(self, pool, raw, slot, nth, turn):
        K = self.K
        pool.wait_ge(self.loaded[raw], 16 * (turn + 1))
        pool.tensor_tensor(K.whi[:, slot, :], K.raw[:, raw, :], K.zero[:, 0:1].to_broadcast([P, KT * P]),
                           ALU.add).then_inc(self.hi_done, 1)
        pool.wait_ge(self.hi_done, nth + 1)
        pool.tensor_tensor(K.wlo[:, slot, :], K.raw[:, raw, :], K.whi[:, slot, :],
                           ALU.subtract).then_inc(self.split, 1)

    def divide(self, pool, tile_done, norm=None):
        for n in range(self.nblk):
            if norm is not None and n <= 3:
                norm.pool(pool, n)
            if n >= 3:
                pool.wait_ge(tile_done, n - 2)
            self.divide_one(pool, n % 2, n % 3, n, n // 2)


def product(pe, K, slot, s, xhi, xlo, k, sub, cols, start, stop):
    mm = None
    w = slice(sub * P, (sub + 1) * P)
    for n, (wt, x) in enumerate([(K.whi, xhi), (K.whi, xlo), (K.wlo, xhi)]):
        for c, (at, width) in enumerate(cols):
            mm = pe.matmul(K.ps[:, slot, c, 0:width], wt[:, s, w], x[:, k, at:at + width],
                           start=start and n == 0, stop=stop and n == 2)
    return mm


def bank_cols(K, slot, cols=COLS):
    n = cols[-1][0] + cols[-1][1]
    return K.ps[:, slot, :, :].rearrange("p b c -> p (b c)")[:, 0:n]


def setup_phase(K):
    nc, a = K.nc, K.a
    ada = K.place("ada_ring", [P, 2, KT * 512], F32, at=K.u_at)
    row = K.place("mod_row", [2, 2, 512], F32, at=K.s_at)
    sc = K.place("silu_c", [P, KT, 2], F32, at=K.s_at + 8192)
    NCH = 2 * 12
    h_in, small_in, ada_in = K.sem("h_in"), K.sem("small_in"), [K.sem("ada_in0"), K.sem("ada_in1")]
    consts, silu_done, rows_done = K.sem("consts"), K.sem("silu_done"), K.sem("ada_rows_done")
    row_out, turned, mod_done = K.sem("ada_row_out"), K.sem("ada_turned"), K.sem("mod_done")
    gains, eye0 = K.sem("gains"), K.sem("eye_zero")
    with nc.Block() as block:
        @block.sync
        def _(sp):
            sp.dma_start(K.small[:, :], a["small"]).then_inc(small_in, 16)
            for n in range(NCH):
                if n >= 2:
                    sp.wait_ge(rows_done, n - 1)
                sp.dma_start(ada[:, n % 2, :], a["ada"][n]).then_inc(ada_in[n % 2], 16)
                if n == 3:
                    for k in range(KT):
                        sp.dma_start(K.h[:, k, :], a["x"][k]).then_inc(h_in, 16)
            sp.wait_ge(h_in, 16 * KT)

        @block.gpsimd
        def _(pool):
            pool.memset(K.ones[:, :], 1.0).then_inc(consts, 1)
            pool.memset(K.epsc[:, 0:1], EPS).then_inc(consts, 1)
            pool.memset(K.epsc[:, 1:2], 64 * EPS).then_inc(consts, 1)
            pool.memset(K.zero[:, :], 0.0).then_inc(consts, 1)
            pool.memset(K.eye[:, :], 0.0).then_inc(eye0, 1)
            pool.wait_ge(eye0, 1)
            pool.affine_select(out=K.eye[:, :], in_=K.eye[:, :], compare_op=ALU.not_equal, fill=1.0,
                               base=0, pattern=[[-1, P]], channel_multiplier=1).then_inc(consts, 1)

        @block.scalar
        def _(act):
            act.wait_ge(small_in, 16)
            act.activation(sc[:, :, :], K.S("cond").rearrange("p (k c) -> p k c", c=2),
                           ACT.Silu).then_inc(silu_done, 1)
            for n in range(NCH):
                act.wait_ge(rows_done, n + 1)
                if n >= 2:
                    act.wait_ge(turned, n - 1)
                act.copy(row[:, n % 2, :], K.ps[0:2, 0, n % 2, :]).then_inc(row_out, 1)

        @block.tensor
        def _(pe):
            def turn(n):
                pe.wait_ge(row_out, n + 1)
                pe.wait_ge(consts, 5)
                if n >= 2:
                    pe.wait_ge(mod_done, n - 1)
                for j in range(4):
                    mm = pe.transpose(K.ps[:, 1, n % 2, 2 * j:2 * j + 2],
                                      row[:, n % 2, j * P:(j + 1) * P], K.eye[0:2, 0:2])
                mm.then_inc(turned, 1)
            pe.wait_ge(silu_done, 1)
            for n in range(NCH):
                pe.wait_ge(ada_in[n % 2], 16 * (n // 2 + 1))
                if n >= 2:
                    pe.wait_ge(row_out, n - 1)
                for k in range(KT):
                    mm = pe.matmul(K.ps[0:2, 0, n % 2, :], sc[:, k, :], ada[:, n % 2, k * 512:(k + 1) * 512],
                                   start=k == 0, stop=k == KT - 1)
                mm.then_inc(rows_done, 1)
                if n:
                    turn(n - 1)
            turn(NCH - 1)

        @block.vector
        def _(dve):
            dve.wait_ge(small_in, 16)
            b = K.S("ada_b").rearrange("p (l t) -> p l t", l=2)
            for n in range(NCH):
                l, t = n // 12, 4 * (n % 12)
                dve.wait_ge(turned, n + 1)
                for c in range(2):
                    ins = dve.tensor_tensor(
                        K.mod[:, l, t:t + 4, c],
                        K.ps[:, 1, n % 2, 0:8].rearrange("p (j c) -> p j c", c=2)[:, :, c],
                        b[:, l, t:t + 4], ALU.add)
                ins.then_inc(mod_done, 1)
            dve.tensor_tensor(K.eye2[:, :], K.eye[:, 0:64], K.eye[:, 64:128], ALU.add).then_inc(gains, 1)
            dve.wait_ge(mod_done, NCH)
            g = K.S("norm").rearrange("p (n k) -> p n k", n=4)
            for n in range(4):
                part = 1 if n % 2 == 0 else 4
                for c in range(2):
                    dve.scalar_tensor_tensor(K.gs[:, n, :, c], K.mod[:, n // 2, part * KT:(part + 1) * KT, c],
                                             1.0, g[:, n, :], ALU.add, ALU.mult).then_inc(gains, 1)


class Norm:
    W = 256
    POOL_K = 2
    ACT_K = 3

    def __init__(self, K, n, n_tok=NT):
        self.K, self.n, self.chunks = K, n, n_tok // self.W
        tag, W = f"n{n}", self.W
        self.sq = K.place(f"{tag}_sq", [P, 2, KT, W], F32, at=K.s_at)
        self.t = K.place(f"{tag}_t", [P, 2, KT, W], F32, at=K.s_at + 16384)
        self.u = K.place(f"{tag}_u", [P, 2, KT, W], F32, at=K.s_at + 32768)
        self.r = K.place(f"{tag}_r", [P, 2 * self.chunks], F32, at=K.s_at + 49152)
        self.sq_done, self.summed, self.root, self.inverted, self.spread = [
            K.sem(f"{tag}_{x}") for x in ("sq", "sum", "root", "inverted", "spread")]
        self.paired, self.shifted_dve = K.sem(f"{tag}_paired"), K.sem(f"{tag}_shifted_dve")
        self.scaled, self.shifted, self.hi_done, self.lo_dve, self.lo_pool = [
            K.sem(f"{tag}_{x}") for x in ("scaled", "shifted", "hi", "lo_dve", "lo_pool")]

    def cols(self, c):
        return slice(c * self.W, (c + 1) * self.W)

    def gain_shift(self, m, k):
        cond = 1 if m * self.W >= SEQ else 0
        return (self.K.gs[:, self.n, k, cond:cond + 1],
                self.K.part(self.n // 2, 0 if self.n % 2 == 0 else 3, k, cond))

    def act(self, act):
        K = self.K

        def square(c):
            if c >= 2:
                act.wait_ge(self.summed, c - 1)
            act.activation(self.sq[:, c % 2, :, :], K.h[:, :, self.cols(c)], ACT.Square).then_inc(self.sq_done, 1)

        def shift_and_hi(m):
            act.wait_ge(self.scaled, m + 1)
            if m >= 2:
                act.wait_ge(self.lo_dve, m - 1)
                act.wait_ge(self.lo_pool, m - 1)
            for k in range(self.ACT_K):
                gain, shift = self.gain_shift(m, k)
                ins = act.activation(self.u[:, m % 2, k, :], self.t[:, m % 2, k, :], ACT.Identity, bias=shift,
                                     scale=gain)
            ins.then_inc(self.shifted, 1)
            act.wait_ge(self.shifted, m + 1)
            act.wait_ge(self.shifted_dve, m + 1)
            act.copy(K.uhi[:, :, self.cols(m)], self.u[:, m % 2, :, :]).then_inc(self.hi_done, 1)
        square(0)
        square(1)
        for c in range(self.chunks):
            act.wait_ge(self.summed, c + 1)
            act.activation(self.r[:, 2 * c:2 * c + 2], K.ps[:, 0, c % 2, 0:2], ACT.Sqrt, bias=K.epsc[:, 0:1],
                           scale=1.0 / D).then_inc(self.root, 1)
            if c + 2 < self.chunks:
                square(c + 2)
            if c >= 1:
                shift_and_hi(c - 1)
        shift_and_hi(self.chunks - 1)

    def pe(self, pe):
        K = self.K

        def sums(c):
            pe.wait_ge(self.paired, c + 1)
            if c >= 2:
                pe.wait_ge(self.root, c - 1)
            for m in range(2):
                for k in range(KT // 2):
                    mm = pe.matmul(K.ps[:, 0, c % 2, m:m + 1], self.sq[:, c % 2, k, m * P:(m + 1) * P],
                                   K.ones[:, 0:1], start=k == 0, stop=k == KT // 2 - 1)
            mm.then_inc(self.summed, 1)
        sums(0)
        for c in range(self.chunks):
            if c and c + 1 < self.chunks:
                sums(c + 1)
            pe.wait_ge(self.inverted, c + 1)
            if c >= 2:
                pe.wait_ge(self.scaled, c - 1)
            for m in range(2):
                mm = pe.matmul(K.ps[:, 0, 2 + c % 2, m * P:(m + 1) * P],
                               self.r[:, 2 * c + m:2 * c + m + 1].to_broadcast([P, P]), K.eye[:, :],
                               start=True, stop=True)
            mm.then_inc(self.spread, 1)
            if c == 0:
                sums(1)
        pe.wait_ge(self.lo_dve, self.chunks)
        pe.wait_ge(self.lo_pool, self.chunks)

    def dve(self, dve):
        K, kd = self.K, KT - self.POOL_K

        def invert(c):
            if c < self.chunks:
                dve.wait_ge(self.root, c + 1)
                r = self.r[:, 2 * c:2 * c + 2]
                dve.reciprocal(r, r).then_inc(self.inverted, 1)
        invert(0)
        for c in range(self.chunks + 1):
            if c < self.chunks:
                dve.wait_ge(self.spread, c + 1)
                if c >= 2:
                    dve.wait_ge(self.shifted, c - 1)
                dve.tensor_tensor(self.t[:, c % 2, :, :], K.h[:, :, self.cols(c)],
                                  K.ps[:, 0, 2 + c % 2, 0:self.W].rearrange("p (o w) -> p o w", o=1).to_broadcast(
                                      [P, KT, self.W]), ALU.mult).then_inc(self.scaled, 1)
                if c >= 2:
                    dve.wait_ge(self.lo_pool, c - 1)
                dve.wait_ge(self.scaled, c + 1)
                for k in range(self.ACT_K, KT):
                    gain, shift = self.gain_shift(c, k)
                    ins = dve.tensor_scalar(self.u[:, c % 2, k, :], self.t[:, c % 2, k, :], gain, shift, ALU.mult,
                                            ALU.add)
                ins.then_inc(self.shifted_dve, 1)
                dve.wait_ge(self.shifted_dve, c + 1)
                invert(c + 1)
            if c >= 1:
                m = c - 1
                dve.wait_ge(self.hi_done, m + 1)
                dve.tensor_tensor(K.ulo[:, 0:kd, self.cols(m)], self.u[:, m % 2, 0:kd, :],
                                  K.uhi[:, 0:kd, self.cols(m)], ALU.subtract).then_inc(self.lo_dve, 1)
                dve.wait_ge(self.lo_dve, m + 1)

    def pool(self, pool, block):
        K, kd, half = self.K, KT - self.POOL_K, KT // 2

        def pair(c):
            if c < self.chunks:
                pool.wait_ge(self.sq_done, c + 1)
                sq = self.sq[:, c % 2]
                pool.tensor_tensor(sq[:, 0:half, :], sq[:, 0:half, :], sq[:, half:KT, :],
                                   ALU.add).then_inc(self.paired, 1)

        def lo(m):
            if m < self.chunks:
                pool.wait_ge(self.hi_done, m + 1)
                pool.tensor_tensor(K.ulo[:, kd:KT, self.cols(m)], self.u[:, m % 2, kd:KT, :],
                                   K.uhi[:, kd:KT, self.cols(m)], ALU.subtract).then_inc(self.lo_pool, 1)
        order = [[(pair, 0), (pair, 1)], [(pair, 2), (pair, 3), (lo, 0)], [(pair, 4), (lo, 1), (lo, 2)],
                 [(lo, 3), (lo, 4)]]
        for step, c in order[block]:
            step(c)


def add_gated(dve, K, layer, part, m, slot, segs):
    for c, (at, n) in enumerate(segs):
        ins = dve.scalar_tensor_tensor(K.h[:, m, at:at + n], bank_cols(K, slot)[:, at:at + n],
                                       K.part(layer, part, m, c), K.h[:, m, at:at + n], ALU.mult, ALU.add)
    return ins


def out_phase(K, tag, dram, layer, cols, segs):
    nc = K.nc
    W = Weights(K, tag, dram, KT)
    done, added = K.sem(f"{tag}_tile_done"), K.sem(f"{tag}_added")
    with nc.Block() as block:
        @block.sync
        def _(sp):
            W.load(sp)

        @block.gpsimd
        def _(pool):
            W.divide(pool, done)

        @block.tensor
        def _(pe):
            for m in range(KT):
                pe.wait_ge(W.split, m + 1)
                if m >= 2:
                    pe.wait_ge(added, m - 1)
                for k in range(KT):
                    mm = product(pe, K, m % 2, m % 3, K.uhi, K.ulo, k, k, cols, k == 0, k == KT - 1)
                mm.then_inc(done, 1)

        @block.vector
        def _(dve):
            for m in range(KT):
                dve.wait_ge(done, m + 1)
                add_gated(dve, K, layer, 2, m, m % 2, segs).then_inc(added, 1)


def conv_taps(dve, K, chain, cv, psum, w0, w2, segs):
    for at, n in segs:
        chain.link(dve.scalar_tensor_tensor(cv[:, at + 1:at + n], psum[:, at:at + n - 1], w0,
                                            cv[:, at + 1:at + n], ALU.mult, ALU.add))
        last = dve.scalar_tensor_tensor(cv[:, at:at + n - 1], psum[:, at + 1:at + n], w2,
                                        cv[:, at:at + n - 1], ALU.mult, ALU.add)
        if at + n != segs[-1][0] + segs[-1][1]:
            chain.link(last)
    return last


def ffn_phase(K, layer, cols, segs):
    nc = K.nc
    tag = f"ffn{layer}"
    n_tok = cols[-1][0] + cols[-1][1]
    G = GROUPS
    W = Weights(K, tag, K.a["ffn"][layer], 6 * G)
    norm = Norm(K, 2 * layer + 1, n_tok)
    cv = K.place(f"{tag}_cv", [P, 2, NT], F32, at=K.t_at)
    up_done, down_done, added = [K.sem(f"{tag}_{x}") for x in ("up_done", "down_done", "added")]
    centre, conv_done, silu_done, act_ready = [K.sem(f"{tag}_{x}") for x in
                                               ("centre", "conv_done", "silu_done", "act_ready")]
    dve_own = K.sem(f"{tag}_dve_own")
    tap0 = SMALL["conv"][0] + layer * 3 * 44

    def tap(t, g, q):
        at = tap0 + t * 44 + (q % 2) * FT + q // 2 + 2 * g
        return K.small[:, bass.ds(at, 1)]

    def schedule(up, down, engine):
        up(0, 0)
        up(1, 1)
        down(0, 0)
        with engine.Fori(1, (G - 1) // 2) as i:
            up(2 * i, 0)
            down(2 * i - 1, 1)
            up(2 * i + 1, 1)
            down(2 * i, 0)
        up(G - 1, 0)
        down(G - 2, 1)
        down(G - 1, 0)

    def is_early(g):
        return isinstance(g, int) and g < 2

    def is_last(g):
        return isinstance(g, int) and g == G - 1

    def before_up(g):
        return 4 * g if is_early(g) else 6 * g - 2

    def before_down(g):
        return 6 * g + (4 if is_last(g) else 8)

    with nc.Block() as block:
        @block.sync
        def _(sp):
            W.load(sp)

        @block.gpsimd
        def _(pool):
            def up(g, par):
                if is_early(g):
                    free = [[None, None, None, (up_done, 1)],
                            [(up_done, 4), (up_done, 2), (up_done, 3), (up_done, 5)]][g]
                else:
                    free = [(up_done, 4 * g), (down_done, 8 * (g - 1)), (down_done, 8 * (g - 1)),
                            (up_done, 4 * g + 1)]
                for q in range(4):
                    if is_early(g) and g == 0:
                        norm.pool(pool, q)
                    if free[q] is not None:
                        pool.wait_ge(*free[q])
                    turn = (2 * g if is_early(g) else 3 * g - 1) + q // 2
                    W.divide_one(pool, q % 2, q % 3, before_up(g) + q, turn)

            def down(g, par):
                for b in range(2):
                    if is_last(g):
                        pool.wait_ge(down_done, 8 * g)
                    else:
                        pool.wait_ge(up_done, 4 * (g + 1) + 2 + b)
                    W.divide_one(pool, b, 1 + b, before_down(g) + b, 3 * g + (2 if is_last(g) else 4))
            schedule(up, down, pool)

        @block.tensor
        def _(pe):
            def up(g, par):
                for q in range(4):
                    if not (is_early(g) and g == 0 and q < 2):
                        pe.wait_ge(conv_done, 4 * g + q - 1)
                    if not is_early(g) and q < 2:
                        pe.wait_ge(added, 8 * (g - 1) - 1 + q)
                    pe.wait_ge(W.split, before_up(g) + q + 1)
                    for k in range(KT):
                        mm = product(pe, K, q % 2, q % 3, K.uhi, K.ulo, k, k, cols, k == 0, k == KT - 1)
                    mm.then_inc(up_done, 1)

            def down(g, par):
                pe.wait_ge(W.split, before_down(g) + 2)
                pe.wait_ge(act_ready, 2 * g + 2)
                for m in range(KT):
                    if m < 2 and not is_last(g):
                        pe.wait_ge(conv_done, 4 * (g + 1) + 3 + m)
                    if m >= 2 or is_last(g):
                        pe.wait_ge(added, 8 * g + m - 1)
                    for f in range(2):
                        mm = product(pe, K, m % 2, 1 + f, K.act_hi[:, par], K.act_lo[:, par], f, m,
                                     cols, f == 0, f == 1)
                    mm.then_inc(down_done, 1)
            norm.pe(pe)
            schedule(up, down, pe)

        @block.scalar
        def _(act):
            def up(g, par):
                for q in range(4):
                    x = q % 2
                    act.wait_ge(up_done, 4 * g + q + 1)
                    if not (is_early(g) and g == 0 and q < 2):
                        act.wait_ge(act_ready, 2 * g + q // 2)
                    act.activation(cv[:, x, 0:n_tok], bank_cols(K, q % 2, cols), ACT.Identity,
                                   scale=tap(1, g, q)).then_inc(centre, 1)
                    if x == 0:
                        act.wait_ge(conv_done, 4 * g + q + 1)
                        act.activation(cv[:, 0, 0:n_tok], cv[:, 0, 0:n_tok], ACT.Silu).then_inc(silu_done, 1)
            norm.act(act)
            schedule(up, lambda g, par: None, act)

        @block.vector
        def _(dve):
            per_conv = 2 * len(segs) - 1
            per_group = 2 * (2 * per_conv + 2)

            def up(g, par):
                own = Chain(dve, dve_own, per_group * g)
                for q in range(4):
                    x = q % 2
                    dve.wait_ge(centre, 4 * g + q + 1)
                    conv_taps(dve, K, own, cv[:, x, :], bank_cols(K, q % 2, cols), tap(0, g, q),
                              tap(2, g, q), segs).then_inc(conv_done, 1)
                    if x == 1:
                        f = q // 2
                        dve.wait_ge(conv_done, 4 * g + q + 1)
                        dve.wait_ge(silu_done, 2 * g + f + 1)
                        own.link(dve.tensor_tensor(cv[:, 1, 0:n_tok], cv[:, 1, 0:n_tok], cv[:, 0, 0:n_tok],
                                                   ALU.mult))
                        if not is_early(g) and f == 0:
                            dve.wait_ge(down_done, 8 * (g - 1))
                        own.link(dve.tensor_copy(K.act_hi[:, par, f, 0:n_tok], cv[:, 1, 0:n_tok]))
                        dve.tensor_tensor(K.act_lo[:, par, f, 0:n_tok], cv[:, 1, 0:n_tok],
                                          K.act_hi[:, par, f, 0:n_tok], ALU.subtract).then_inc(act_ready, 1)
                assert own.n == per_group

            def down(g, par):
                for m in range(KT):
                    dve.wait_ge(down_done, 8 * g + m + 1)
                    add_gated(dve, K, layer, 5, m, m % 2, segs).then_inc(added, 1)
            norm.dve(dve)
            schedule(up, down, dve)


def ab_in_phase(K):
    nc = K.nc
    K.za = K.place("za", [P, 6, PW], F32, at=K.s_at)
    K.zb = K.place("zb", [P, 2, NT], F32, at=K.s_at + 4 * 6 * PW)
    W = Weights(K, "abin", K.a["ab_in"], KT)
    norm = Norm(K, 0)
    done, stored, zeroed = K.sem("abin_done"), K.sem("abin_stored"), K.sem("abin_zeroed")
    with nc.Block() as block:
        @block.sync
        def _(sp):
            W.load(sp)

        @block.gpsimd
        def _(pool):
            W.divide(pool, done, norm)

        @block.tensor
        def _(pe):
            norm.pe(pe)
            for m in range(KT):
                pe.wait_ge(W.split, m + 1)
                if m >= 2:
                    pe.wait_ge(stored, m - 1)
                for k in range(KT):
                    mm = product(pe, K, m % 2, m % 3, K.uhi, K.ulo, k, k, COLS, k == 0, k == KT - 1)
                mm.then_inc(done, 1)

        @block.vector
        def _(dve):
            norm.dve(dve)
            dve.wait_ge(norm.lo_dve, norm.chunks)
            dve.wait_ge(norm.lo_pool, norm.chunks)
            dve.memset(K.za[:, :, :], 0.0).then_inc(zeroed, 1)

        @block.scalar
        def _(act):
            norm.act(act)
            act.wait_ge(zeroed, 1)
            for m in range(KT):
                act.wait_ge(done, m + 1)
                z = bank_cols(K, m % 2)
                if m < 6:
                    act.copy(K.za[:, m, ZA_AT[0]:ZA_AT[0] + SEQ], z[:, 0:SEQ])
                    act.copy(K.za[:, m, ZA_AT[1]:ZA_AT[1] + CTX], z[:, SEQ:NT]).then_inc(stored, 1)
                else:
                    act.copy(K.zb[:, m - 6, :], z).then_inc(stored, 1)


def pool_fourier_phase(K):
    nc, a = K.nc, K.a
    za, zb = K.za, K.zb
    PQ = K.place("dft_pq", [P, NT // P, 512], F32, at=K.u_at)
    mats = K.place("dft_mats", [P, 3, 2, 256], F32, at=K.u_at + 20480)
    G = K.place("dft_g", [P, 2, 512], F32, at=K.u_at + 26624)
    tab = K.place("dft_tab", [P, 2, 2, SEQ], F32, at=K.u_at + 40960)
    ctab = K.place("dft_ctab", [P, 2, 2, CTX], F32, at=K.u_at + 57344)
    pmat = K.place("pool_mats", [P, 14, P], F32, at=K.w_at)
    win = K.place("pool_win", [P, 2, PW], F32, at=K.w_at + 7168)
    yt = K.place("mix_y", [P, NT], F32, at=K.w_at + 7168 + 8 * PW)
    mats_in, ctab_in, pmat_in = K.sem("dft_mats_in"), K.sem("dft_ctab_in"), K.sem("pool_mats_in")
    tab_in = [K.sem("dft_tab_in0"), K.sem("dft_tab_in1")]
    g_done, g_out, pq_done, pq_out, tab_used = [K.sem(f"dft_{x}") for x in ("g", "g_out", "pq", "pq_out", "tab_used")]
    yb_done, dve_own, pooled, ya_done, y_out, y_hi, y_split = [
        K.sem(f"mix_{x}") for x in ("yb", "dve_own", "pooled", "ya", "y_out", "y_hi", "y_split")]
    TT = SEQ // P
    pieces = [(0, 0, 128, 2), (1, 0, 64, 2), (1, 64, 128, 4), (2, 0, 128, 4),
              (3, 0, 128, 8), (4, 0, 64, 8), (4, 64, 128, 16), (5, 0, 128, 16)]
    outs = [(0, [0, 1]), (1, [0, 1, 2]), (2, [1, 2])]
    order = [6, 7] + list(range(6))
    with nc.Block() as block:
        @block.sync
        def _(sp):
            sp.dma_start(mats[:, :, :, :], a["dft_ch"]).then_inc(mats_in, 16)
            for t in range(2):
                sp.dma_start(tab[:, t, :, :], a["dft_tok"][t]).then_inc(tab_in[t], 16)
            sp.dma_start(ctab[:, :, :, :], a["dft_ctx"]).then_inc(ctab_in, 16)
            sp.dma_start(pmat[:, :, :], a["pool_w"]).then_inc(pmat_in, 16)
            for t in range(2, TT):
                sp.wait_ge(tab_used, t - 1)
                sp.dma_start(tab[:, t % 2, :, :], a["dft_tok"][t]).then_inc(tab_in[t % 2], 16)

        @block.tensor
        def _(pe):
            pe.wait_ge(mats_in, 16)
            for m in range(2):
                for s in range(2):
                    for k in range(2):
                        mm = pe.matmul(K.ps[:, 0, m, s * 256:(s + 1) * 256], mats[:, s, k, m * P:(m + 1) * P],
                                       mats[:, 2, k, :], start=k == 0, stop=k == 1)
            mm.then_inc(g_done, 1)
            pe.wait_ge(g_out, 1)
            for t in range(NT // P):
                if t >= 4:
                    pe.wait_ge(pq_out, t - 3)
                for k in range(2):
                    mm = pe.matmul(K.ps[:, 1, t % 4, :], zb[:, k, t * P:(t + 1) * P], G[:, k, :],
                                   start=k == 0, stop=k == 1)
                mm.then_inc(pq_done, 1)
            for t in range(TT):
                pe.wait_ge(pq_out, t + 1)
                pe.wait_ge(tab_in[t % 2], 16 * (t // 2 + 1))
                for s in range(2):
                    for m in range(2):
                        for c in range(2):
                            mm = pe.matmul(K.ps[:, 0, 2 * m + c, :], PQ[:, t, s * 256 + m * P:s * 256 + (m + 1) * P],
                                           tab[:, t % 2, s, c * 512:(c + 1) * 512], start=t == 0 and s == 0,
                                           stop=t == TT - 1 and s == 1)
                mm.then_inc(tab_used, 1)
            pe.wait_ge(ctab_in, 16)
            pe.wait_ge(pq_out, NT // P)
            for m in range(2):
                for t in range(2):
                    for s in range(2):
                        mm = pe.matmul(K.ps[:, 1, m, 0:CTX], PQ[:, TT + t, s * 256 + m * P:s * 256 + (m + 1) * P],
                                       ctab[:, t, s, :], start=t == 0 and s == 0, stop=t == 1 and s == 1)
            mm.then_inc(yb_done, 1)
            pe.wait_ge(pmat_in, 16)
            pe.wait_ge(pooled, 1)
            n = 0
            for half in range(2):
                for o, ins in outs:
                    m = 3 * half + o
                    pe.wait_ge(y_out, max(2, m + 1))
                    for j, k in enumerate(ins):
                        for c, (at, w) in enumerate(COLS):
                            mm = pe.matmul(K.ps[:, m % 2, c, 0:w], pmat[:, n, :],
                                           za[:, 3 * half + k, za_col(at):za_col(at) + w],
                                           start=j == 0, stop=j == len(ins) - 1)
                        n += 1
                    mm.then_inc(ya_done, 1)

        @block.scalar
        def _(act):
            act.wait_ge(g_done, 1)
            act.copy(G[:, :, :], K.ps[:, 0, 0:2, :]).then_inc(g_out, 1)
            for t in range(NT // P):
                act.wait_ge(pq_done, t + 1)
                act.copy(PQ[:, t, :], K.ps[:, 1, t % 4, :]).then_inc(pq_out, 1)
            for n, m in enumerate(order):
                if n == 0:
                    act.wait_ge(yb_done, 1)
                if n >= 2:
                    act.wait_ge(ya_done, n - 1)
                if n >= 1:
                    act.wait_ge(y_split, n)
                if m >= 6:
                    act.copy(yt[:, 0:SEQ], K.ps[:, 0, 2 * (m - 6):2 * (m - 6) + 2, :].rearrange("p b c -> p (b c)"))
                    act.copy(yt[:, SEQ:NT], K.ps[:, 1, m - 6, 0:CTX]).then_inc(y_out, 1)
                else:
                    act.activation(yt[:, :], bank_cols(K, m % 2), ACT.Identity,
                                   scale=K.S("pool_scale")[:, m:m + 1]).then_inc(y_out, 1)

        @block.vector
        def _(dve):
            own = Chain(dve, dve_own)
            edge = K.S("edge").rearrange("p (w s e) -> p w s e", w=4, s=2)
            for t, p0, p1, w in pieces:
                x = za[p0:p1, t, :]
                cur, n, s = x, PW, 1
                b = 0
                while s < w:
                    n -= s
                    nxt = win[p0:p1, b, :]
                    own.link(dve.tensor_tensor(nxt[:, 0:n], cur[:, 0:n], cur[:, s:s + n], ALU.add))
                    cur, s, b = nxt, 2 * s, 1 - b
                wi = w.bit_length() - 2
                for seg, at in enumerate(ZA_AT):
                    size = SEGS[seg][1]
                    first = at - w // 2
                    ends = cur[:, first:first + size].rearrange("p (s e) -> p s e", e=8)[:, ::size // 8 - 1, :]
                    own.link(dve.tensor_tensor(ends, ends, edge[p0:p1, wi, :, :], ALU.mult))
                for seg, at in enumerate(ZA_AT):
                    size = SEGS[seg][1]
                    first = at - w // 2
                    own.link(dve.scalar_tensor_tensor(za[p0:p1, t, at:at + size], cur[:, first:first + size], 1.0 / w,
                                                      za[p0:p1, t, at:at + size], ALU.mult, ALU.subtract))
            dve.sem_inc(pooled, 1)
            for n, m in enumerate(order):
                dve.wait_ge(y_out, n + 1)
                dve.tensor_copy(K.uhi[:, m, :], yt[:, :]).then_inc(y_hi, 1)
                dve.wait_ge(y_hi, n + 1)
                dve.tensor_tensor(K.ulo[:, m, :], yt[:, :], K.uhi[:, m, :], ALU.subtract).then_inc(y_split, 1)


def cd_in_phase(K):
    nc = K.nc
    st = K.place("cd_stage", [P, 3, NT], F32, at=K.s_at)
    W = Weights(K, "cdin", K.a["cd_in"], ZT)
    norm = Norm(K, 2)
    done, centre, ready = K.sem("cdin_done"), K.sem("cdin_centre"), K.sem("cdin_ready")
    dve_own = K.sem("cdin_dve_own")
    out = [K.sem(f"cdin_out{s}") for s in range(3)]
    rc = K.S("rconv")

    def conv(m):
        return 6 <= m < 18
    with nc.Block() as block:
        @block.sync
        def _(sp):
            W.load(sp)

        @block.gpsimd
        def _(pool):
            W.divide(pool, done, norm)

        @block.tensor
        def _(pe):
            norm.pe(pe)
            for m in range(ZT):
                pe.wait_ge(W.split, m + 1)
                if m >= 2:
                    pe.wait_ge(ready, m - 1)
                for k in range(KT):
                    mm = product(pe, K, m % 2, m % 3, K.uhi, K.ulo, k, k, COLS, k == 0, k == KT - 1)
                mm.then_inc(done, 1)

        @block.scalar
        def _(act):
            norm.act(act)
            n_conv = 0
            for m in range(ZT + 1):
                if m >= 1:
                    act.wait_ge(ready, m)
                    act.dma_start(K.z[m - 1], st[:, (m - 1) % 3, :]).then_inc(out[(m - 1) % 3], 16)
                if m == ZT:
                    break
                act.wait_ge(done, m + 1)
                if m >= 3:
                    act.wait_ge(out[m % 3], 16 * (m // 3))
                z, o = bank_cols(K, m % 2), st[:, m % 3, :]
                if conv(m):
                    act.activation(o, z, ACT.Identity, scale=rc[:, 12 + m - 6:13 + m - 6]).then_inc(centre, 1)
                elif m == 18:
                    act.activation(st[0:64, m % 3, :], z[0:64, :], ACT.Tanh)
                    act.copy(st[64:128, m % 3, :], z[64:128, :]).then_inc(ready, 1)
                elif m == 19:
                    act.activation(o, z, ACT.Sigmoid).then_inc(ready, 1)
                else:
                    act.copy(o, z).then_inc(ready, 1)
            for s in range(3):
                act.wait_ge(out[s], 16 * ((ZT - s + 2) // 3))

        @block.vector
        def _(dve):
            norm.dve(dve)
            own = Chain(dve, dve_own)
            for m in range(6, 18):
                dve.wait_ge(centre, m - 5)
                conv_taps(dve, K, own, st[:, m % 3, :], bank_cols(K, m % 2), rc[:, m - 6:m - 5],
                          rc[:, 24 + m - 6:25 + m - 6], SEGS).then_inc(ready, 1)


def attention_phase(K, g):
    nc, a = K.nc, K.a
    NB = SEQ // P
    at = [K.u_at]

    def buf(name, shape, dt=F32):
        t = K.place("att_" + name, shape, dt, at=at[0])
        at[0] += -(-4 * int(np.prod(shape[1:])) // 32) * 32
        assert at[0] <= K.s_end
        return t
    X = buf("x", [P, 3, NT])
    tab = buf("tab", [P, 2, SEQ])
    aux = buf("aux", [P, 3 * P + 384])
    v = buf("v", [64, NT])
    sink = buf("sink", [P, 4])
    vt = buf("vt", [P, 10, 66])
    sq = K.place("att_sq", [P, 3, NT], F32, at=K.w_at)
    rms = buf("rms", [P, 26, 2])
    qf = K.place("att_q_factor", [P, 16, 2, 64], F32, at=K.w_at + 23552)
    t1 = buf("t1", [P, 2, 2, 512])
    qh = buf("q_hi", [P, NB, 4, P], F32R)
    ql = buf("q_lo", [P, NB, 4, P], F32R)
    kk = buf("k_parts", [P, NT], F32R)
    eye = buf("eye", [P, P], F32R)
    band = buf("band", [P, 384], F32R)
    one8 = buf("one8", [P, P], F32R)
    mx = buf("max", [P, 2, 4])
    top = buf("top", [P, 2, 4])
    nhi = buf("neg_hi", [P, 2, 4], F32R)
    neg = buf("neg", [P, 2, 8])
    ds = buf("sink_off", [P, 2, 4])
    es = buf("sink_exp", [P, 2, 4])
    den = buf("den", [P, 4])
    rd = buf("rden", [P, 4])
    negT = buf("negT", [P, 2, 4, P], F32R)
    pT = buf("pT", [P, 2, 5, 4, P])
    yn = buf("yn", [P, 2, 4, 64])
    yo = K.place("att_out", [P, 2, SEQ], F32, at=K.w_at + 3 * NT * 4)
    hones, rot, hrow, band_in = aux[:, 0:P], aux[:, P:2 * P], aux[0:8, 2 * P:2 * P + 4], aux[:, 3 * P:]
    S = lambda n: K.sem("att_" + n)
    sq_done, summed, root_done, rms_done, rms_spread, normed, turned, cos_done, roped, dve_own = [
        S(x) for x in ("sq", "sum", "root", "rms", "rms_spread", "normed", "turned", "cos", "roped",
                       "dve_own")]
    k_in, aux_in, tab_in, v_in, sink_in = [S(x) for x in ("k_in", "aux_in", "tab_in", "v_in", "sink_in")]
    q_in, hi3_done, kc_hi = [S("q_in0"), S("q_in1")], S("hi3"), S("kc_hi")
    vt_done, vt_out, ones_set, consts, hi_done, lo_pool, lo_dve, qf_done = [
        S(x) for x in ("vt", "vt_out", "ones", "consts", "hi", "lo_pool", "lo_dve", "q_factor")]
    scored, maxed, neg_done, neg_turned, neg_spread, keyed, exp_done, es_done = [
        S(x) for x in ("scored", "maxed", "neg", "neg_turned", "neg_spread", "keyed", "exp", "sink_exp")]
    pv_done, scaled, y_turned, y_out, stored = [S(x) for x in ("pv", "scaled", "y_turned", "y_out", "stored")]
    chunks = [(2, 0, 512), (2, 512, 512)] + [(x, c, 512) for x in range(2) for c in (0, 512)] + [(2, SEQ, CTX)]
    NCK = len(chunks)
    ROT = NCK - 1
    col0 = {0: 10, 1: 18, 2: 0}
    s_ps = lambda n: K.ps[:, n % 2, 0:2, :].rearrange("p b c -> p (b c)")
    sT_ps = lambda n: K.ps[:, n % 2, 2, :]
    pv_ps = K.ps[:, 0, 3, 0:4 * 66].rearrange("p (h c) -> p h c", h=4)
    negT_ps = K.ps[0:8, 1, 3, 0:P]
    yT_ps = K.ps[:, 1, 3, 2 * P:4 * P]

    def keys(i):
        return list(range(max(i - 1, 0), min(i + 1, NB - 1) + 1))

    def tiles(i):
        return keys(i) + [8, 9]
    first = [sum(len(tiles(m)) for m in range(i)) for i in range(NB + 1)]

    with nc.Block() as block:
        @block.sync
        def _(sp):
            for half in range(2):
                sp.dma_start(X[64 * half:64 * half + 64, 2, :], K.z[4][bass.ds(64 * g, 64), :]).then_inc(k_in, 16)
            sp.dma_start(aux[:, :], a["att_aux"]).then_inc(aux_in, 16)
            sp.dma_start(X[:, 0, 0:SEQ], K.z[2 * g][:, 0:SEQ]).then_inc(q_in[0], 16)
            sp.dma_start(tab[:, :, :], a["rope"]).then_inc(tab_in, 16)
            sp.dma_start(X[:, 1, 0:SEQ], K.z[2 * g + 1][:, 0:SEQ]).then_inc(q_in[1], 16)
            sp.dma_start(v[:, :], K.z[5][bass.ds(64 * g, 64), :]).then_inc(v_in, 16)
            sp.dma_start(sink[:, :], a["sink"][g]).then_inc(sink_in, 16)
            sp.wait_ge(y_out, NB)
            for x in range(2):
                sp.dma_start(K.y[2 * g + x], yo[:, x, :]).then_inc(stored, 16)
            sp.wait_ge(stored, 32)

        @block.gpsimd
        def _(pool):
            pool.memset(vt[:, :, 64:66], 1.0).then_inc(ones_set, 1)
            pool.memset(ql[:, :, :, :].bitcast(F32), 0.0).then_inc(ones_set, 1)
            pool.memset(negT[:, :, :, :].bitcast(F32), 0.0).then_inc(ones_set, 1)
            pool.memset(one8[:, :].bitcast(F32), 0.0).then_inc(ones_set, 1)
            pool.wait_ge(tab_in, 16)

            def cos_part(j):
                x, c, w = chunks[j]
                pool.wait_ge(normed, j + 1)
                if j >= 2:
                    pool.wait_ge(roped, j - 1)
                pool.tensor_tensor(t1[:, j % 2, 0, 0:w], X[:, x, c:c + w], tab[:, 0, c:c + w],
                                   ALU.mult).then_inc(cos_done, 1)
            for j in range(ROT):
                cos_part(j)
            pool.wait_ge(cos_done, ROT)
            pool.wait_ge(hi_done, 1)
            pool.tensor_tensor(kk[64:128, 0:SEQ], X[64:128, 2, 0:SEQ], kk[64:128, 0:SEQ],
                               ALU.subtract).then_inc(lo_pool, 1)
            pool.wait_ge(hi_done, 5)
            for h in range(2):
                q = slice(64 * h, 64 * h + 64)
                pool.wait_ge(lo_pool, h + 1)
                pool.tensor_tensor(ql[0:64, :, h, :], X[q, 0, 0:SEQ].rearrange("p (b c) -> p b c", c=P),
                                   qh[q, :, h, :], ALU.subtract).then_inc(lo_pool, 1)

        @block.tensor
        def _(pe):
            pe.wait_ge(aux_in, 16)

            def sums_of(i, x):
                pe.wait_ge(sq_done, i + 1)
                for m in range(10 if x == 2 else 8):
                    mm = pe.matmul(K.ps[:, 1, 0, 2 * (col0[x] + m):2 * (col0[x] + m) + 2], sq[:, x, m * P:(m + 1) * P],
                                   hones[:, 0::64], start=True, stop=True)
                mm.then_inc(summed, 1)

            def factors(j):
                x, c, w = chunks[j]
                if j >= 2:
                    pe.wait_ge(normed, j - 1)
                for m in range(w // P):
                    m0 = c // P + m
                    r = rms[:, m0, 0:1].to_broadcast([P, P]) if x == 2 else qf[:, 8 * x + m0, :, :].rearrange(
                        "p h d -> p (h d)")
                    mm = pe.matmul(K.ps[:, 0, j % 2, m * P:(m + 1) * P], r, K.eye[:, :], start=True, stop=True)
                mm.then_inc(rms_spread, 1)
            sums_of(0, 2)
            pe.wait_ge(rms_done, 1)
            factors(0)
            sums_of(1, 0)
            for j in range(ROT):
                if j in (1, 3):
                    pe.wait_ge(qf_done, 1 + j // 2)
                if j == 2:
                    sums_of(2, 1)
                factors(j + 1)
                x, c, w = chunks[j]
                pe.wait_ge(normed, j + 1)
                if j >= 2:
                    pe.wait_ge(roped, j - 1)
                pe.matmul(K.ps[:, 0, 2 + j % 2, 0:w], rot, X[:, x, c:c + w], start=True,
                          stop=True).then_inc(turned, 1)
            pe.wait_ge(v_in, 16)
            for t in range(10):
                mm = pe.transpose(K.ps[:, 1, 2 + t // 5, (t % 5) * 64:(t % 5) * 64 + 64],
                                  v[:, t * P:(t + 1) * P], K.eye[0:64, 0:64])
            mm.then_inc(vt_done, 1)

            def scores(n):
                i, h = n // 4, n % 4
                ks = keys(i)
                W = P * len(ks)
                o = s_ps(n)
                if n >= 2:
                    pe.wait_ge(maxed, n - 1)
                off = (ks[0] - (i - 1)) * P
                pe.matmul(o[:, 0:W], eye[:, :], band[:, off:off + W], start=True, stop=False)
                pe.matmul(o[:, 0:W], qh[:, i, h, :], kk[:, ks[0] * P:ks[0] * P + W], start=False, stop=False)
                pe.matmul(o[:, 0:W], ql[:, i, h, :], kk[:, ks[0] * P:ks[0] * P + W], start=False, stop=True)
                for c, w in ((0, P), (P, P)) if W + CTX > 512 else ((0, CTX),):
                    pe.matmul(o[:, W + c:W + c + w], qh[:, i, h, :], kk[:, SEQ + c:SEQ + c + w],
                              start=True, stop=False)
                    mm = pe.matmul(o[:, W + c:W + c + w], ql[:, i, h, :], kk[:, SEQ + c:SEQ + c + w],
                                   start=False, stop=True)
                mm.then_inc(scored, 1)

            def keyed_scores(i, j):
                t = tiles(i)[j]
                n = first[i] + j
                o = sT_ps(n)
                if n >= 2:
                    pe.wait_ge(exp_done, n - 1)
                pe.matmul(o, kk[:, t * P:(t + 1) * P], qh[:, i, :, :], start=True, stop=False)
                pe.matmul(o, kk[:, t * P:(t + 1) * P], ql[:, i, :, :], start=False, stop=False)
                if t < 8 and t != i:
                    pe.matmul(o, band[:, (t - i + 1) * P:(t - i + 2) * P],
                              eye[:, :].rearrange("p (o c) -> p o c", o=1).to_broadcast([P, 4, P]),
                              start=False, stop=False)
                pe.wait_ge(neg_spread, i + 1)
                pe.matmul(o, one8[:, :], negT[:, i % 2, :, :], start=False, stop=True).then_inc(keyed, 1)

            def values(i):
                pe.wait_ge(exp_done, first[i + 1])
                if i >= 1:
                    pe.wait_ge(scaled, i)
                ts = tiles(i)
                for h in range(4):
                    for j, t in enumerate(ts):
                        mm = pe.matmul(pv_ps[:, h, 0:65], pT[:, i % 2, j, h, :], vt[:, t, 0:65],
                                       start=j == 0, stop=j == len(ts) - 1)
                mm.then_inc(pv_done, 1)

            def turn_out(i):
                pe.wait_ge(scaled, i + 1)
                if i >= 1:
                    pe.wait_ge(y_out, i)
                for x in range(2):
                    mm = pe.transpose(yT_ps[:, x * P:(x + 1) * P],
                                      yn[:, i % 2, 2 * x:2 * x + 2, :].rearrange("p h d -> p (h d)"), K.eye[:, :])
                mm.then_inc(y_turned, 1)

            pe.wait_ge(roped, ROT)
            pe.wait_ge(vt_out, 1)
            pe.wait_ge(ones_set, 3)
            pe.wait_ge(consts, 3)
            pe.wait_ge(hi_done, 7)
            pe.wait_ge(hi3_done, 2)
            pe.wait_ge(kc_hi, 1)
            pe.wait_ge(lo_pool, 3)
            pe.wait_ge(lo_dve, 3)
            for h in range(4):
                scores(h)
            for i in range(NB):
                pe.wait_ge(neg_done, i + 1)
                if i >= 1:
                    pe.wait_ge(neg_spread, i)
                pe.transpose(negT_ps, neg[:, i % 2, :], K.eye[:, :]).then_inc(neg_turned, 1)
                if i >= 2:
                    turn_out(i - 2)
                for j in range(5):
                    if j < 4 and i + 1 < NB:
                        scores(4 * (i + 1) + j)
                    if j < len(tiles(i)):
                        keyed_scores(i, j)
                if i >= 1:
                    values(i - 1)
            turn_out(NB - 2)
            values(NB - 1)
            turn_out(NB - 1)

        def q_hi(act, x, heads):
            act.wait_ge(roped, 2 * x + 4)
            for h in range(heads):
                src = X[64 * h:64 * h + 64, x, 0:SEQ].rearrange("p (b c) -> p b c", c=P)
                for half in range(2):
                    act.copy(qh[64 * half:64 * half + 64, :, 2 * x + h, :], src).then_inc(hi_done, 1)

        @block.scalar
        def _(act):
            def square(x, n):
                act.wait_ge(k_in if x == 2 else q_in[x], 32 if x == 2 else 16)
                act.activation(sq[:, x, 0:n], X[:, x, 0:n], ACT.Square).then_inc(sq_done, 1)

            def root(i, x, n):
                act.wait_ge(summed, i + 1)
                sums = K.ps[:, 1, 0, 2 * col0[x]:2 * (col0[x] + n)].rearrange("p (t h) -> p t h", h=2)
                act.activation(rms[:, col0[x]:col0[x] + n, :], sums, ACT.Sqrt,
                               bias=K.epsc[:, 0:1] if x == 2 else K.epsc[:, 1:2],
                               scale=1.0 / 64 if x == 2 else 1.0).then_inc(root_done, 1)
            square(2, NT)
            square(0, SEQ)
            root(0, 2, 10)
            square(1, SEQ)
            root(1, 0, 8)
            root(2, 1, 8)
            act.wait_ge(roped, 2)
            act.copy(kk[:, 0:SEQ], X[:, 2, 0:SEQ]).then_inc(hi_done, 1)
            q_hi(act, 0, 2)
            act.wait_ge(normed, NCK)
            act.copy(kk[:, SEQ:NT], X[:, 2, SEQ:NT]).then_inc(kc_hi, 1)
            act.wait_ge(vt_done, 1)
            act.copy(vt[:, :, 0:64].rearrange("p (b t) d -> p b t d", b=2),
                     K.ps[:, 1, 2:4, 0:320].rearrange("p b (t d) -> p b t d", d=64)).then_inc(vt_out, 1)
            q_hi(act, 1, 1)
            act.wait_ge(sink_in, 16)

            def out(i):
                act.wait_ge(y_turned, i + 1)
                act.copy(yo[:, :, i * P:(i + 1) * P],
                         yT_ps.rearrange("p (x c) -> p x c", x=2)).then_inc(y_out, 1)
            for i in range(NB):
                act.wait_ge(neg_done, i + 1)
                if i >= 2:
                    act.wait_ge(scaled, i - 1)
                act.activation(es[:, i % 2, :], ds[:, i % 2, :], ACT.Exp).then_inc(es_done, 1)
                for j in range(len(tiles(i))):
                    n = first[i] + j
                    act.wait_ge(keyed, n + 1)
                    if j == 0 and i >= 2:
                        act.wait_ge(pv_done, i - 1)
                    act.activation(pT[:, i % 2, j, :, :].rearrange("p h c -> p (h c)"), sT_ps(n),
                                   ACT.Exp).then_inc(exp_done, 1)
                    if j == 1 and i >= 2:
                        out(i - 2)
            out(NB - 2)
            out(NB - 1)

        @block.vector
        def _(dve):
            own = Chain(dve, dve_own)
            dve.wait_ge(aux_in, 16)
            dve.tensor_copy(eye[:, :], K.eye[:, :]).then_inc(consts, 1)
            dve.tensor_copy(band[:, :], band_in).then_inc(consts, 1)
            dve.wait_ge(ones_set, 4)
            dve.tensor_copy(one8[0:8, :], K.ones[0:8, :]).then_inc(consts, 1)

            def invert(i, x, n):
                dve.wait_ge(root_done, i + 1)
                r = rms[:, col0[x]:col0[x] + n, :]
                dve.reciprocal(r, r).then_inc(rms_done, 1)
                if x < 2:
                    dve.wait_ge(rms_done, i + 1)
                    dve.tensor_copy(qf[:, 8 * x:8 * x + 8, :, :], r.rearrange("p t (h o) -> p t h o", o=1).to_broadcast(
                        [P, 8, 2, 64])).then_inc(qf_done, 1)
            invert(0, 2, 10)

            def norm(j):
                x, c, w = chunks[j]
                dve.wait_ge(rms_spread, j + 1)
                dve.scalar_tensor_tensor(X[:, x, c:c + w], X[:, x, c:c + w], K.S("qn" if x < 2 else "kn"),
                                         K.ps[:, 0, j % 2, 0:w], ALU.mult, ALU.mult).then_inc(normed, 1)
            norm(0)
            for j in range(ROT):
                norm(j + 1)
                if j == 0:
                    dve.wait_ge(tab_in, 16)
                    invert(1, 0, 8)
                if j == 2:
                    invert(2, 1, 8)
                x, c, w = chunks[j]
                dve.wait_ge(turned, j + 1)
                own.link(dve.tensor_tensor(t1[:, j % 2, 1, 0:w], K.ps[:, 0, 2 + j % 2, 0:w], tab[:, 1, c:c + w],
                                           ALU.mult))
                dve.wait_ge(cos_done, j + 1)
                dve.tensor_tensor(X[:, x, c:c + w], t1[:, j % 2, 0, 0:w], t1[:, j % 2, 1, 0:w],
                                  ALU.add).then_inc(roped, 1)
            dve.wait_ge(roped, 6)
            src = X[64:128, 1, 0:SEQ].rearrange("p (b c) -> p b c", c=P)
            for half in range(2):
                dve.tensor_copy(qh[64 * half:64 * half + 64, :, 3, :], src).then_inc(hi3_done, 1)
            for h in (1, 0):
                if h == 0:
                    dve.wait_ge(hi_done, 7)
                else:
                    dve.wait_ge(hi3_done, 2)
                q = slice(64 * h, 64 * h + 64)
                dve.tensor_tensor(ql[0:64, :, 2 + h, :], X[q, 1, 0:SEQ].rearrange("p (b c) -> p b c", c=P),
                                  qh[q, :, 2 + h, :], ALU.subtract).then_inc(lo_dve, 1)
            dve.wait_ge(kc_hi, 1)
            dve.tensor_tensor(kk[64:128, SEQ:NT], X[64:128, 2, SEQ:NT], kk[64:128, SEQ:NT],
                              ALU.subtract).then_inc(lo_dve, 1)

            def maxima(i):
                for h in range(4):
                    n = 4 * i + h
                    dve.wait_ge(scored, n + 1)
                    dve.reduce_max(mx[:, i % 2, h:h + 1], s_ps(n)[:, 0:P * len(tiles(i))],
                                   AX.X).then_inc(maxed, 1)
                dve.wait_ge(maxed, 4 * (i + 1))
                s = i % 2
                own.link(dve.tensor_tensor(top[:, s, :], mx[:, s, :], sink[:, :], ALU.max))
                if i >= 2:
                    dve.wait_ge(es_done, i - 1)
                    dve.wait_ge(neg_turned, i - 1)
                dve.tensor_tensor(ds[:, s, :], sink[:, :], top[:, s, :], ALU.subtract)
                own.link(dve.tensor_scalar(nhi[:, s, :], top[:, s, :], -1.0, None, ALU.mult))
                dve.tensor_copy(neg[:, s, 0:4], nhi[:, s, :])
                dve.scalar_tensor_tensor(neg[:, s, 4:8], top[:, s, :], -1.0, nhi[:, s, :], ALU.mult,
                                         ALU.subtract).then_inc(neg_done, 1)

            def spread(i):
                dve.wait_ge(neg_turned, i + 1)
                if i >= 2:
                    dve.wait_ge(keyed, first[i - 1])
                dve.tensor_tensor(negT[0:8, i % 2, :, :],
                                  negT_ps.rearrange("p (o c) -> p o c", o=1).to_broadcast([8, 4, P]),
                                  hrow.rearrange("p (h o) -> p h o", o=1).to_broadcast([8, 4, P]),
                                  ALU.mult).then_inc(neg_spread, 1)

            def scale_out(i):
                dve.wait_ge(pv_done, i + 1)
                dve.wait_ge(es_done, i + 1)
                own.link(dve.tensor_tensor(den[:, :], pv_ps[:, :, 64], es[:, i % 2, :], ALU.add))
                own.link(dve.reciprocal(rd[:, :], den[:, :]))
                if i >= 2:
                    dve.wait_ge(y_turned, i - 1)
                dve.tensor_tensor(yn[:, i % 2, :, :], pv_ps[:, :, 0:64],
                                  rd[:, :].rearrange("p (h o) -> p h o", o=1).to_broadcast([P, 4, 64]),
                                  ALU.mult).then_inc(scaled, 1)
                dve.wait_ge(scaled, i + 1)
            dve.wait_ge(sink_in, 16)
            maxima(0)
            for i in range(NB):
                spread(i)
                if i >= 2:
                    scale_out(i - 2)
                if i + 1 < NB:
                    maxima(i + 1)
            scale_out(NB - 2)
            scale_out(NB - 1)


CL = 64
NC = NT // CL
NL = SEQ // CL
TOK = NT // P
DECAY = float(np.exp(-0.5))
UNITS = [(d, hp) for d in range(2) for hp in range(2)]


class Rwkv:

    def __init__(self, K):
        self.K = K
        self.at = K.u_at
        self.low = K.w_at

        def keep(name, shape):
            t = K.place("rw_" + name, shape, F32, at=self.at)
            self.at += -(-4 * int(np.prod(shape[1:])) // 32) * 32
            assert self.at <= K.s_end
            return t

        def low(name, shape):
            t = K.place("rw_" + name, shape, F32, at=self.low)
            self.low += -(-4 * int(np.prod(shape[1:])) // 32) * 32
            assert self.low <= K.u_at
            return t
        self.ar = keep("ar", [P, 2, TOK, 2, P])
        self.beta = keep("beta", [P, 2, NT])
        self.kappa = keep("kappa", [P, 2, NT])
        self.v = keep("v", [P, NT])
        self.bonus = low("bonus", [P, SEQ])
        self.gate = low("gate", [P, SEQ])
        self.pend = keep("pend", [P, 2, NC])
        self.mask = keep("mask", [P, 2, 2, P])
        self.level = keep("level", [P, 6, 2, P])
        self.hones = keep("hones", [P, P])
        self.vec = keep("vec", [P, 10])
        self.G = low("G", [P, 2, NC, CL])
        self.Q = low("Q", [P, 2, SEQ])
        self.HP = keep("HP", [P, 2, NC, CL])
        self.Y = low("Y", [P, SEQ])                  
        self.temp_at = self.at


def rwkv_prepare(K, p):
    nc, a = K.nc, K.a
    R = Rwkv(K)
    K.R = R
    t0 = R.temp_at

    def temp(i, name, n=NT, at=None):
        at = t0 + 4 * NT * i if at is None else at
        assert at + 4 * n <= K.s_end, (name, at + 4 * n - K.s_end)
        return K.place("rwp_" + name, [P, n], F32, at=at)
    k, kk, wa, sg, av, cc, ex = [temp(i, n) for i, n in enumerate(("k", "kk", "wa", "sg", "a", "c", "ex"))]
    base = K.w_at + 8192
    r = K.place("rwp_r", [P, NT], F32, at=base)
    x = K.place("rwp_x", [P, NT], F32, at=base + 5120)
    km = K.place("rwp_km", [P, NT], F32, at=base + 10240)
    gl = K.place("rwp_gl", [P, SEQ], F32, at=base + 15360)
    mats = K.place("rwp_mats", [P, 3 * P], F32, at=base + 19456)
    one = temp(7, "one")
    loads, e_own, d_own = K.sem("rwp_loads"), K.sem("rwp_act_own"), K.sem("rwp_dve_own")
    wl_done, al_done, wl_out, al_out, sq_done, summed, g_done, gate_out = [
        K.sem(f"rwp_{n}") for n in ("wl", "al", "wl_out", "al_out", "sq", "sum", "g", "gate_out")]
    root, c_done, bk_done, bsum, ex_done, ex_used, b_out = [K.sem(f"rwp_{n}") for n in
                                                     ("root", "c", "bk", "bsum", "ex", "ex_used", "b_out")]
    w0, a0 = (lambda d: R.vec[:, d:d + 1]), (lambda d: R.vec[:, 2 + d:3 + d])
    k_k, k_a, r_k = R.vec[:, 4:5], R.vec[:, 5:6], R.vec[:, 6:7]

    def chunked(t):
        return t.rearrange("p (c l) -> p c l", l=CL)

    def in_tiles(t):
        return t.rearrange("p (t c) -> p t c", c=P)
    with nc.Block() as block:
        @block.sync
        def _(sp):
            for t, n in ((k, 10), (r, 6), (R.v, 14)):
                sp.dma_start(t[:, :], K.z[n + p]).then_inc(loads, 16)
            sp.dma_start(wa[:, :], K.z[18]).then_inc(loads, 16)
            sp.dma_start(gl[:, :], K.z[19][:, 0:SEQ]).then_inc(loads, 16)
            sp.dma_start(mats[:, :], a["rw_mats"][p]).then_inc(loads, 16)
            sp.dma_start(R.vec[:, :], a["rw_vec"][p]).then_inc(loads, 16)
            sp.dma_start(R.hones[:, :], a["att_aux"][:, 0:P]).then_inc(loads, 16)
            sp.dma_start(R.mask[:, :, :, :], a["rw_mask"]).then_inc(loads, 16)
            sp.dma_start(R.level[:, :, :, :], a["rw_level"]).then_inc(loads, 16)
            sp.wait_ge(loads, 160)

        @block.tensor
        def _(pe):
            pe.wait_ge(loads, 160)
            pe.wait_ge(sq_done, 1)
            for c, (at, w) in enumerate(COLS):
                mm = pe.matmul(K.ps[:, 0, c, 0:w], R.hones[:, :], x[:, at:at + w], start=True, stop=True)
            mm.then_inc(summed, 1)
            for d in range(2):
                if d:
                    pe.wait_ge(wl_out, d)
                for c, (at, w) in enumerate(COLS):
                    mm = pe.matmul(K.ps[:, 1, c, 0:w], mats[0:64, d * P:(d + 1) * P], wa[0:64, at:at + w],
                                   start=True, stop=True)
                mm.then_inc(wl_done, 1)
                pe.wait_ge(root, 1)
                if d:
                    pe.wait_ge(al_out, d)
                for c, (at, w) in enumerate(COLS):
                    mm = pe.matmul(K.ps[:, 0, c, 0:w], mats[64:128, d * P:(d + 1) * P], wa[64:128, at:at + w],
                                   start=True, stop=True)
                mm.then_inc(al_done, 1)
            pe.wait_ge(wl_out, 2)
            for c, (at, w) in enumerate(COLS[:2]):
                mm = pe.matmul(K.ps[:, 1, c, :], mats[:, 2 * P:3 * P], gl[:, at:at + w], start=True, stop=True)
            mm.then_inc(g_done, 1)
            pe.wait_ge(bk_done, 1)
            for c, (at, w) in enumerate(COLS[:2]):
                mm = pe.matmul(K.ps[:, 1, 2 + c, :], R.hones[:, :], R.bonus[:, at:at + w], start=True, stop=True)
            mm.then_inc(bsum, 1)

        @block.scalar
        def _(act):
            own = Chain(act, e_own)
            act.wait_ge(summed, 1)
            act.activation(x[:, :], bank_cols(K, 0), ACT.Sqrt, bias=K.epsc[:, 0:1]).then_inc(root, 1)
            for d in range(2):
                act.wait_ge(wl_done, d + 1)
                if d:
                    act.wait_ge(c_done, d)
                act.activation(sg[:, :], bank_cols(K, 1), ACT.Sigmoid, bias=w0(d)).then_inc(wl_out, 1)
                act.wait_ge(al_done, d + 1)
                if d:
                    act.wait_ge(ex_used, 4 * d)
                act.activation(av[:, :], bank_cols(K, 0), ACT.Sigmoid, bias=a0(d)).then_inc(al_out, 1)
                act.wait_ge(c_done, d + 1)
                act.activation(ex[:, :], x[:, :], ACT.Exp, scale=-DECAY).then_inc(ex_done, 1)
                act.wait_ge(ex_used, 4 * d + 1)
                act.activation(ex[:, :], cc[:, :], ACT.Exp, scale=-DECAY).then_inc(ex_done, 1)
                act.wait_ge(ex_used, 4 * d + 2)
                act.activation(ex[:, :], cc[:, :], ACT.Exp, scale=DECAY).then_inc(ex_done, 1)
                act.activation(R.pend[:, d, :], R.pend[:, d, :], ACT.Exp, scale=-DECAY).then_inc(ex_done, 1)
            act.wait_ge(g_done, 1)
            act.copy(R.gate[:, :], K.ps[:, 1, 0:2, :].rearrange("p b c -> p (b c)")).then_inc(gate_out, 1)

        @block.gpsimd
        def _(pool):
            pool.memset(one[:, :], 1.0).then_inc(b_out, 1)
            pool.wait_ge(b_out, 1)
            pool.memset(one[:, 0::CL], 0.0).then_inc(b_out, 1)

        @block.vector
        def _(dve):
            own = Chain(dve, d_own)
            dve.wait_ge(loads, 160)
            own.link(dve.tensor_scalar(kk[:, :], k[:, :], k_k, None, ALU.mult))
            dve.tensor_tensor(x[:, :], kk[:, :], kk[:, :], ALU.mult).then_inc(sq_done, 1)
            dve.wait_ge(root, 1)
            own.link(dve.reciprocal(x[:, :], x[:, :]))
            own.link(dve.tensor_tensor(kk[:, :], kk[:, :], x[:, :], ALU.mult))
            for d in range(2):
                dve.wait_ge(wl_out, d + 1)
                dve.wait_ge(b_out, 2)
                own.link(dve.tensor_tensor_scan(cc[:, :], one[:, :], sg[:, :], 0.0, ALU.mult, ALU.add))
                end = chunked(cc[:, :])[:, :, CL - 1]
                own.link(dve.tensor_copy(R.pend[:, d, :], end))
                if d == 0:
                    dve.tensor_tensor(x[:, :], cc[:, :], sg[:, :], ALU.subtract).then_inc(c_done, 1)
                else:
                    tot = R.pend[:, d, :].rearrange("p (c o) -> p c o", o=1).to_broadcast([P, NC, CL])
                    own.link(dve.tensor_tensor(chunked(x[:, :]), tot, chunked(cc[:, :]), ALU.subtract))
                    dve.tensor_tensor(cc[:, :], x[:, :], sg[:, :], ALU.add).then_inc(c_done, 1)
                dve.wait_ge(al_out, d + 1)
                own.link(dve.tensor_scalar(km[:, :], av[:, :], -1.0, k_a, ALU.add, ALU.mult))
                own.link(dve.scalar_tensor_tensor(km[:, :], km[:, :], 1.0, k[:, :], ALU.add, ALU.mult))
                if d == 0:
                    own.link(dve.tensor_copy(R.bonus[:, :], km[:, 0:SEQ]))
                else:
                    own.link(dve.tensor_tensor(R.bonus[:, :], R.bonus[:, :], km[:, 0:SEQ], ALU.add))
                dve.wait_ge(ex_done, 4 * d + 1)
                dve.tensor_tensor(R.ar[:, d, :, 0, :], in_tiles(ex[:, :]), in_tiles(kk[:, :]),
                                  ALU.mult).then_inc(ex_used, 1)
                dve.wait_ge(ex_done, 4 * d + 2)
                dve.tensor_tensor(R.ar[:, d, :, 1, :], in_tiles(ex[:, :]), in_tiles(r[:, :]),
                                  ALU.mult).then_inc(ex_used, 1)
                own.link(dve.scalar_tensor_tensor(av[:, :], av[:, :], -1.0, kk[:, :], ALU.mult, ALU.mult))
                dve.wait_ge(ex_done, 4 * d + 3)
                dve.tensor_tensor(R.beta[:, d, :], av[:, :], ex[:, :], ALU.mult).then_inc(ex_used, 1)
                dve.tensor_tensor(R.kappa[:, d, :], km[:, :], ex[:, :], ALU.mult).then_inc(ex_used, 1)
                dve.wait_ge(ex_used, 4 * d + 4)
                dve.wait_ge(ex_done, 4 * d + 4)
            dve.scalar_tensor_tensor(R.bonus[:, :], r[:, 0:SEQ], r_k, R.bonus[:, :], ALU.mult,
                                     ALU.mult).then_inc(bk_done, 1)
            dve.wait_ge(bsum, 1)
            own.link(dve.tensor_tensor(R.bonus[:, :], K.ps[:, 1, 2:4, :].rearrange("p b c -> p (b c)"),
                                       R.v[:, 0:SEQ], ALU.mult))


def rwkv_chunks(K, p):
    nc = K.nc
    R = K.R
    t0 = [R.temp_at]

    def temp(name, shape):
        n = -(-4 * int(np.prod(shape[1:])) // 32) * 32
        t = K.place("rwc_" + name, shape, F32, at=t0[0])
        t0[0] += n
        assert t0[0] <= K.s_end, (name, t0[0] - K.s_end)
        return t
    TM = temp("tm", [P, 2, 5, P])
    AZ = temp("az", [P, 2, 4, P])
    SB = temp("sb", [P, 2, 2, 2, 2, P])
    SK = temp("sk", [P, 2, 2, 2, 2, P])
    M = temp("m", [P, 2, 4, P])
    X = temp("x", [P, 2, 4, 2, P])
    PX = temp("px", [P, 2, 4, P])
    TW = temp("tw", [P, 2, 4, P])
    pe_done = [K.sem(f"rwc_pe{s}") for s in range(2)]
    dve_done = [K.sem(f"rwc_dve{s}") for s in range(2)]
    act_done = [K.sem(f"rwc_act{s}") for s in range(2)]
    d_own = K.sem("rwc_dve_own")
    LV = 5
    STAGES = 3 + 2 * LV + 2

    def unit(t, d, hp):
        return slice(64 * hp, 64 * hp + 64), slice(t * P, (t + 1) * P)

    def eye_over(n):
        return K.eye[:, :].rearrange("p (o c) -> p o c", o=1).to_broadcast([P, n, P])

    def over_heads(m):
        return m.rearrange("p d (o c) -> p d o c", o=1).to_broadcast([P, 2, 2, P])

    def flip_d(m):
        return m[:, ::-1, :]

    def by_unit(x):
        return x.rearrange("p (d h) c -> p d h c", d=2)

    def pe_stage(pe, n, t, s):
        ps = K.ps[:, s]
        if n == 0:
            for d in range(2):
                pe.transpose(ps[:, 0, d * P:(d + 1) * P], R.ar[:, d, t, 0, :], K.eye[:, :])
                pe.transpose(ps[:, 0, (2 + d) * P:(3 + d) * P], R.beta[:, d, t * P:(t + 1) * P], K.eye[:, :])
                pe.transpose(ps[:, 1, d * P:(d + 1) * P], R.kappa[:, d, t * P:(t + 1) * P], K.eye[:, :])
            return pe.transpose(ps[:, 1, 2 * P:3 * P], R.v[:, t * P:(t + 1) * P], K.eye[:, :])
        if n == 1:
            for i, src in enumerate((R.beta, R.kappa)):
                for d, hp in UNITS:
                    q, tok = unit(t, d, hp)
                    mm = pe.matmul(ps[:, 2 * i + hp, d * 256:(d + 1) * 256], src[q, d, tok],
                                   R.ar[q, d, t, :, :], start=True, stop=True)
            return mm
        if n == 2:
            for d, hp in UNITS:
                q, tok = unit(t, d, hp)
                pe.matmul(ps[:, hp, d * P:(d + 1) * P], R.ar[q, d, t, 0, :], R.beta[q, d, tok],
                          start=True, stop=True)
            for d, hp in UNITS:
                u = 2 * d + hp
                mm = pe.matmul(ps[:, 2, u * 64:(u + 1) * 64], SK[:, s, hp, d, 0, :],
                               TM[:, s, 4, 64 * hp:64 * hp + 64], start=True, stop=True)
            return mm
        if n < 3 + 2 * LV:
            for u in range(4):
                if (n - 3) % 2 == 0:
                    mm = pe.matmul(ps[:, 0, u * P:(u + 1) * P], M[:, s, u, :], X[:, s, u, 1, :],
                                   start=True, stop=True)
                else:
                    bank, at = 1 + u // 2, (u % 2) * 256
                    if n < 2 + 2 * LV:
                        pe.matmul(ps[:, bank, at:at + P], PX[:, s, u, :], X[:, s, u, 0, :],
                                  start=True, stop=True)
                    mm = pe.matmul(ps[:, bank, at + P:at + 256], X[:, s, u, 0, :], PX[:, s, u, :],
                                   start=True, stop=True)
            return mm
        if n == 3 + 2 * LV:
            for u in range(4):
                mm = pe.matmul(ps[:, 3, u * P:(u + 1) * P], X[:, s, u, 1, :], AZ[:, s, u, :],
                               start=True, stop=True)
            return mm
        for d, hp in UNITS:
            u = 2 * d + hp
            hq = slice(64 * hp, 64 * hp + 64)
            for c in range(2):
                cq = slice(64 * c, 64 * c + 64)
                pe.matmul(ps[hq, c, d * P:d * P + 64], TW[cq, s, u, 0:64], TM[cq, s, d, hq],
                          start=True, stop=True)
                pe.matmul(ps[hq, c, d * P + 64:(d + 1) * P], TM[cq, s, 2 + d, hq], TM[cq, s, 4, hq],
                          start=True, stop=False)
                mm = pe.matmul(ps[hq, c, d * P + 64:(d + 1) * P], TM[cq, s, d, hq], TW[cq, s, u, 64:128],
                               start=False, stop=True)
            if t < SEQ // P:
                mm = pe.matmul(ps[hq, 2, d * P:(d + 1) * P], TW[:, s, u, 0:64], SB[:, s, hp, d, 1, :],
                               start=True, stop=True)
        if t < SEQ // P:
            for hp in range(2):
                hq = slice(64 * hp, 64 * hp + 64)
                for d in range(2):
                    pe.matmul(ps[hq, 3, 0:P], TM[:, s, 4, hq], SK[:, s, hp, d, 1, :], start=d == 0, stop=False)
                    mm = pe.matmul(ps[hq, 3, 0:P], TW[:, s, 2 * d + hp, 64:128], SB[:, s, hp, d, 1, :],
                                   start=False, stop=d == 1)
        return mm

    def act_stage(act, n, t, s):
        ps = K.ps[:, s]
        if n == 0:
            act.copy(AZ[:, s, :, 0:64], ps[:, 0, 0:256].rearrange("p (u c) -> p u c", u=4))
            act.copy(TM[:, s, 0:2, :], ps[:, 0, 256:512].rearrange("p (u c) -> p u c", u=2))
            return act.copy(TM[:, s, 2:5, :], ps[:, 1, 0:384].rearrange("p (u c) -> p u c", u=3))
        if n == 2:
            return act.copy(AZ[:, s, :, 64:128], ps[:, 2, 0:256].rearrange("p (u c) -> p u c", u=4))
        if n == 3 + 2 * LV:
            return act.copy(TW[:, s, :, :], ps[:, 3, :].rearrange("p (u c) -> p u c", u=4))
        if n == 4 + 2 * LV and t < SEQ // P:
            return act.copy(R.Y[:, t * P:(t + 1) * P], ps[:, 3, 0:P])
        return None

    def dve_stage(dve, own, n, t, s):
        ps = K.ps[:, s]
        if n == 1:
            for hp in range(2):
                for b, o in ((hp, SB), (2 + hp, SK)):
                    ins = dve.tensor_tensor(o[:, s, hp, :, :, :], ps[:, b, :].rearrange("p (d m c) -> p d m c", d=2, m=2),
                                            R.mask[:, :, :, :], ALU.mult)
            return ins
        if n == 2:
            own.link(dve.tensor_tensor(by_unit(M[:, s]), ps[:, 0:2, 0:256].rearrange("p h (d c) -> p d h c", d=2),
                                       over_heads(flip_d(R.mask[:, :, 0, :])), ALU.mult))
            sb = SB[:, s, :, :, 0, :].rearrange("p h d c -> p d h c")
            own.link(dve.tensor_tensor(by_unit(X[:, s, :, 1, :]), sb, over_heads(R.level[:, 0, :, :]), ALU.mult))
            own.link(dve.tensor_tensor(by_unit(X[:, s, :, 0, :]), by_unit(M[:, s]),
                                       over_heads(flip_d(R.level[:, 0, :, :])), ALU.mult))
            return dve.tensor_tensor(X[:, s].rearrange("p u m c -> p (u m) c"),
                                     X[:, s].rearrange("p u m c -> p (u m) c"), eye_over(8), ALU.add)
        if 3 <= n < 3 + 2 * LV:
            j = (n - 3) // 2
            if (n - 3) % 2 == 0:
                return dve.tensor_tensor(by_unit(PX[:, s]), by_unit(ps[:, 0, :].rearrange("p (u c) -> p u c", u=4)),
                                         over_heads(R.level[:, 1 + j, :, :]), ALU.mult)
            if j < LV - 1:
                x = X[:, s].rearrange("p u m c -> p (u m c)")
                return dve.tensor_tensor(x, x, ps[:, 1:3, :].rearrange("p b c -> p (b c)"), ALU.add)
            x = X[:, s, :, 1, :]
            return dve.tensor_tensor(x, x, ps[:, 1:3, :].rearrange("p b (u m c) -> p (b u) m c", u=2, m=2)[:, :, 1, :],
                                     ALU.add)
        if n == 4 + 2 * LV:
            c0 = 2 * t
            for d in range(2):
                gh = ps[:, 0:2, d * P:(d + 1) * P]
                dve.tensor_tensor(R.G[:, d, c0:c0 + 2, :], gh[:, :, 0:64],
                                  K.eye2[:, :].rearrange("p (o c) -> p o c", o=1).to_broadcast([P, 2, 64]), ALU.add)
                ins = dve.tensor_tensor(R.HP[:, d, c0:c0 + 2, :], gh[:, :, 64:128],
                                        R.pend[:, d, c0:c0 + 2].rearrange("p (c o) -> p c o", o=1)
                                        .to_broadcast([P, 2, 64]), ALU.mult)
            if t < SEQ // P:
                ins = dve.tensor_tensor(R.Q[:, :, t * P:(t + 1) * P],
                                        ps[:, 2, 0:256].rearrange("p (d c) -> p d c", d=2),
                                        R.ar[:, :, t, 1, :], ALU.add)
            return ins
        return None

    on_act = lambda n, t: n in (0, 2, 3 + 2 * LV) or (n == 4 + 2 * LV and t < SEQ // P)
    on_dve = lambda n, t: n in (1, 2, 4 + 2 * LV) or 3 <= n < 3 + 2 * LV
    steps = [(n, t, s) for pair in range(TOK // 2) for n in range(STAGES)
             for s, t in ((0, 2 * pair), (1, 2 * pair + 1))]

    def before(n, t, s):
        past = [(m, u) for m, u, q in steps if q == s]
        past = past[:past.index((n, t))]
        return sum(on_act(*x) for x in past), sum(on_dve(*x) for x in past)

    with nc.Block() as block:
        @block.tensor
        def _(pe):
            for n, t, s in steps:
                na, nd = before(n, t, s)
                if na:
                    pe.wait_ge(act_done[s], na)
                if nd:
                    pe.wait_ge(dve_done[s], nd)
                pe_stage(pe, n, t, s).then_inc(pe_done[s], 1)

        @block.scalar
        def _(act):
            for n, t, s in steps:
                if on_act(n, t):
                    act.wait_ge(pe_done[s], STAGES * (t // 2) + n + 1)
                    act_stage(act, n, t, s).then_inc(act_done[s], 1)

        @block.vector
        def _(dve):
            own = Chain(dve, d_own)
            for n, t, s in steps:
                if on_dve(n, t):
                    nd = before(n, t, s)[1]
                    dve.wait_ge(pe_done[s], STAGES * (t // 2) + n + 1)
                    if nd:
                        dve.wait_ge(dve_done[s], nd)
                    dve_stage(dve, own, n, t, s).then_inc(dve_done[s], 1)


def rwkv_scan(K, p):
    nc = K.nc
    R = K.R
    S = K.place("rws_s", [P, 2, NC, CL], F32, at=R.temp_at)
    sq = K.place("rws_sq", [P, SEQ], F32, at=R.temp_at + 8 * NC * CL)
    rs = K.place("rws_rs", [P, SEQ], F32, at=R.temp_at + 8 * NC * CL + 4 * SEQ)
    zero = K.place("rws_gneps", [P, 1], F32, at=R.temp_at + 8 * NC * CL + 8 * SEQ)
    order = [list(range(NL, NC)) + list(range(NL)), list(range(NC - 1, NL - 1, -1)) + list(range(NL - 1, -1, -1))]
    stepped = [K.sem("rws_step0"), K.sem("rws_step1")]
    moved = [K.sem("rws_move0"), K.sem("rws_move1")]
    y_done, added, mean_done, sq_done, var_done, root, own_s, fin, stored, eps_set = [
        K.sem(f"rws_{n}") for n in ("y", "added", "mean", "sq", "var", "root", "dve_own", "fin", "stored", "eps")]
    with nc.Block() as block:
        @block.gpsimd
        def _(pool):
            pool.memset(zero[:, :], 64e-5).then_inc(eps_set, 1)

        @block.tensor
        def _(pe):
            for n in range(1, NC - 1):
                for d in range(2):
                    pe.wait_ge(moved[d], n)
                    for hp in range(2):
                        q = slice(64 * hp, 64 * hp + 64)
                        mm = pe.matmul(K.ps[q, 0, d, 0:64], R.G[q, d, order[d][n], :], S[q, d, n, :],
                                       start=True, stop=True)
                    mm.then_inc(stepped[d], 1)
            for d in range(2):
                pe.wait_ge(moved[d], NC - 1)
            for c in range(NL):
                for hp in range(2):
                    q = slice(64 * hp, 64 * hp + 64)
                    for d in range(2):
                        mm = pe.matmul(K.ps[q, 1, c // 8, (c % 8) * 64:(c % 8) * 64 + 64],
                                       S[q, d, order[d].index(c), :], R.Q[q, d, c * 64:(c + 1) * 64],
                                       start=d == 0, stop=d == 1)
            mm.then_inc(y_done, 1)
            for src, done, ready, slot in ((R.Y, mean_done, added, 0), (sq, var_done, sq_done, 1)):
                pe.wait_ge(ready, 1)
                for c, (at, w) in enumerate(COLS[:2]):
                    mm = pe.matmul(K.ps[:, slot, 2 + c, :], R.hones[:, :], src[:, at:at + w], start=True, stop=True)
                mm.then_inc(done, 1)

        @block.vector
        def _(dve):
            own = Chain(dve, own_s)
            for d in range(2):
                dve.tensor_copy(S[:, d, 1, :], R.HP[:, d, order[d][0], :]).then_inc(moved[d], 1)
            for n in range(1, NC - 1):
                for d in range(2):
                    c = order[d][n]
                    dve.wait_ge(stepped[d], n)
                    dve.scalar_tensor_tensor(S[:, d, n + 1, :], K.ps[:, 0, d, 0:64], R.pend[:, d, c:c + 1],
                                             R.HP[:, d, c, :], ALU.mult, ALU.add).then_inc(moved[d], 1)
            both = lambda slot, b: K.ps[:, slot, b:b + 2, :].rearrange("p b c -> p (b c)")
            dve.wait_ge(y_done, 1)
            dve.tensor_tensor(R.Y[:, :], R.Y[:, :], both(1, 0), ALU.add).then_inc(added, 1)
            dve.wait_ge(added, 1)
            dve.wait_ge(mean_done, 1)
            own.link(dve.scalar_tensor_tensor(R.Y[:, :], both(0, 2), -1.0 / 64, R.Y[:, :], ALU.mult, ALU.add))
            dve.tensor_tensor(sq[:, :], R.Y[:, :], R.Y[:, :], ALU.mult).then_inc(sq_done, 1)
            dve.wait_ge(root, 1)
            own.link(dve.reciprocal(rs[:, :], rs[:, :]))
            own.link(dve.tensor_tensor(R.Y[:, :], R.Y[:, :], rs[:, :], ALU.mult))
            own.link(dve.tensor_scalar(R.Y[:, :], R.Y[:, :], R.vec[:, 7:8], R.vec[:, 8:9], ALU.mult, ALU.add))
            own.link(dve.tensor_tensor(R.Y[:, :], R.Y[:, :], R.bonus[:, :], ALU.add))
            dve.tensor_tensor(R.Y[:, :], R.Y[:, :], R.gate[:, :], ALU.mult).then_inc(fin, 1)

        @block.scalar
        def _(act):
            act.wait_ge(eps_set, 1)
            act.wait_ge(var_done, 1)
            act.activation(rs[:, :], K.ps[:, 1, 2:4, :].rearrange("p b c -> p (b c)"), ACT.Sqrt,
                           bias=zero[:, 0:1], scale=1.0 / 64).then_inc(root, 1)

        @block.sync
        def _(sp):
            sp.wait_ge(fin, 1)
            sp.dma_start(K.y[4 + p], R.Y[:, :]).then_inc(stored, 16)
            sp.wait_ge(stored, 16)


def cd_out_load_phase(K):
    nc = K.nc
    yt = K.place("cdo_y", [P, 2, SEQ], F32, at=K.s_at)
    y_in = [K.sem("cdo_in0"), K.sem("cdo_in1")]
    hi_done, split = K.sem("cdo_hi"), K.sem("cdo_split")
    with nc.Block() as block:
        @block.sync
        def _(sp):
            for k in range(KT):
                if k >= 2:
                    sp.wait_ge(split, k - 1)
                sp.dma_start(yt[:, k % 2, :], K.y[k]).then_inc(y_in[k % 2], 16)

        @block.vector
        def _(dve):
            for k in range(KT):
                dve.wait_ge(y_in[k % 2], 16 * (k // 2 + 1))
                dve.tensor_copy(K.uhi[:, k, 0:SEQ], yt[:, k % 2, :]).then_inc(hi_done, 1)
                dve.wait_ge(hi_done, k + 1)
                dve.tensor_tensor(K.ulo[:, k, 0:SEQ], yt[:, k % 2, :], K.uhi[:, k, 0:SEQ],
                                  ALU.subtract).then_inc(split, 1)


def store_phase(K):
    nc = K.nc
    stored = K.sem("stored")
    with nc.Block() as block:
        @block.sync
        def _(sp):
            for k in range(KT):
                sp.dma_start(K.out[k], K.h[:, k, 0:K.out.shape[2]]).then_inc(stored, 16)
            sp.wait_ge(stored, 16 * KT)


LAT_COLS, LAT_SEGS = COLS[:2], SEGS[:1]


def build(nc, a, out):
    K = Kernel(nc, a, out)
    K.z = nc.dram_tensor("z_scratch", (ZT, P, NT), F32, kind="Internal").ap()
    K.y = nc.dram_tensor("y_scratch", (KT, P, SEQ), F32, kind="Internal").ap()

    def per(n, phase):
        def run():
            with nc.Fori(0, n) as i:
                phase(i)
                K.phase_over()
        return run

    phases = [lambda: setup_phase(K),
              lambda: ab_in_phase(K),
              lambda: pool_fourier_phase(K),
              lambda: out_phase(K, "about", a["ab_out"], 0, COLS, SEGS),
              lambda: ffn_phase(K, 0, COLS, SEGS),
              lambda: cd_in_phase(K),
              per(2, lambda g: attention_phase(K, g)),
              ] + rwkv_phases(K, per) + [
              lambda: cd_out_load_phase(K),
              lambda: out_phase(K, "cdout", a["cd_out"], 1, LAT_COLS, LAT_SEGS),
              lambda: ffn_phase(K, 1, LAT_COLS, LAT_SEGS)]
    for f in phases[:STOP]:
        f()
        if K.sems:
            K.phase_over()
    store_phase(K)


def rwkv_phases(K, per):
    def pair(p):
        rwkv_prepare(K, p)
        K.phase_over()
        rwkv_chunks(K, p)
        K.phase_over()
        rwkv_scan(K, p)
    return [per(4, pair)]


def _tiles(v):
    return np.ascontiguousarray(v.reshape(-1, P).T)


def _blocks(w):
    k, m = w.shape
    return w.reshape(k // P, P, m // P, P).transpose(2, 1, 0, 3).reshape(m // P, P, k)


def _layout(i):
    f = {n: np.asarray(v) for n, v in i.items()}
    arr = {}
    x = np.concatenate([f["x"][0].T, f["ctx"][0].T], axis=1)
    arr["x"] = x.reshape(KT, P, NT)
    arr["ada"] = np.concatenate([
        f["ada_w"][l].reshape(KT, P, 12, 512).transpose(2, 1, 0, 3).reshape(12, P, KT * 512) for l in range(2)])
    cond = np.stack([_tiles(f["c"][0]), _tiles(f["c_ctx"])], axis=2).reshape(P, 16)
    ada_b = np.concatenate([_tiles(f["ada_b"][l]) for l in range(2)], axis=1)
    norm = np.concatenate([_tiles(f[n][l]) for l in range(2) for n in ("norm1", "norm2")], axis=1)
    conv = np.concatenate([_tiles(f["ffn_conv"][l, t]) for l in range(2) for t in range(3)], axis=1)
    edge = np.ones((4, 2, 8), np.float32)
    for wi, w in enumerate((2, 4, 8, 16)):
        for e in range(8):
            edge[wi, 0, e] = w / (min(e, w // 2) + w - w // 2)
            edge[wi, 1, e] = w / (w // 2 + min(w - w // 2, 8 - e))
    two = lambda v: np.concatenate([v, v])[:, None]
    rconv = np.concatenate([_tiles(f["rwkv_conv"][0, t]) for t in range(3)], axis=1)
    cols = {"cond": cond, "ada_b": ada_b, "norm": norm, "conv": conv, "pool_scale": _tiles(f["pool_scale"][0]),
            "edge": np.broadcast_to(edge.reshape(1, -1), (P, 64)), "qn": two(f["q_norm"][0]),
            "kn": two(f["k_norm"][0]), "rconv": rconv,
            "sink": np.broadcast_to(f["attn_sink"][0], (P, 8))}
    arr["small"] = np.concatenate([cols[n] for n, _ in _SMALL], axis=1)
    arr["ab_in"] = _blocks(f["ab_w_in"][0])
    arr["ab_out"] = _blocks(f["ab_w_out"][0])
    big = []
    for half in range(2):
        w = np.zeros((384, 384), np.float32)
        w[:192, :192] = f["pool_w"][0, 2 * half]
        w[192:, 192:] = f["pool_w"][0, 2 * half + 1]
        for m, ks in ((0, (0, 1)), (1, (0, 1, 2)), (2, (1, 2))):
            big += [w[k * P:(k + 1) * P, m * P:(m + 1) * P] for k in ks]
    arr["pool_w"] = np.stack(big, axis=1)
    ch = 2 * np.pi * (np.outer(np.arange(256), np.arange(256)) % 256) / 256
    as_k = lambda w: w.reshape(2, P, 256).transpose(1, 0, 2)
    arr["dft_ch"] = np.stack([as_k(np.cos(ch).astype(np.float32)), as_k(-np.sin(ch).astype(np.float32)),
                              as_k(f["fourier_w"][0])], axis=1)
    for name, n in (("dft_tok", SEQ), ("dft_ctx", CTX)):
        ang = 2 * np.pi * (np.outer(np.arange(n), np.arange(n)) % n) / n
        s = 1 / np.sqrt(n * 256)
        t = np.stack([np.cos(ang) * s, np.sin(ang) * s]).astype(np.float32)
        t = t.reshape(2, n // P, P, n).transpose(1, 2, 0, 3)
        arr[name] = t if n == SEQ else t.transpose(1, 0, 2, 3)
    ffn = []
    for l in range(2):
        up, down = _blocks(f["ffn_up"][l]), f["ffn_down"][l].reshape(FT, P, D)
        ups = [[up[2 * g], up[FT + 2 * g], up[2 * g + 1], up[FT + 2 * g + 1]] for g in range(GROUPS)]
        seq = ups[0] + ups[1] + [down[0], down[1]]
        for g in range(2, GROUPS):
            seq += ups[g] + [down[2 * g - 2], down[2 * g - 1]]
        seq += [down[FT - 2], down[FT - 1]]
        ffn.append(np.stack(seq))
    arr["ffn"] = np.stack(ffn)
    arr["cd_in"] = _blocks(f["cd_w_in"][0])
    arr["cd_out"] = _blocks(f["cd_w_out"][0])
    _constants(arr, f)
    return {n: np.ascontiguousarray(v, dtype=np.float32) for n, v in arr.items()}


OUT_COLS = SEQ
STOP = None


def _constants(arr, f):
    half = 32
    inv = (np.float32(10000.0) ** (-np.arange(0, half, 2, dtype=np.float32) / half)).astype(np.float32)
    t = np.arange(SEQ)
    pos = np.stack([t // GRID_W, t % GRID_W]).astype(np.float32)
    ang = np.concatenate([np.concatenate([pos[s][None, :] * inv[:, None]] * 2) for s in range(2)])
    ang = np.concatenate([ang, ang]).astype(np.float32)
    arr["rope"] = np.stack([np.cos(ang), np.sin(ang)], axis=1)
    d = np.arange(P)
    head = (d[:, None] // 64 == d[None, :] // 64).astype(np.float32)
    rot = np.zeros((P, P), np.float32)
    for m in range(P):
        if m % 32 < 16:
            rot[m + 16, m] = -1.0
        else:
            rot[m - 16, m] = 1.0
    j, r = np.arange(384)[None, :], np.arange(P)[:, None]
    band = np.where((j >= r) & (j <= r + 256), 0.0, -1e30).astype(np.float32)
    row = np.zeros((P, P), np.float32)
    row[:8, :4] = np.concatenate([np.eye(4), np.eye(4)])
    arr["att_aux"] = np.concatenate([head, rot, row, band], axis=1)
    ch, sub = d // CL, np.arange(P)
    mask = np.zeros((P, 2, 2, P), np.float32)
    level = np.zeros((P, 6, 2, P), np.float32)
    src, dst = sub[:, None], sub[None, :]
    same = (src // CL) == (dst // CL)
    for way in range(2):
        before = src < dst if way == 0 else src > dst
        mask[:, way, 0] = same & before
        mask[:, way, 1] = same & (before | (src == dst))
        for i in range(6):
            b = 1 << i
            near = (src // (2 * b)) == (dst // (2 * b))
            level[:, i, way] = near & ((src // b) != (dst // b)) & before
    arr["rw_mask"], arr["rw_level"] = mask, level
    col = lambda v: v.reshape(4, P)
    zero = np.zeros(512, np.float32)
    arr["rw_vec"] = np.stack([col(v) for v in (
        f["rwkv_w0"][0, 0], f["rwkv_w0"][0, 1], f["rwkv_a0"][0, 0], f["rwkv_a0"][0, 1], f["rwkv_k_k"][0],
        f["rwkv_k_a"][0], f["rwkv_r_k"][0].reshape(-1), f["rwkv_lnx_w"][0], f["rwkv_lnx_b"][0], zero)], axis=2)
    lora = [np.concatenate([f["rwkv_w2"][0, way], f["rwkv_a2"][0, way]]) for way in range(2)]
    lora.append(f["rwkv_g_up"][0])
    arr["rw_mats"] = np.stack([m.reshape(P, 4, P) for m in lora]).transpose(2, 1, 0, 3).reshape(4, P, 3 * P)
    arr["sink"] = np.broadcast_to(f["attn_sink"][0].reshape(2, 1, 4), (2, P, 4))


def kernel(**inputs):
    import concourse.bacc as bacc
    from concourse.bass_utils import run_bass_kernel_spmd

    arrays = _layout(inputs)
    nc = bacc.Bacc("TRN2", target_bir_lowering=False, num_devices=1)
    a = {n: nc.dram_tensor(f"in_{n}", v.shape, F32, kind="ExternalInput").ap() for n, v in arrays.items()}
    out = nc.dram_tensor("out", (KT, P, OUT_COLS), F32, kind="ExternalOutput").ap()
    build(nc, a, out)
    r = run_bass_kernel_spmd(nc, [{f"in_{n}": v for n, v in arrays.items()}], core_ids=[0])
    return r.results[0]["out"].reshape(D, OUT_COLS).T[None]
```

```python
import numpy as np
import concourse.bass as bass
from concourse import mybir

ALU = mybir.AluOpType
ACT = mybir.ActivationFunctionType
AX = mybir.AxisListType
F32 = mybir.dt.float32
F32R = mybir.dt.float32r

P = 128
D = 1024
KT = D // P
SEQ = 1024
CTX = 256
NT = SEQ + CTX
COLS = [(0, 512), (512, 512), (1024, 256)]
SEGS = [(0, SEQ), (SEQ, CTX)]
FF = 2816
FT = FF // P
GROUPS = FT // 2
EPS = 1e-6
GRID_W = 64
ZT = 2560 // P
ZA_AT = [8, 8 + SEQ + 16]
PW = ZA_AT[1] + CTX + 8


def za_col(at):
    return at + (ZA_AT[0] if at < SEQ else ZA_AT[1] - SEQ)


class Chain:

    def __init__(self, eng, sem, base=0):
        self.eng, self.sem, self.n, self.base = eng, sem, 0, base

    def link(self, ins):
        ins.then_inc(self.sem, 1)
        self.n += 1
        self.eng.wait_ge(self.sem, self.n + self.base)


class Kernel:
    def __init__(self, nc, a, out):
        self.nc, self.a, self.out = nc, a, out
        self.base = -(-nc.sbuf_base // 32) * 32
        self.top = 0
        self.sems = []
        place = self.place
        self.h = place("h", [P, KT, NT], F32)
        self.w_at = self.top
        self.raw = place("w_raw", [P, 2, KT * P], F32)
        self.whi = place("w_hi", [P, 3, KT * P], F32R)
        self.wlo = place("w_lo", [P, 3, KT * P], F32R)
        self.u_at = self.top
        self.uhi = place("u_hi", [P, KT, NT], F32R)
        self.ulo = place("u_lo", [P, KT, NT], F32R)
        self.s_at = self.top
        self.act_hi = place("act_hi", [P, 2, 2, NT], F32R)
        self.act_lo = place("act_lo", [P, 2, 2, NT], F32R)
        self.t_at = self.top
        self.top += 2 * NT * 4
        self.s_end = self.top
        self.mod = place("mod", [P, 2, 48, 2], F32)
        self.gs = place("gs", [P, 4, KT, 2], F32)
        self.small = place("small", [P, SMALL_N], F32)
        self.ones = place("ones", [P, P], F32)
        self.eye = place("eye", [P, P], F32)
        self.eye2 = place("eye2", [P, P // 2], F32)
        self.epsc = place("epsc", [P, 2], F32)
        self.zero = place("zero", [P, 2], F32)
        self.ps = nc.psum_tensor("ps", [P, 2, 4, 512], F32).__enter__()

    def place(self, name, shape, dt, at=None):
        size = -(-4 * int(np.prod(shape[1:])) // 32) * 32
        if at is None:
            at = self.top
            self.top += size
        return self.nc.alloc_sbuf_tensor_at(name, shape, dt, offset=self.base + at)

    def sem(self, name):
        sem = self.nc.alloc_semaphore(name)
        self.sems.append(sem)
        return sem

    def phase_over(self):
        self.nc.clear_and_free_semaphores(self.sems)
        self.nc.all_engine_barrier(sem_only=True)
        self.sems = []

    def S(self, name):
        o, n = SMALL[name]
        return self.small[:, o:o + n]

    def part(self, layer, part, k, cond):
        return self.mod[:, layer, part * KT + k, cond:cond + 1]


_SMALL = [("cond", 16), ("ada_b", 96), ("norm", 32), ("conv", 2 * 3 * 44), ("pool_scale", 6),
          ("edge", 4 * 16), ("qn", 1), ("kn", 1), ("rconv", 3 * 12), ("sink", 8)]
SMALL, _o = {}, 0
for _n, _c in _SMALL:
    SMALL[_n] = (_o, _c)
    _o += _c
SMALL_N = _o


class Weights:

    def __init__(self, K, name, dram, nblk):
        self.K, self.dram, self.nblk = K, dram, nblk
        self.loaded = [K.sem(f"{name}_w_loaded{s}") for s in range(2)]
        self.hi_done = K.sem(f"{name}_w_hi_done")
        self.split = K.sem(f"{name}_w_split")

    def load(self, sp):
        def pair(i, first):
            for s in range(2):
                if not first:
                    sp.wait_ge(self.split, 2 * i + s - 1)
                sp.dma_start(self.K.raw[:, s, :], self.dram[2 * i + s]).then_inc(self.loaded[s], 16)
        pair(0, True)
        with sp.Fori(1, self.nblk // 2) as i:
            pair(i, False)

    def divide_one(self, pool, raw, slot, nth, turn):
        K = self.K
        pool.wait_ge(self.loaded[raw], 16 * (turn + 1))
        pool.tensor_tensor(K.whi[:, slot, :], K.raw[:, raw, :], K.zero[:, 0:1].to_broadcast([P, KT * P]),
                           ALU.add).then_inc(self.hi_done, 1)
        pool.wait_ge(self.hi_done, nth + 1)
        pool.tensor_tensor(K.wlo[:, slot, :], K.raw[:, raw, :], K.whi[:, slot, :],
                           ALU.subtract).then_inc(self.split, 1)

    def divide(self, pool, tile_done, norm=None):
        for n in range(self.nblk):
            if norm is not None and n <= 3:
                norm.pool(pool, n)
            if n >= 3:
                pool.wait_ge(tile_done, n - 2)
            self.divide_one(pool, n % 2, n % 3, n, n // 2)


def product(pe, K, slot, s, xhi, xlo, k, sub, cols, start, stop):
    mm = None
    w = slice(sub * P, (sub + 1) * P)
    for n, (wt, x) in enumerate([(K.whi, xhi), (K.whi, xlo), (K.wlo, xhi)]):
        for c, (at, width) in enumerate(cols):
            mm = pe.matmul(K.ps[:, slot, c, 0:width], wt[:, s, w], x[:, k, at:at + width],
                           start=start and n == 0, stop=stop and n == 2)
    return mm


def bank_cols(K, slot, cols=COLS):
    n = cols[-1][0] + cols[-1][1]
    return K.ps[:, slot, :, :].rearrange("p b c -> p (b c)")[:, 0:n]


def setup_phase(K):
    nc, a = K.nc, K.a
    RING = 4
    ada = K.place("ada_ring", [P, RING, KT * 512], F32, at=K.u_at)
    row = K.place("mod_row", [2, 2, 512], F32, at=K.s_at)
    sc = K.place("silu_c", [P, KT, 2], F32, at=K.s_at + 8192)
    NCH = 2 * 12
    h_in, small_in, ada_in = K.sem("h_in"), K.sem("small_in"), [K.sem(f"ada_in{s}") for s in range(RING)]
    consts, silu_done, rows_done = K.sem("consts"), K.sem("silu_done"), K.sem("ada_rows_done")
    row_out, turned, mod_done = K.sem("ada_row_out"), K.sem("ada_turned"), K.sem("mod_done")
    gains, eye0 = K.sem("gains"), K.sem("eye_zero")
    with nc.Block() as block:
        @block.sync
        def _(sp):
            sp.dma_start(K.small[:, :], a["small"]).then_inc(small_in, 16)
            for n in range(NCH):
                if n >= RING:
                    sp.wait_ge(rows_done, n - RING + 1)
                sp.dma_start(ada[:, n % RING, :], a["ada"][n]).then_inc(ada_in[n % RING], 16)
                if n == NCH - 4:
                    for k in range(KT):
                        sp.dma_start(K.h[:, k, :], a["x"][k]).then_inc(h_in, 16)
            sp.wait_ge(h_in, 16 * KT)

        @block.gpsimd
        def _(pool):
            pool.memset(K.ones[:, :], 1.0).then_inc(consts, 1)
            pool.memset(K.epsc[:, 0:1], EPS).then_inc(consts, 1)
            pool.memset(K.epsc[:, 1:2], 64 * EPS).then_inc(consts, 1)
            pool.memset(K.zero[:, :], 0.0).then_inc(consts, 1)
            pool.memset(K.eye[:, :], 0.0).then_inc(eye0, 1)
            pool.wait_ge(eye0, 1)
            pool.affine_select(out=K.eye[:, :], in_=K.eye[:, :], compare_op=ALU.not_equal, fill=1.0,
                               base=0, pattern=[[-1, P]], channel_multiplier=1).then_inc(consts, 1)

        @block.scalar
        def _(act):
            act.wait_ge(small_in, 16)
            act.activation(sc[:, :, :], K.S("cond").rearrange("p (k c) -> p k c", c=2),
                           ACT.Silu).then_inc(silu_done, 1)
            for n in range(NCH):
                act.wait_ge(rows_done, n + 1)
                if n >= 2:
                    act.wait_ge(turned, n - 1)
                act.copy(row[:, n % 2, :], K.ps[0:2, 0, n % 2, :]).then_inc(row_out, 1)

        @block.tensor
        def _(pe):
            def turn(n):
                pe.wait_ge(row_out, n + 1)
                pe.wait_ge(consts, 5)
                if n >= 2:
                    pe.wait_ge(mod_done, n - 1)
                for j in range(4):
                    mm = pe.transpose(K.ps[:, 1, n % 2, 2 * j:2 * j + 2],
                                      row[:, n % 2, j * P:(j + 1) * P], K.eye[0:2, 0:2])
                mm.then_inc(turned, 1)
            pe.wait_ge(silu_done, 1)
            for n in range(NCH):
                pe.wait_ge(ada_in[n % RING], 16 * (n // RING + 1))
                if n >= 2:
                    pe.wait_ge(row_out, n - 1)
                for k in range(KT):
                    mm = pe.matmul(K.ps[0:2, 0, n % 2, :], sc[:, k, :], ada[:, n % RING, k * 512:(k + 1) * 512],
                                   start=k == 0, stop=k == KT - 1)
                mm.then_inc(rows_done, 1)
                if n:
                    turn(n - 1)
            turn(NCH - 1)

        @block.vector
        def _(dve):
            dve.wait_ge(small_in, 16)
            b = K.S("ada_b").rearrange("p (l t) -> p l t", l=2)
            for n in range(NCH):
                l, t = n // 12, 4 * (n % 12)
                dve.wait_ge(turned, n + 1)
                for c in range(2):
                    ins = dve.tensor_tensor(
                        K.mod[:, l, t:t + 4, c],
                        K.ps[:, 1, n % 2, 0:8].rearrange("p (j c) -> p j c", c=2)[:, :, c],
                        b[:, l, t:t + 4], ALU.add)
                ins.then_inc(mod_done, 1)
            dve.tensor_tensor(K.eye2[:, :], K.eye[:, 0:64], K.eye[:, 64:128], ALU.add).then_inc(gains, 1)
            dve.wait_ge(mod_done, NCH)
            g = K.S("norm").rearrange("p (n k) -> p n k", n=4)
            for n in range(4):
                part = 1 if n % 2 == 0 else 4
                for c in range(2):
                    dve.scalar_tensor_tensor(K.gs[:, n, :, c], K.mod[:, n // 2, part * KT:(part + 1) * KT, c],
                                             1.0, g[:, n, :], ALU.add, ALU.mult).then_inc(gains, 1)


class Norm:
    W = 256
    POOL_K = 2
    ACT_K = 3

    def __init__(self, K, n, n_tok=NT):
        self.K, self.n, self.chunks = K, n, n_tok // self.W
        tag, W = f"n{n}", self.W
        self.sq = K.place(f"{tag}_sq", [P, 2, KT, W], F32, at=K.s_at)
        self.t = K.place(f"{tag}_t", [P, 2, KT, W], F32, at=K.s_at + 16384)
        self.u = K.place(f"{tag}_u", [P, 2, KT, W], F32, at=K.s_at + 32768)
        self.r = K.place(f"{tag}_r", [P, 2 * self.chunks], F32, at=K.s_at + 49152)
        self.sq_done, self.summed, self.root, self.inverted, self.spread = [
            K.sem(f"{tag}_{x}") for x in ("sq", "sum", "root", "inverted", "spread")]
        self.paired, self.shifted_dve = K.sem(f"{tag}_paired"), K.sem(f"{tag}_shifted_dve")
        self.scaled, self.shifted, self.hi_done, self.lo_dve, self.lo_pool = [
            K.sem(f"{tag}_{x}") for x in ("scaled", "shifted", "hi", "lo_dve", "lo_pool")]

    def cols(self, c):
        return slice(c * self.W, (c + 1) * self.W)

    def gain_shift(self, m, k):
        cond = 1 if m * self.W >= SEQ else 0
        return (self.K.gs[:, self.n, k, cond:cond + 1],
                self.K.part(self.n // 2, 0 if self.n % 2 == 0 else 3, k, cond))

    def act(self, act):
        K = self.K

        def square(c):
            if c >= 2:
                act.wait_ge(self.summed, c - 1)
            act.activation(self.sq[:, c % 2, :, :], K.h[:, :, self.cols(c)], ACT.Square).then_inc(self.sq_done, 1)

        def shift_and_hi(m):
            act.wait_ge(self.scaled, m + 1)
            if m >= 2:
                act.wait_ge(self.lo_dve, m - 1)
                act.wait_ge(self.lo_pool, m - 1)
            for k in range(self.ACT_K):
                gain, shift = self.gain_shift(m, k)
                ins = act.activation(self.u[:, m % 2, k, :], self.t[:, m % 2, k, :], ACT.Identity, bias=shift,
                                     scale=gain)
            ins.then_inc(self.shifted, 1)
            act.wait_ge(self.shifted, m + 1)
            act.wait_ge(self.shifted_dve, m + 1)
            act.copy(K.uhi[:, :, self.cols(m)], self.u[:, m % 2, :, :]).then_inc(self.hi_done, 1)
        square(0)
        square(1)
        for c in range(self.chunks):
            act.wait_ge(self.summed, c + 1)
            act.activation(self.r[:, 2 * c:2 * c + 2], K.ps[:, 0, c % 2, 0:2], ACT.Sqrt, bias=K.epsc[:, 0:1],
                           scale=1.0 / D).then_inc(self.root, 1)
            if c + 2 < self.chunks:
                square(c + 2)
            if c >= 1:
                shift_and_hi(c - 1)
        shift_and_hi(self.chunks - 1)

    def pe(self, pe):
        K = self.K

        def sums(c):
            pe.wait_ge(self.paired, c + 1)
            if c >= 2:
                pe.wait_ge(self.root, c - 1)
            for m in range(2):
                for k in range(KT // 2):
                    mm = pe.matmul(K.ps[:, 0, c % 2, m:m + 1], self.sq[:, c % 2, k, m * P:(m + 1) * P],
                                   K.ones[:, 0:1], start=k == 0, stop=k == KT // 2 - 1)
            mm.then_inc(self.summed, 1)
        sums(0)
        for c in range(self.chunks):
            if c and c + 1 < self.chunks:
                sums(c + 1)
            pe.wait_ge(self.inverted, c + 1)
            if c >= 2:
                pe.wait_ge(self.scaled, c - 1)
            for m in range(2):
                mm = pe.matmul(K.ps[:, 0, 2 + c % 2, m * P:(m + 1) * P],
                               self.r[:, 2 * c + m:2 * c + m + 1].to_broadcast([P, P]), K.eye[:, :],
                               start=True, stop=True)
            mm.then_inc(self.spread, 1)
            if c == 0:
                sums(1)
        pe.wait_ge(self.lo_dve, self.chunks)
        pe.wait_ge(self.lo_pool, self.chunks)

    def dve(self, dve):
        K, kd = self.K, KT - self.POOL_K

        def invert(c):
            if c < self.chunks:
                dve.wait_ge(self.root, c + 1)
                r = self.r[:, 2 * c:2 * c + 2]
                dve.reciprocal(r, r).then_inc(self.inverted, 1)
        invert(0)
        for c in range(self.chunks + 1):
            if c < self.chunks:
                dve.wait_ge(self.spread, c + 1)
                if c >= 2:
                    dve.wait_ge(self.shifted, c - 1)
                dve.tensor_tensor(self.t[:, c % 2, :, :], K.h[:, :, self.cols(c)],
                                  K.ps[:, 0, 2 + c % 2, 0:self.W].rearrange("p (o w) -> p o w", o=1).to_broadcast(
                                      [P, KT, self.W]), ALU.mult).then_inc(self.scaled, 1)
                if c >= 2:
                    dve.wait_ge(self.lo_pool, c - 1)
                dve.wait_ge(self.scaled, c + 1)
                for k in range(self.ACT_K, KT):
                    gain, shift = self.gain_shift(c, k)
                    ins = dve.tensor_scalar(self.u[:, c % 2, k, :], self.t[:, c % 2, k, :], gain, shift, ALU.mult,
                                            ALU.add)
                ins.then_inc(self.shifted_dve, 1)
                dve.wait_ge(self.shifted_dve, c + 1)
                invert(c + 1)
            if c >= 1:
                m = c - 1
                dve.wait_ge(self.hi_done, m + 1)
                dve.tensor_tensor(K.ulo[:, 0:kd, self.cols(m)], self.u[:, m % 2, 0:kd, :],
                                  K.uhi[:, 0:kd, self.cols(m)], ALU.subtract).then_inc(self.lo_dve, 1)
                dve.wait_ge(self.lo_dve, m + 1)

    def pool(self, pool, block):
        K, kd, half = self.K, KT - self.POOL_K, KT // 2

        def pair(c):
            if c < self.chunks:
                pool.wait_ge(self.sq_done, c + 1)
                sq = self.sq[:, c % 2]
                pool.tensor_tensor(sq[:, 0:half, :], sq[:, 0:half, :], sq[:, half:KT, :],
                                   ALU.add).then_inc(self.paired, 1)

        def lo(m):
            if m < self.chunks:
                pool.wait_ge(self.hi_done, m + 1)
                pool.tensor_tensor(K.ulo[:, kd:KT, self.cols(m)], self.u[:, m % 2, kd:KT, :],
                                   K.uhi[:, kd:KT, self.cols(m)], ALU.subtract).then_inc(self.lo_pool, 1)
        order = [[(pair, 0), (pair, 1)], [(pair, 2), (pair, 3), (lo, 0)], [(pair, 4), (lo, 1), (lo, 2)],
                 [(lo, 3), (lo, 4)]]
        for step, c in order[block]:
            step(c)


def add_gated(dve, K, layer, part, m, slot, segs):
    for c, (at, n) in enumerate(segs):
        ins = dve.scalar_tensor_tensor(K.h[:, m, at:at + n], bank_cols(K, slot)[:, at:at + n],
                                       K.part(layer, part, m, c), K.h[:, m, at:at + n], ALU.mult, ALU.add)
    return ins


def out_phase(K, tag, dram, layer, cols, segs, y_dram=None):
    nc = K.nc
    W = Weights(K, tag, dram, KT)
    done, added = K.sem(f"{tag}_tile_done"), K.sem(f"{tag}_added")
    if y_dram is not None:
        y = K.place(f"{tag}_y", [P, KT, SEQ], F32, at=K.s_at)
        y_in = [K.sem(f"{tag}_y_in{k}") for k in range(KT)]
        y_hi, y_split = K.sem(f"{tag}_y_hi"), K.sem(f"{tag}_y_split")
    with nc.Block() as block:
        @block.scalar
        def _(act):
            if y_dram is not None:
                for k in range(KT):
                    act.dma_start(y[:, k, :], y_dram[k]).then_inc(y_in[k], 16)

        @block.sync
        def _(sp):
            W.load(sp)

        @block.gpsimd
        def _(pool):
            W.divide(pool, done)

        @block.tensor
        def _(pe):
            for m in range(KT):
                pe.wait_ge(W.split, m + 1)
                if m >= 2:
                    pe.wait_ge(added, m - 1)
                for k in range(KT):
                    if y_dram is not None and m == 0:
                        pe.wait_ge(y_split, k + 1)
                    mm = product(pe, K, m % 2, m % 3, K.uhi, K.ulo, k, k, cols, k == 0, k == KT - 1)
                mm.then_inc(done, 1)

        @block.vector
        def _(dve):
            if y_dram is not None:
                for k in range(KT):
                    dve.wait_ge(y_in[k], 16)
                    dve.tensor_copy(K.uhi[:, k, 0:SEQ], y[:, k, :]).then_inc(y_hi, 1)
                    dve.wait_ge(y_hi, k + 1)
                    dve.tensor_tensor(K.ulo[:, k, 0:SEQ], y[:, k, :], K.uhi[:, k, 0:SEQ],
                                      ALU.subtract).then_inc(y_split, 1)
            for m in range(KT):
                dve.wait_ge(done, m + 1)
                add_gated(dve, K, layer, 2, m, m % 2, segs).then_inc(added, 1)


def conv_taps(dve, K, chain, cv, psum, w0, w2, segs):
    for at, n in segs:
        chain.link(dve.scalar_tensor_tensor(cv[:, at + 1:at + n], psum[:, at:at + n - 1], w0,
                                            cv[:, at + 1:at + n], ALU.mult, ALU.add))
        last = dve.scalar_tensor_tensor(cv[:, at:at + n - 1], psum[:, at + 1:at + n], w2,
                                        cv[:, at:at + n - 1], ALU.mult, ALU.add)
        if at + n != segs[-1][0] + segs[-1][1]:
            chain.link(last)
    return last


def ffn_phase(K, layer, cols, segs, out=None):
    nc = K.nc
    tag = f"ffn{layer}"
    n_tok = cols[-1][0] + cols[-1][1]
    G = GROUPS
    W = Weights(K, tag, K.a["ffn"][layer], 6 * G)
    norm = Norm(K, 2 * layer + 1, n_tok)
    cv = K.place(f"{tag}_cv", [P, 2, NT], F32, at=K.t_at)
    up_done, down_done, added = [K.sem(f"{tag}_{x}") for x in ("up_done", "down_done", "added")]
    centre, conv_done, silu_done, act_ready = [K.sem(f"{tag}_{x}") for x in
                                               ("centre", "conv_done", "silu_done", "act_ready")]
    dve_own, stored = K.sem(f"{tag}_dve_own"), K.sem(f"{tag}_stored")
    tap0 = SMALL["conv"][0] + layer * 3 * 44

    def tap(t, g, q):
        at = tap0 + t * 44 + (q % 2) * FT + q // 2 + 2 * g
        return K.small[:, bass.ds(at, 1)]

    def schedule(up, down, engine):
        up(0, 0)
        up(1, 1)
        down(0, 0)
        with engine.Fori(1, (G - 1) // 2) as i:
            up(2 * i, 0)
            down(2 * i - 1, 1)
            up(2 * i + 1, 1)
            down(2 * i, 0)
        up(G - 1, 0)
        down(G - 2, 1)
        down(G - 1, 0)

    def is_early(g):
        return isinstance(g, int) and g < 2

    def is_last(g):
        return isinstance(g, int) and g == G - 1

    def before_up(g):
        return 4 * g if is_early(g) else 6 * g - 2

    def before_down(g):
        return 6 * g + (4 if is_last(g) else 8)

    with nc.Block() as block:
        @block.sync
        def _(sp):
            W.load(sp)
            if out is not None:
                for m in range(KT):
                    sp.wait_ge(added, 8 * (G - 1) + m + 1)
                    sp.dma_start(out[m], K.h[:, m, 0:n_tok]).then_inc(stored, 16)
                sp.wait_ge(stored, 16 * KT)

        @block.gpsimd
        def _(pool):
            def up(g, par):
                if is_early(g):
                    free = [[None, None, None, (up_done, 1)],
                            [(up_done, 4), (up_done, 2), (up_done, 3), (up_done, 5)]][g]
                else:
                    free = [(up_done, 4 * g), (down_done, 8 * (g - 1)), (down_done, 8 * (g - 1)),
                            (up_done, 4 * g + 1)]
                for q in range(4):
                    if is_early(g) and g == 0:
                        norm.pool(pool, q)
                    if free[q] is not None:
                        pool.wait_ge(*free[q])
                    turn = (2 * g if is_early(g) else 3 * g - 1) + q // 2
                    W.divide_one(pool, q % 2, q % 3, before_up(g) + q, turn)

            def down(g, par):
                for b in range(2):
                    if is_last(g):
                        pool.wait_ge(*((down_done, 8 * g) if b else (up_done, 4 * (g + 1))))
                    else:
                        pool.wait_ge(up_done, 4 * (g + 1) + 2 + b)
                    W.divide_one(pool, b, b if is_last(g) else 1 + b, before_down(g) + b, 3 * g + (2 if is_last(g) else 4))
            schedule(up, down, pool)

        @block.tensor
        def _(pe):
            def up(g, par):
                for q in range(4):
                    if not (is_early(g) and g == 0 and q < 2):
                        pe.wait_ge(conv_done, 4 * g + q - 1)
                    if not is_early(g) and q < 2:
                        pe.wait_ge(added, 8 * (g - 1) - 1 + q)
                    pe.wait_ge(W.split, before_up(g) + q + 1)
                    for k in range(KT):
                        mm = product(pe, K, q % 2, q % 3, K.uhi, K.ulo, k, k, cols, k == 0, k == KT - 1)
                    mm.then_inc(up_done, 1)

            def down(g, par):
                pe.wait_ge(W.split, before_down(g) + 2)
                pe.wait_ge(act_ready, 2 * g + 2)
                for m in range(KT):
                    if m < 2 and not is_last(g):
                        pe.wait_ge(conv_done, 4 * (g + 1) + 3 + m)
                    if m >= 2 or is_last(g):
                        pe.wait_ge(added, 8 * g + m - 1)
                    for f in range(2):
                        mm = product(pe, K, m % 2, f if is_last(g) else 1 + f, K.act_hi[:, par], K.act_lo[:, par], f, m,
                                     cols, f == 0, f == 1)
                    mm.then_inc(down_done, 1)
            norm.pe(pe)
            schedule(up, down, pe)

        @block.scalar
        def _(act):
            def up(g, par):
                for q in range(4):
                    x = q % 2
                    act.wait_ge(up_done, 4 * g + q + 1)
                    if not (is_early(g) and g == 0 and q < 2):
                        act.wait_ge(act_ready, 2 * g + q // 2)
                    act.activation(cv[:, x, 0:n_tok], bank_cols(K, q % 2, cols), ACT.Identity,
                                   scale=tap(1, g, q)).then_inc(centre, 1)
                    if x == 0:
                        act.wait_ge(conv_done, 4 * g + q + 1)
                        act.activation(cv[:, 0, 0:n_tok], cv[:, 0, 0:n_tok], ACT.Silu).then_inc(silu_done, 1)
            norm.act(act)
            schedule(up, lambda g, par: None, act)

        @block.vector
        def _(dve):
            per_conv = 2 * len(segs) - 1
            per_group = 2 * (2 * per_conv + 2)

            def activation(own, g, par, f):
                dve.wait_ge(conv_done, 4 * g + 2 * f + 2)
                dve.wait_ge(silu_done, 2 * g + f + 1)
                own.link(dve.tensor_tensor(cv[:, 1, 0:n_tok], cv[:, 1, 0:n_tok], cv[:, 0, 0:n_tok], ALU.mult))
                if not is_early(g) and f == 0:
                    dve.wait_ge(down_done, 8 * (g - 1))
                own.link(dve.tensor_copy(K.act_hi[:, par, f, 0:n_tok], cv[:, 1, 0:n_tok]))
                dve.tensor_tensor(K.act_lo[:, par, f, 0:n_tok], cv[:, 1, 0:n_tok],
                                  K.act_hi[:, par, f, 0:n_tok], ALU.subtract).then_inc(act_ready, 1)

            def up(g, par):
                own = Chain(dve, dve_own, per_group * g)
                for q in range(4):
                    x = q % 2
                    dve.wait_ge(centre, 4 * g + q + 1)
                    conv_taps(dve, K, own, cv[:, x, :], bank_cols(K, q % 2, cols), tap(0, g, q),
                              tap(2, g, q), segs).then_inc(conv_done, 1)
                    if q == 1 or (q == 3 and is_early(g) and g == 0):
                        activation(own, g, par, q // 2)

            def down(g, par):
                for m in range(KT):
                    dve.wait_ge(down_done, 8 * g + m + 1)
                    add_gated(dve, K, layer, 5, m, m % 2, segs).then_inc(added, 1)
                    if m == 1 and not is_last(g):
                        own = Chain(dve, dve_own, per_group * (g + 1) + per_group - 2)
                        activation(own, g + 1, 1 - par, 1)

            norm.dve(dve)
            schedule(up, down, dve)


def ab_in_phase(K):
    nc = K.nc
    K.za = K.place("za", [P, 6, PW], F32, at=K.s_at)
    K.zb = K.place("zb", [P, 2, NT], F32, at=K.s_at + 4 * 6 * PW)
    W = Weights(K, "abin", K.a["ab_in"], KT)
    norm = Norm(K, 0)
    done, stored, zeroed = K.sem("abin_done"), K.sem("abin_stored"), K.sem("abin_zeroed")
    with nc.Block() as block:
        @block.sync
        def _(sp):
            W.load(sp)

        @block.gpsimd
        def _(pool):
            W.divide(pool, done, norm)

        @block.tensor
        def _(pe):
            norm.pe(pe)
            for m in range(KT):
                pe.wait_ge(W.split, m + 1)
                if m >= 2:
                    pe.wait_ge(stored, m - 1)
                for k in range(KT):
                    mm = product(pe, K, m % 2, m % 3, K.uhi, K.ulo, k, k, COLS, k == 0, k == KT - 1)
                mm.then_inc(done, 1)

        @block.vector
        def _(dve):
            norm.dve(dve)
            dve.wait_ge(norm.lo_dve, norm.chunks)
            dve.wait_ge(norm.lo_pool, norm.chunks)
            dve.memset(K.za[:, :, :], 0.0).then_inc(zeroed, 1)

        @block.scalar
        def _(act):
            norm.act(act)
            act.wait_ge(zeroed, 1)
            for m in range(KT):
                act.wait_ge(done, m + 1)
                z = bank_cols(K, m % 2)
                if m < 6:
                    act.copy(K.za[:, m, ZA_AT[0]:ZA_AT[0] + SEQ], z[:, 0:SEQ])
                    act.copy(K.za[:, m, ZA_AT[1]:ZA_AT[1] + CTX], z[:, SEQ:NT]).then_inc(stored, 1)
                else:
                    act.copy(K.zb[:, m - 6, :], z).then_inc(stored, 1)


def pool_fourier_phase(K):
    nc, a = K.nc, K.a
    za, zb = K.za, K.zb
    PQ = K.place("dft_pq", [P, NT // P, 512], F32, at=K.u_at)
    mats = K.place("dft_mats", [P, 3, 2, 256], F32, at=K.u_at + 20480)
    G = K.place("dft_g", [P, 2, 512], F32, at=K.u_at + 26624)
    tab = K.place("dft_tab", [P, 2, 2, SEQ], F32, at=K.u_at + 40960)
    ctab = K.place("dft_ctab", [P, 2, 2, CTX], F32, at=K.u_at + 57344)
    pmat = K.place("pool_mats", [P, 14, P], F32, at=K.w_at)
    win = K.place("pool_win", [P, 2, PW], F32, at=K.w_at + 7168)
    yt = K.place("mix_y", [P, NT], F32, at=K.w_at + 7168 + 8 * PW)
    mats_in, ctab_in, pmat_in = K.sem("dft_mats_in"), K.sem("dft_ctab_in"), K.sem("pool_mats_in")
    tab_in = [K.sem("dft_tab_in0"), K.sem("dft_tab_in1")]
    g_done, g_out, pq_done, pq_out, tab_used = [K.sem(f"dft_{x}") for x in ("g", "g_out", "pq", "pq_out", "tab_used")]
    yb_done, dve_own, pooled, ya_done, y_out, y_hi, y_split = [
        K.sem(f"mix_{x}") for x in ("yb", "dve_own", "pooled", "ya", "y_out", "y_hi", "y_split")]
    TT = SEQ // P
    pieces = [(0, 0, 128, 2), (1, 0, 64, 2), (1, 64, 128, 4), (2, 0, 128, 4),
              (3, 0, 128, 8), (4, 0, 64, 8), (4, 64, 128, 16), (5, 0, 128, 16)]
    outs = [(0, [0, 1]), (1, [0, 1, 2]), (2, [1, 2])]
    order = [6, 7] + list(range(6))
    with nc.Block() as block:
        @block.sync
        def _(sp):
            sp.dma_start(mats[:, :, :, :], a["dft_ch"]).then_inc(mats_in, 16)
            for t in range(2):
                sp.dma_start(tab[:, t, :, :], a["dft_tok"][t]).then_inc(tab_in[t], 16)
            sp.dma_start(ctab[:, :, :, :], a["dft_ctx"]).then_inc(ctab_in, 16)
            sp.dma_start(pmat[:, :, :], a["pool_w"]).then_inc(pmat_in, 16)
            for t in range(2, TT):
                sp.wait_ge(tab_used, t - 1)
                sp.dma_start(tab[:, t % 2, :, :], a["dft_tok"][t]).then_inc(tab_in[t % 2], 16)

        @block.tensor
        def _(pe):
            pe.wait_ge(mats_in, 16)
            for m in range(2):
                for s in range(2):
                    for k in range(2):
                        mm = pe.matmul(K.ps[:, 0, m, s * 256:(s + 1) * 256], mats[:, s, k, m * P:(m + 1) * P],
                                       mats[:, 2, k, :], start=k == 0, stop=k == 1)
            mm.then_inc(g_done, 1)
            pe.wait_ge(g_out, 1)
            for t in range(NT // P):
                if t >= 4:
                    pe.wait_ge(pq_out, t - 3)
                for k in range(2):
                    mm = pe.matmul(K.ps[:, 1, t % 4, :], zb[:, k, t * P:(t + 1) * P], G[:, k, :],
                                   start=k == 0, stop=k == 1)
                mm.then_inc(pq_done, 1)
            for t in range(TT):
                pe.wait_ge(pq_out, t + 1)
                pe.wait_ge(tab_in[t % 2], 16 * (t // 2 + 1))
                for s in range(2):
                    for m in range(2):
                        for c in range(2):
                            mm = pe.matmul(K.ps[:, 0, 2 * m + c, :], PQ[:, t, s * 256 + m * P:s * 256 + (m + 1) * P],
                                           tab[:, t % 2, s, c * 512:(c + 1) * 512], start=t == 0 and s == 0,
                                           stop=t == TT - 1 and s == 1)
                mm.then_inc(tab_used, 1)
            pe.wait_ge(ctab_in, 16)
            pe.wait_ge(pq_out, NT // P)
            for m in range(2):
                for t in range(2):
                    for s in range(2):
                        mm = pe.matmul(K.ps[:, 1, m, 0:CTX], PQ[:, TT + t, s * 256 + m * P:s * 256 + (m + 1) * P],
                                       ctab[:, t, s, :], start=t == 0 and s == 0, stop=t == 1 and s == 1)
            mm.then_inc(yb_done, 1)
            pe.wait_ge(pmat_in, 16)
            pe.wait_ge(pooled, 1)
            n = 0
            for half in range(2):
                for o, ins in outs:
                    m = 3 * half + o
                    pe.wait_ge(y_out, max(2, m + 1))
                    for j, k in enumerate(ins):
                        for c, (at, w) in enumerate(COLS):
                            mm = pe.matmul(K.ps[:, m % 2, c, 0:w], pmat[:, n, :],
                                           za[:, 3 * half + k, za_col(at):za_col(at) + w],
                                           start=j == 0, stop=j == len(ins) - 1)
                        n += 1
                    mm.then_inc(ya_done, 1)

        @block.scalar
        def _(act):
            act.wait_ge(g_done, 1)
            act.copy(G[:, :, :], K.ps[:, 0, 0:2, :]).then_inc(g_out, 1)
            for t in range(NT // P):
                act.wait_ge(pq_done, t + 1)
                act.copy(PQ[:, t, :], K.ps[:, 1, t % 4, :]).then_inc(pq_out, 1)
            for n, m in enumerate(order):
                if n == 0:
                    act.wait_ge(yb_done, 1)
                if n >= 2:
                    act.wait_ge(ya_done, n - 1)
                if n >= 1:
                    act.wait_ge(y_split, n)
                if m >= 6:
                    act.copy(yt[:, 0:SEQ], K.ps[:, 0, 2 * (m - 6):2 * (m - 6) + 2, :].rearrange("p b c -> p (b c)"))
                    act.copy(yt[:, SEQ:NT], K.ps[:, 1, m - 6, 0:CTX]).then_inc(y_out, 1)
                else:
                    act.activation(yt[:, :], bank_cols(K, m % 2), ACT.Identity,
                                   scale=K.S("pool_scale")[:, m:m + 1]).then_inc(y_out, 1)

        @block.vector
        def _(dve):
            own = Chain(dve, dve_own)
            edge = K.S("edge").rearrange("p (w s e) -> p w s e", w=4, s=2)
            for t, p0, p1, w in pieces:
                x = za[p0:p1, t, :]
                cur, n, s = x, PW, 1
                b = 0
                while s < w:
                    n -= s
                    nxt = win[p0:p1, b, :]
                    own.link(dve.tensor_tensor(nxt[:, 0:n], cur[:, 0:n], cur[:, s:s + n], ALU.add))
                    cur, s, b = nxt, 2 * s, 1 - b
                wi = w.bit_length() - 2
                for seg, at in enumerate(ZA_AT):
                    size = SEGS[seg][1]
                    first = at - w // 2
                    ends = cur[:, first:first + size].rearrange("p (s e) -> p s e", e=8)[:, ::size // 8 - 1, :]
                    own.link(dve.tensor_tensor(ends, ends, edge[p0:p1, wi, :, :], ALU.mult))
                for seg, at in enumerate(ZA_AT):
                    size = SEGS[seg][1]
                    first = at - w // 2
                    own.link(dve.scalar_tensor_tensor(za[p0:p1, t, at:at + size], cur[:, first:first + size], 1.0 / w,
                                                      za[p0:p1, t, at:at + size], ALU.mult, ALU.subtract))
            dve.sem_inc(pooled, 1)
            for n, m in enumerate(order):
                dve.wait_ge(y_out, n + 1)
                dve.tensor_copy(K.uhi[:, m, :], yt[:, :]).then_inc(y_hi, 1)
                dve.wait_ge(y_hi, n + 1)
                dve.tensor_tensor(K.ulo[:, m, :], yt[:, :], K.uhi[:, m, :], ALU.subtract).then_inc(y_split, 1)


def cd_in_phase(K):
    nc = K.nc
    st = K.place("cd_stage", [P, 3, NT], F32, at=K.s_at)
    W = Weights(K, "cdin", K.a["cd_in"], ZT)
    norm = Norm(K, 2)
    done, centre, ready = K.sem("cdin_done"), K.sem("cdin_centre"), K.sem("cdin_ready")
    dve_own = K.sem("cdin_dve_own")
    out = [K.sem(f"cdin_out{s}") for s in range(3)]
    rc = K.S("rconv")

    def conv(m):
        return 6 <= m < 18

    def m_cols(m):
        return COLS[:2] if m < 4 or m == 19 else COLS
    with nc.Block() as block:
        @block.sync
        def _(sp):
            W.load(sp)

        @block.gpsimd
        def _(pool):
            W.divide(pool, done, norm)

        @block.tensor
        def _(pe):
            norm.pe(pe)
            for m in range(ZT):
                pe.wait_ge(W.split, m + 1)
                if m >= 2:
                    pe.wait_ge(ready, m - 1)
                for k in range(KT):
                    mm = product(pe, K, m % 2, m % 3, K.uhi, K.ulo, k, k, m_cols(m), k == 0, k == KT - 1)
                mm.then_inc(done, 1)

        @block.scalar
        def _(act):
            norm.act(act)
            for m in range(ZT + 1):
                if m >= 1:
                    act.wait_ge(ready, m)
                    n = sum(w for _, w in m_cols(m - 1))
                    act.dma_start(K.z[m - 1][:, 0:n], st[:, (m - 1) % 3, 0:n]).then_inc(out[(m - 1) % 3], 16)
                if m == ZT:
                    break
                act.wait_ge(done, m + 1)
                if m >= 3:
                    act.wait_ge(out[m % 3], 16 * (m // 3))
                z = bank_cols(K, m % 2, m_cols(m))
                o = st[:, m % 3, 0:sum(w for _, w in m_cols(m))]
                if conv(m):
                    act.activation(o, z, ACT.Identity, scale=rc[:, 12 + m - 6:13 + m - 6]).then_inc(centre, 1)
                elif m == 18:
                    act.activation(st[0:64, m % 3, :], z[0:64, :], ACT.Tanh)
                    act.copy(st[64:128, m % 3, :], z[64:128, :]).then_inc(ready, 1)
                elif m == 19:
                    act.activation(o, z, ACT.Sigmoid).then_inc(ready, 1)
                else:
                    act.copy(o, z).then_inc(ready, 1)
            for s in range(3):
                act.wait_ge(out[s], 16 * ((ZT - s + 2) // 3))

        @block.vector
        def _(dve):
            norm.dve(dve)
            own = Chain(dve, dve_own)
            for m in range(6, 18):
                dve.wait_ge(centre, m - 5)
                conv_taps(dve, K, own, st[:, m % 3, :], bank_cols(K, m % 2), rc[:, m - 6:m - 5],
                          rc[:, 24 + m - 6:25 + m - 6], SEGS).then_inc(ready, 1)


def attention_phase(K, g):
    nc, a = K.nc, K.a
    NB = SEQ // P
    at = [K.u_at]

    def buf(name, shape, dt=F32):
        t = K.place("att_" + name, shape, dt, at=at[0])
        at[0] += -(-4 * int(np.prod(shape[1:])) // 32) * 32
        assert at[0] <= K.s_end
        return t
    X = buf("x", [P, 3, NT])
    tab = buf("tab", [P, 2, SEQ])
    aux = buf("aux", [P, 3 * P + 384])
    v = buf("v", [64, NT])
    sink = buf("sink", [P, 4])
    vt = buf("vt", [P, 10, 66])
    sq = K.place("att_sq", [P, 3, NT], F32, at=K.w_at)
    rms = buf("rms", [P, 26, 2])
    qf = K.place("att_q_factor", [P, 16, 2, 64], F32, at=K.w_at + 23552)
    t1 = buf("t1", [P, 2, 2, 512])
    qh = buf("q_hi", [P, NB, 4, P], F32R)
    ql = buf("q_lo", [P, NB, 4, P], F32R)
    kk = buf("k_parts", [P, NT], F32R)
    eye = buf("eye", [P, P], F32R)
    band = buf("band", [P, 384], F32R)
    one8 = buf("one8", [P, P], F32R)
    mx = buf("max", [P, 2, 4])
    top = buf("top", [P, 2, 4])
    nhi = buf("neg_hi", [P, 2, 4], F32R)
    neg = buf("neg", [P, 2, 8])
    ds = buf("sink_off", [P, 2, 4])
    es = buf("sink_exp", [P, 2, 4])
    den = buf("den", [P, 4])
    rd = buf("rden", [P, 4])
    negT = buf("negT", [P, 2, 4, P], F32R)
    pT = buf("pT", [P, 2, 5, 4, P])
    yn = buf("yn", [P, 2, 4, 64])
    yo = K.place("att_out", [P, 2, SEQ], F32, at=K.w_at + 3 * NT * 4)
    hones, rot, hrow, band_in = aux[:, 0:P], aux[:, P:2 * P], aux[0:8, 2 * P:2 * P + 4], aux[:, 3 * P:]
    S = lambda n: K.sem("att_" + n)
    sq_done, summed, root_done, rms_done, rms_spread, normed, turned, cos_done, roped, dve_own = [
        S(x) for x in ("sq", "sum", "root", "rms", "rms_spread", "normed", "turned", "cos", "roped",
                       "dve_own")]
    k_in, aux_in, tab_in, v_in, sink_in = [S(x) for x in ("k_in", "aux_in", "tab_in", "v_in", "sink_in")]
    q_in, hi3_done, kc_hi = [S("q_in0"), S("q_in1")], S("hi3"), S("kc_hi")
    vt_done, vt_out, ones_set, consts, hi_done, lo_pool, lo_dve, qf_done = [
        S(x) for x in ("vt", "vt_out", "ones", "consts", "hi", "lo_pool", "lo_dve", "q_factor")]
    scored, maxed, neg_done, neg_turned, neg_spread, keyed, exp_done, es_done = [
        S(x) for x in ("scored", "maxed", "neg", "neg_turned", "neg_spread", "keyed", "exp", "sink_exp")]
    pv_done, scaled, y_turned, y_out, stored = [S(x) for x in ("pv", "scaled", "y_turned", "y_out", "stored")]
    chunks = [(2, 0, 512), (2, 512, 512)] + [(x, c, 512) for x in range(2) for c in (0, 512)] + [(2, SEQ, CTX)]
    NCK = len(chunks)
    ROT = NCK - 1
    col0 = {0: 10, 1: 18, 2: 0}
    s_ps = lambda n: K.ps[:, n % 2, 0:2, :].rearrange("p b c -> p (b c)")
    sT_ps = lambda n: K.ps[:, n % 2, 2, :]
    pv_ps = K.ps[:, 0, 3, 0:4 * 66].rearrange("p (h c) -> p h c", h=4)
    negT_ps = K.ps[0:8, 1, 3, 0:P]
    yT_ps = K.ps[:, 1, 3, 2 * P:4 * P]

    def keys(i):
        return list(range(max(i - 1, 0), min(i + 1, NB - 1) + 1))

    def tiles(i):
        return keys(i) + [8, 9]
    first = [sum(len(tiles(m)) for m in range(i)) for i in range(NB + 1)]

    with nc.Block() as block:
        @block.sync
        def _(sp):
            for half in range(2):
                sp.dma_start(X[64 * half:64 * half + 64, 2, :], K.z[4][bass.ds(64 * g, 64), :]).then_inc(k_in, 16)
            sp.dma_start(aux[:, :], a["att_aux"]).then_inc(aux_in, 16)
            sp.dma_start(X[:, 0, 0:SEQ], K.z[2 * g][:, 0:SEQ]).then_inc(q_in[0], 16)
            sp.dma_start(tab[:, :, :], a["rope"]).then_inc(tab_in, 16)
            sp.dma_start(X[:, 1, 0:SEQ], K.z[2 * g + 1][:, 0:SEQ]).then_inc(q_in[1], 16)
            sp.dma_start(v[:, :], K.z[5][bass.ds(64 * g, 64), :]).then_inc(v_in, 16)
            sp.dma_start(sink[:, :], a["sink"][g]).then_inc(sink_in, 16)
            sp.wait_ge(y_out, NB)
            for x in range(2):
                sp.dma_start(K.y[2 * g + x], yo[:, x, :]).then_inc(stored, 16)
            sp.wait_ge(stored, 32)

        @block.gpsimd
        def _(pool):
            pool.memset(vt[:, :, 64:66], 1.0).then_inc(ones_set, 1)
            pool.memset(ql[:, :, :, :].bitcast(F32), 0.0).then_inc(ones_set, 1)
            pool.memset(negT[:, :, :, :].bitcast(F32), 0.0).then_inc(ones_set, 1)
            pool.memset(one8[:, :].bitcast(F32), 0.0).then_inc(ones_set, 1)
            pool.wait_ge(tab_in, 16)

            def cos_part(j):
                x, c, w = chunks[j]
                pool.wait_ge(normed, j + 1)
                if j >= 2:
                    pool.wait_ge(roped, j - 1)
                pool.tensor_tensor(t1[:, j % 2, 0, 0:w], X[:, x, c:c + w], tab[:, 0, c:c + w],
                                   ALU.mult).then_inc(cos_done, 1)
            for j in range(ROT):
                cos_part(j)
            pool.wait_ge(cos_done, ROT)
            pool.wait_ge(hi_done, 1)
            pool.tensor_tensor(kk[64:128, 0:SEQ], X[64:128, 2, 0:SEQ], kk[64:128, 0:SEQ],
                               ALU.subtract).then_inc(lo_pool, 1)
            pool.wait_ge(hi_done, 5)
            for h in range(2):
                q = slice(64 * h, 64 * h + 64)
                pool.wait_ge(lo_pool, h + 1)
                pool.tensor_tensor(ql[0:64, :, h, :], X[q, 0, 0:SEQ].rearrange("p (b c) -> p b c", c=P),
                                   qh[q, :, h, :], ALU.subtract).then_inc(lo_pool, 1)

        @block.tensor
        def _(pe):
            pe.wait_ge(aux_in, 16)

            def sums_of(i, x):
                pe.wait_ge(sq_done, i + 1)
                for m in range(10 if x == 2 else 8):
                    mm = pe.matmul(K.ps[:, 1, 0, 2 * (col0[x] + m):2 * (col0[x] + m) + 2], sq[:, x, m * P:(m + 1) * P],
                                   hones[:, 0::64], start=True, stop=True)
                mm.then_inc(summed, 1)

            def factors(j):
                x, c, w = chunks[j]
                if j >= 2:
                    pe.wait_ge(normed, j - 1)
                for m in range(w // P):
                    m0 = c // P + m
                    r = rms[:, m0, 0:1].to_broadcast([P, P]) if x == 2 else qf[:, 8 * x + m0, :, :].rearrange(
                        "p h d -> p (h d)")
                    mm = pe.matmul(K.ps[:, 0, j % 2, m * P:(m + 1) * P], r, K.eye[:, :], start=True, stop=True)
                mm.then_inc(rms_spread, 1)
            sums_of(0, 2)
            pe.wait_ge(rms_done, 1)
            factors(0)
            sums_of(1, 0)
            for j in range(ROT):
                if j in (1, 3):
                    pe.wait_ge(qf_done, 1 + j // 2)
                if j == 2:
                    sums_of(2, 1)
                factors(j + 1)
                x, c, w = chunks[j]
                pe.wait_ge(normed, j + 1)
                if j >= 2:
                    pe.wait_ge(roped, j - 1)
                pe.matmul(K.ps[:, 0, 2 + j % 2, 0:w], rot, X[:, x, c:c + w], start=True,
                          stop=True).then_inc(turned, 1)
            pe.wait_ge(v_in, 16)
            for t in range(10):
                mm = pe.transpose(K.ps[:, 1, 2 + t // 5, (t % 5) * 64:(t % 5) * 64 + 64],
                                  v[:, t * P:(t + 1) * P], K.eye[0:64, 0:64])
            mm.then_inc(vt_done, 1)

            def scores(n):
                i, h = n // 4, n % 4
                ks = keys(i)
                W = P * len(ks)
                o = s_ps(n)
                if n >= 2:
                    pe.wait_ge(maxed, n - 1)
                off = (ks[0] - (i - 1)) * P
                pe.matmul(o[:, 0:W], eye[:, :], band[:, off:off + W], start=True, stop=False)
                pe.matmul(o[:, 0:W], qh[:, i, h, :], kk[:, ks[0] * P:ks[0] * P + W], start=False, stop=False)
                pe.matmul(o[:, 0:W], ql[:, i, h, :], kk[:, ks[0] * P:ks[0] * P + W], start=False, stop=True)
                for c, w in ((0, P), (P, P)) if W + CTX > 512 else ((0, CTX),):
                    pe.matmul(o[:, W + c:W + c + w], qh[:, i, h, :], kk[:, SEQ + c:SEQ + c + w],
                              start=True, stop=False)
                    mm = pe.matmul(o[:, W + c:W + c + w], ql[:, i, h, :], kk[:, SEQ + c:SEQ + c + w],
                                   start=False, stop=True)
                mm.then_inc(scored, 1)

            def keyed_scores(i, j):
                t = tiles(i)[j]
                n = first[i] + j
                o = sT_ps(n)
                if n >= 2:
                    pe.wait_ge(exp_done, n - 1)
                pe.matmul(o, kk[:, t * P:(t + 1) * P], qh[:, i, :, :], start=True, stop=False)
                pe.matmul(o, kk[:, t * P:(t + 1) * P], ql[:, i, :, :], start=False, stop=False)
                if t < 8 and t != i:
                    pe.matmul(o, band[:, (t - i + 1) * P:(t - i + 2) * P],
                              eye[:, :].rearrange("p (o c) -> p o c", o=1).to_broadcast([P, 4, P]),
                              start=False, stop=False)
                pe.wait_ge(neg_spread, i + 1)
                pe.matmul(o, one8[:, :], negT[:, i % 2, :, :], start=False, stop=True).then_inc(keyed, 1)

            def values(i):
                pe.wait_ge(exp_done, first[i + 1])
                if i >= 1:
                    pe.wait_ge(scaled, i)
                ts = tiles(i)
                for h in range(4):
                    for j, t in enumerate(ts):
                        mm = pe.matmul(pv_ps[:, h, 0:65], pT[:, i % 2, j, h, :], vt[:, t, 0:65],
                                       start=j == 0, stop=j == len(ts) - 1)
                mm.then_inc(pv_done, 1)

            def turn_out(i):
                pe.wait_ge(scaled, i + 1)
                if i >= 1:
                    pe.wait_ge(y_out, i)
                for x in range(2):
                    mm = pe.transpose(yT_ps[:, x * P:(x + 1) * P],
                                      yn[:, i % 2, 2 * x:2 * x + 2, :].rearrange("p h d -> p (h d)"), K.eye[:, :])
                mm.then_inc(y_turned, 1)

            pe.wait_ge(roped, ROT)
            pe.wait_ge(vt_out, 1)
            pe.wait_ge(ones_set, 3)
            pe.wait_ge(consts, 3)
            pe.wait_ge(hi_done, 7)
            pe.wait_ge(hi3_done, 2)
            pe.wait_ge(kc_hi, 1)
            pe.wait_ge(lo_pool, 3)
            pe.wait_ge(lo_dve, 3)
            for h in range(4):
                scores(h)
            for i in range(NB):
                pe.wait_ge(neg_done, i + 1)
                if i >= 1:
                    pe.wait_ge(neg_spread, i)
                if i >= 3:
                    pe.wait_ge(y_out, i - 2)
                pe.transpose(negT_ps, neg[:, i % 2, :], K.eye[:, :]).then_inc(neg_turned, 1)
                for j in range(5):
                    if j == 2 and i >= 2:
                        turn_out(i - 2)
                    if j < 4 and i + 1 < NB:
                        scores(4 * (i + 1) + j)
                    if j < len(tiles(i)):
                        keyed_scores(i, j)
                if i >= 1:
                    values(i - 1)
            turn_out(NB - 2)
            values(NB - 1)
            turn_out(NB - 1)

        def q_hi(act, x, heads):
            act.wait_ge(roped, 2 * x + 4)
            for h in range(heads):
                src = X[64 * h:64 * h + 64, x, 0:SEQ].rearrange("p (b c) -> p b c", c=P)
                for half in range(2):
                    act.copy(qh[64 * half:64 * half + 64, :, 2 * x + h, :], src).then_inc(hi_done, 1)

        @block.scalar
        def _(act):
            def square(x, n):
                act.wait_ge(k_in if x == 2 else q_in[x], 32 if x == 2 else 16)
                act.activation(sq[:, x, 0:n], X[:, x, 0:n], ACT.Square).then_inc(sq_done, 1)

            def root(i, x, n):
                act.wait_ge(summed, i + 1)
                sums = K.ps[:, 1, 0, 2 * col0[x]:2 * (col0[x] + n)].rearrange("p (t h) -> p t h", h=2)
                act.activation(rms[:, col0[x]:col0[x] + n, :], sums, ACT.Sqrt,
                               bias=K.epsc[:, 0:1] if x == 2 else K.epsc[:, 1:2],
                               scale=1.0 / 64 if x == 2 else 1.0).then_inc(root_done, 1)
            square(2, NT)
            square(0, SEQ)
            root(0, 2, 10)
            square(1, SEQ)
            root(1, 0, 8)
            root(2, 1, 8)
            act.wait_ge(roped, 2)
            act.copy(kk[:, 0:SEQ], X[:, 2, 0:SEQ]).then_inc(hi_done, 1)
            q_hi(act, 0, 2)
            act.wait_ge(normed, NCK)
            act.copy(kk[:, SEQ:NT], X[:, 2, SEQ:NT]).then_inc(kc_hi, 1)
            act.wait_ge(vt_done, 1)
            act.copy(vt[:, :, 0:64].rearrange("p (b t) d -> p b t d", b=2),
                     K.ps[:, 1, 2:4, 0:320].rearrange("p b (t d) -> p b t d", d=64)).then_inc(vt_out, 1)
            q_hi(act, 1, 1)
            act.wait_ge(sink_in, 16)

            def out(i):
                act.wait_ge(y_turned, i + 1)
                act.copy(yo[:, :, i * P:(i + 1) * P],
                         yT_ps.rearrange("p (x c) -> p x c", x=2)).then_inc(y_out, 1)
            for i in range(NB):
                act.wait_ge(neg_done, i + 1)
                if i >= 2:
                    act.wait_ge(scaled, i - 1)
                act.activation(es[:, i % 2, :], ds[:, i % 2, :], ACT.Exp).then_inc(es_done, 1)
                for j in range(len(tiles(i))):
                    n = first[i] + j
                    act.wait_ge(keyed, n + 1)
                    if j == 0 and i >= 2:
                        act.wait_ge(pv_done, i - 1)
                    act.activation(pT[:, i % 2, j, :, :].rearrange("p h c -> p (h c)"), sT_ps(n),
                                   ACT.Exp).then_inc(exp_done, 1)
                    if j == 2 and i >= 2:
                        out(i - 2)
            out(NB - 2)
            out(NB - 1)

        @block.vector
        def _(dve):
            own = Chain(dve, dve_own)
            dve.wait_ge(aux_in, 16)
            dve.tensor_copy(eye[:, :], K.eye[:, :]).then_inc(consts, 1)
            dve.tensor_copy(band[:, :], band_in).then_inc(consts, 1)
            dve.wait_ge(ones_set, 4)
            dve.tensor_copy(one8[0:8, :], K.ones[0:8, :]).then_inc(consts, 1)

            def invert(i, x, n):
                dve.wait_ge(root_done, i + 1)
                r = rms[:, col0[x]:col0[x] + n, :]
                dve.reciprocal(r, r).then_inc(rms_done, 1)
                if x < 2:
                    dve.wait_ge(rms_done, i + 1)
                    dve.tensor_copy(qf[:, 8 * x:8 * x + 8, :, :], r.rearrange("p t (h o) -> p t h o", o=1).to_broadcast(
                        [P, 8, 2, 64])).then_inc(qf_done, 1)
            invert(0, 2, 10)

            def norm(j):
                x, c, w = chunks[j]
                dve.wait_ge(rms_spread, j + 1)
                dve.scalar_tensor_tensor(X[:, x, c:c + w], X[:, x, c:c + w], K.S("qn" if x < 2 else "kn"),
                                         K.ps[:, 0, j % 2, 0:w], ALU.mult, ALU.mult).then_inc(normed, 1)
            norm(0)
            for j in range(ROT):
                norm(j + 1)
                if j == 0:
                    dve.wait_ge(tab_in, 16)
                    invert(1, 0, 8)
                if j == 2:
                    invert(2, 1, 8)
                x, c, w = chunks[j]
                dve.wait_ge(turned, j + 1)
                own.link(dve.tensor_tensor(t1[:, j % 2, 1, 0:w], K.ps[:, 0, 2 + j % 2, 0:w], tab[:, 1, c:c + w],
                                           ALU.mult))
                dve.wait_ge(cos_done, j + 1)
                dve.tensor_tensor(X[:, x, c:c + w], t1[:, j % 2, 0, 0:w], t1[:, j % 2, 1, 0:w],
                                  ALU.add).then_inc(roped, 1)
            dve.wait_ge(roped, 6)
            src = X[64:128, 1, 0:SEQ].rearrange("p (b c) -> p b c", c=P)
            for half in range(2):
                dve.tensor_copy(qh[64 * half:64 * half + 64, :, 3, :], src).then_inc(hi3_done, 1)
            for h in (1, 0):
                if h == 0:
                    dve.wait_ge(hi_done, 7)
                else:
                    dve.wait_ge(hi3_done, 2)
                q = slice(64 * h, 64 * h + 64)
                dve.tensor_tensor(ql[0:64, :, 2 + h, :], X[q, 1, 0:SEQ].rearrange("p (b c) -> p b c", c=P),
                                  qh[q, :, 2 + h, :], ALU.subtract).then_inc(lo_dve, 1)
            dve.wait_ge(kc_hi, 1)
            dve.tensor_tensor(kk[64:128, SEQ:NT], X[64:128, 2, SEQ:NT], kk[64:128, SEQ:NT],
                              ALU.subtract).then_inc(lo_dve, 1)

            def maxima(i):
                for h in range(4):
                    n = 4 * i + h
                    dve.wait_ge(scored, n + 1)
                    dve.reduce_max(mx[:, i % 2, h:h + 1], s_ps(n)[:, 0:P * len(tiles(i))],
                                   AX.X).then_inc(maxed, 1)
                dve.wait_ge(maxed, 4 * (i + 1))
                s = i % 2
                own.link(dve.tensor_tensor(top[:, s, :], mx[:, s, :], sink[:, :], ALU.max))
                if i >= 2:
                    dve.wait_ge(es_done, i - 1)
                    dve.wait_ge(neg_turned, i - 1)
                dve.tensor_tensor(ds[:, s, :], sink[:, :], top[:, s, :], ALU.subtract)
                own.link(dve.tensor_scalar(nhi[:, s, :], top[:, s, :], -1.0, None, ALU.mult))
                dve.tensor_copy(neg[:, s, 0:4], nhi[:, s, :])
                dve.scalar_tensor_tensor(neg[:, s, 4:8], top[:, s, :], -1.0, nhi[:, s, :], ALU.mult,
                                         ALU.subtract).then_inc(neg_done, 1)

            def spread(i):
                dve.wait_ge(neg_turned, i + 1)
                if i >= 2:
                    dve.wait_ge(keyed, first[i - 1])
                dve.tensor_tensor(negT[0:8, i % 2, :, :],
                                  negT_ps.rearrange("p (o c) -> p o c", o=1).to_broadcast([8, 4, P]),
                                  hrow.rearrange("p (h o) -> p h o", o=1).to_broadcast([8, 4, P]),
                                  ALU.mult).then_inc(neg_spread, 1)

            def scale_out(i):
                dve.wait_ge(pv_done, i + 1)
                dve.wait_ge(es_done, i + 1)
                own.link(dve.tensor_tensor(den[:, :], pv_ps[:, :, 64], es[:, i % 2, :], ALU.add))
                own.link(dve.reciprocal(rd[:, :], den[:, :]))
                if i >= 2:
                    dve.wait_ge(y_turned, i - 1)
                dve.tensor_tensor(yn[:, i % 2, :, :], pv_ps[:, :, 0:64],
                                  rd[:, :].rearrange("p (h o) -> p h o", o=1).to_broadcast([P, 4, 64]),
                                  ALU.mult).then_inc(scaled, 1)
                dve.wait_ge(scaled, i + 1)
            dve.wait_ge(sink_in, 16)
            maxima(0)
            for i in range(NB):
                spread(i)
                if i >= 2:
                    scale_out(i - 2)
                if i + 1 < NB:
                    maxima(i + 1)
            scale_out(NB - 2)
            scale_out(NB - 1)


CL = 64
NC = NT // CL
NL = SEQ // CL
TOK = NT // P
DECAY = float(np.exp(-0.5))
UNITS = [(d, hp) for d in range(2) for hp in range(2)]


class Rwkv:

    def __init__(self, K):
        self.K = K
        self.at = K.u_at
        self.low = K.w_at

        def keep(name, shape):
            t = K.place("rw_" + name, shape, F32, at=self.at)
            self.at += -(-4 * int(np.prod(shape[1:])) // 32) * 32
            assert self.at <= K.s_end
            return t

        def low(name, shape):
            t = K.place("rw_" + name, shape, F32, at=self.low)
            self.low += -(-4 * int(np.prod(shape[1:])) // 32) * 32
            assert self.low <= K.u_at
            return t
        self.ar = keep("ar", [P, 2, TOK, 2, P])
        self.beta = keep("beta", [P, 2, NT])
        self.kappa = keep("kappa", [P, 2, NT])
        self.v = keep("v", [P, NT])
        self.bonus = low("bonus", [P, SEQ])
        self.gate = low("gate", [P, SEQ])
        self.pend = keep("pend", [P, 2, NC])
        self.mask = keep("mask", [P, 2, 2, P])
        self.level = keep("level", [P, 6, 2, P])
        self.hones = keep("hones", [P, P])
        self.vec = keep("vec", [P, 10])
        self.G = low("G", [P, 2, NC, CL])
        self.Q = low("Q", [P, 2, SEQ])
        self.HP = keep("HP", [P, 2, NC, CL])
        self.Y = low("Y", [P, SEQ])
        self.temp_at = self.at


def rwkv_prepare(K, p):
    nc, a = K.nc, K.a
    R = Rwkv(K)
    K.R = R
    t0 = R.temp_at

    def temp(i, name):
        assert t0 + 4 * NT * (i + 1) <= K.s_end, name
        return K.place("rwp_" + name, [P, NT], F32, at=t0 + 4 * NT * i)
    k, kk, wa = [temp(i, n) for i, n in enumerate(("k", "kk", "wa"))]
    sg, av, cc = [[temp(3 + 2 * i + d, f"{n}{d}") for d in range(2)] for i, n in enumerate(("sg", "a", "c"))]
    cx = [sg[0], temp(9, "cx")]
    ex = [temp(10 + i, f"ex{i}") for i in range(3)]
    fac = ex[0][:, :].rearrange("p (t h d) -> p t h d", h=2, d=64)
    base = K.w_at + 8192
    r = K.place("rwp_r", [P, NT], F32, at=base)
    km = [K.place(f"rwp_km{d}", [P, NT], F32, at=base + 5120 * (1 + d)) for d in range(2)]
    kk2 = km[1]
    one = K.place("rwp_one", [P, NT], F32, at=base + 15360)
    mats = K.place("rwp_mats", [P, 3 * P], F32, at=base + 20480)
    inv = K.place("rwp_inv", [P, TOK, 2], F32, at=base + 22016)
    gl = R.gate
    names = ("k_in", "wa_in", "r_in", "v_in", "gl_in", "kk2", "sum", "root", "inv", "fac", "spread", "kk", "one",
             "sg", "a", "c", "akk", "km", "km_sum", "ex", "ar", "bk", "wl", "al", "g", "gate", "own", "bonus", "bsum",
             "tail_in")
    (k_in, wa_in, r_in, v_in, gl_in, kk2_done, summed, root, inverted, fac_done, spread, kk_done, one_set, sg_done,
     a_done, c_done, akk_done, km_done, km_sum, ex_done, used, bk_done, wl_done, al_done, g_done, gate_out, d_own,
     bonus_done, bsum, tail_in) = [K.sem("rwp_" + n) for n in names]
    w0, a0 = (lambda d: R.vec[:, d:d + 1]), (lambda d: R.vec[:, 2 + d:3 + d])
    k_k, k_a, r_k = R.vec[:, 4:5], R.vec[:, 5:6], R.vec[:, 6:7]

    def chunked(t):
        return t.rearrange("p (c l) -> p c l", l=CL)

    def in_tiles(t):
        return t.rearrange("p (t c) -> p t c", c=P)
    with nc.Block() as block:
        @block.sync
        def _(sp):
            sp.dma_start(R.vec[:, :], a["rw_vec"][p]).then_inc(k_in, 16)
            sp.dma_start(R.hones[:, :], a["att_aux"][:, 0:P]).then_inc(k_in, 16)
            sp.dma_start(k[:, :], K.z[10 + p]).then_inc(k_in, 16)
            sp.dma_start(mats[:, :], a["rw_mats"][p]).then_inc(wa_in, 16)
            sp.dma_start(wa[:, :], K.z[18]).then_inc(wa_in, 16)
            sp.dma_start(r[:, :], K.z[6 + p]).then_inc(r_in, 16)
            sp.dma_start(gl[:, :], K.z[19][:, 0:SEQ]).then_inc(gl_in, 16)
            sp.dma_start(R.v[:, :], K.z[14 + p]).then_inc(v_in, 16)
            sp.dma_start(R.mask[:, :, :, :], a["rw_mask"]).then_inc(tail_in, 16)
            sp.dma_start(R.level[:, :, :, :], a["rw_level"]).then_inc(tail_in, 16)
            sp.wait_ge(tail_in, 32)

        @block.tensor
        def _(pe):
            def wide(slot, lhsT, x, cols=COLS, bank=0):
                for c, (at, w) in enumerate(cols):
                    mm = pe.matmul(K.ps[:, slot, bank + c, 0:w], lhsT, x[:, at:at + w], start=True, stop=True)
                return mm
            wide_w = lambda d: wide(1, mats[0:64, d * P:(d + 1) * P], wa[0:64, :]).then_inc(wl_done, 1)
            wide_a = lambda d: wide(0, mats[64:128, d * P:(d + 1) * P], wa[64:128, :]).then_inc(al_done, 1)
            pe.wait_ge(wa_in, 32)
            wide_w(0)
            wide_a(0)
            pe.wait_ge(kk2_done, 1)
            for m in range(TOK):
                mm = pe.matmul(K.ps[:, 0, 3, 2 * m:2 * m + 2], kk2[:, m * P:(m + 1) * P], R.hones[:, 0::64],
                               start=True, stop=True)
            mm.then_inc(summed, 1)
            pe.wait_ge(sg_done, 1)
            wide_w(1)
            pe.wait_ge(a_done, 1)
            wide_a(1)
            pe.wait_ge(sg_done, 2)
            pe.wait_ge(fac_done, 1)
            for m in range(TOK):
                mm = pe.matmul(K.ps[:, 1, m // 4, (m % 4) * P:(m % 4 + 1) * P],
                               fac[:, m, :, :].rearrange("p h d -> p (h d)"), K.eye[:, :], start=True, stop=True)
            mm.then_inc(spread, 1)
            pe.wait_ge(a_done, 2)
            pe.wait_ge(gl_in, 16)
            wide(0, mats[:, 2 * P:3 * P], gl, COLS[:2]).then_inc(g_done, 1)
            pe.wait_ge(kk_done, 1)
            pe.wait_ge(bk_done, 1)
            wide(1, R.hones[:, :], R.bonus, COLS[:2]).then_inc(bsum, 1)

        @block.scalar
        def _(act):
            act.wait_ge(k_in, 48)
            for d in range(2):
                act.wait_ge(wl_done, d + 1)
                act.activation(sg[d][:, :], bank_cols(K, 1), ACT.Sigmoid, bias=w0(d)).then_inc(sg_done, 1)
                act.wait_ge(al_done, d + 1)
                act.activation(av[d][:, :], bank_cols(K, 0), ACT.Sigmoid, bias=a0(d)).then_inc(a_done, 1)
                if d == 0:
                    act.wait_ge(summed, 1)
                    act.activation(inv[:, :, :], K.ps[:, 0, 3, 0:2 * TOK].rearrange("p (t h) -> p t h", h=2),
                                   ACT.Sqrt, bias=K.epsc[:, 0:1]).then_inc(root, 1)
            act.wait_ge(spread, 1)
            for d in range(2):
                act.wait_ge(c_done, d + 1)
                for i, (src, sign) in enumerate(((cx[d], -1), (cc[d], -1), (cc[d], 1))):
                    if d:
                        act.wait_ge(used, (1, 2, 4)[i])
                    act.activation(ex[i][:, :], src[:, :], ACT.Exp, scale=sign * DECAY).then_inc(ex_done, 1)
                act.activation(R.pend[:, d, :], R.pend[:, d, :], ACT.Exp, scale=-DECAY).then_inc(ex_done, 1)
            act.wait_ge(g_done, 1)
            act.copy(R.gate[:, :], K.ps[:, 0, 0:2, :].rearrange("p b c -> p (b c)")).then_inc(gate_out, 1)

        @block.gpsimd
        def _(pool):
            pool.memset(one[:, :], 1.0).then_inc(one_set, 1)
            pool.wait_ge(one_set, 1)
            pool.memset(one[:, 0::CL], 0.0).then_inc(one_set, 1)
            pool.wait_ge(km_done, 2)
            pool.tensor_tensor(R.bonus[:, :], km[0][:, 0:SEQ], km[1][:, 0:SEQ], ALU.add).then_inc(km_sum, 1)
            pool.wait_ge(kk_done, 1)
            for d in range(2):
                pool.tensor_tensor(av[d][:, :], av[d][:, :], kk[:, :], ALU.mult).then_inc(akk_done, 1)

        @block.vector
        def _(dve):
            own = Chain(dve, d_own)
            dve.wait_ge(k_in, 48)
            own.link(dve.tensor_scalar(kk[:, :], k[:, :], k_k, None, ALU.mult))
            dve.tensor_tensor(kk2[:, :], kk[:, :], kk[:, :], ALU.mult).then_inc(kk2_done, 1)
            def running(d):
                dve.wait_ge(sg_done, d + 1)
                own.link(dve.tensor_tensor_scan(cc[d][:, :], one[:, :], sg[d][:, :], 0.0, ALU.mult, ALU.add))
                own.link(dve.tensor_copy(R.pend[:, d, :], chunked(cc[d][:, :])[:, :, CL - 1]))
                if d == 0:
                    dve.tensor_tensor(cx[d][:, :], cc[d][:, :], sg[d][:, :], ALU.subtract).then_inc(c_done, 1)
                else:
                    tot = R.pend[:, d, :].rearrange("p (c o) -> p c o", o=1).to_broadcast([P, NC, CL])
                    own.link(dve.tensor_tensor(chunked(cx[d][:, :]), tot, chunked(cc[d][:, :]), ALU.subtract))
                    dve.tensor_tensor(cc[d][:, :], cx[d][:, :], sg[d][:, :], ALU.add).then_inc(c_done, 1)

            def kmod(d):
                dve.wait_ge(a_done, d + 1)
                own.link(dve.tensor_scalar(km[d][:, :], av[d][:, :], -1.0, k_a, ALU.add, ALU.mult))
                dve.scalar_tensor_tensor(km[d][:, :], km[d][:, :], 1.0, k[:, :], ALU.add,
                                         ALU.mult).then_inc(km_done, 1)

            def scaled(d):
                dve.wait_ge(ex_done, 4 * d + 1)
                dve.tensor_tensor(R.ar[:, d, :, 0, :], in_tiles(ex[0][:, :]), in_tiles(kk[:, :]),
                                  ALU.mult).then_inc(used, 1)
                dve.wait_ge(ex_done, 4 * d + 2)
                dve.wait_ge(r_in, 16)
                dve.tensor_tensor(R.ar[:, d, :, 1, :], in_tiles(ex[1][:, :]), in_tiles(r[:, :]),
                                  ALU.mult).then_inc(used, 1)
                dve.wait_ge(ex_done, 4 * d + 3)
                dve.wait_ge(km_done, d + 1)
                dve.tensor_tensor(R.kappa[:, d, :], km[d][:, :], ex[2][:, :], ALU.mult).then_inc(used, 1)
                dve.wait_ge(akk_done, d + 1)
                dve.scalar_tensor_tensor(R.beta[:, d, :], av[d][:, :], -1.0, ex[2][:, :], ALU.mult,
                                         ALU.mult).then_inc(used, 1)
            dve.wait_ge(one_set, 2)
            running(0)
            kmod(0)
            dve.wait_ge(root, 1)
            dve.reciprocal(inv[:, :, :], inv[:, :, :]).then_inc(inverted, 1)
            dve.wait_ge(inverted, 1)
            dve.tensor_copy(fac, inv[:, :, :].rearrange("p t (h o) -> p t h o", o=1).to_broadcast(
                [P, TOK, 2, 64])).then_inc(fac_done, 1)
            running(1)
            kmod(1)
            dve.wait_ge(spread, 1)
            dve.tensor_tensor(kk[:, :], kk[:, :], bank_cols(K, 1), ALU.mult).then_inc(kk_done, 1)
            dve.wait_ge(kk_done, 1)
            scaled(0)
            dve.wait_ge(km_sum, 1)
            dve.scalar_tensor_tensor(R.bonus[:, :], r[:, 0:SEQ], r_k, R.bonus[:, :], ALU.mult,
                                     ALU.mult).then_inc(bk_done, 1)
            scaled(1)
            dve.wait_ge(bsum, 1)
            dve.wait_ge(v_in, 16)
            dve.tensor_tensor(R.bonus[:, :], K.ps[:, 1, 0:2, :].rearrange("p b c -> p (b c)"),
                              R.v[:, 0:SEQ], ALU.mult).then_inc(bonus_done, 1)
            dve.wait_ge(ex_done, 8)


def rwkv_chunks(K, p):
    nc = K.nc
    R = K.R
    t0 = [R.temp_at]

    def temp(name, shape):
        n = -(-4 * int(np.prod(shape[1:])) // 32) * 32
        t = K.place("rwc_" + name, shape, F32, at=t0[0])
        t0[0] += n
        assert t0[0] <= K.s_end, (name, t0[0] - K.s_end)
        return t
    TM = temp("tm", [P, 2, 5, P])
    AZ = temp("az", [P, 2, 4, P])
    SB = temp("sb", [P, 2, 2, 2, 2, P])
    SK = temp("sk", [P, 2, 2, 2, 2, P])
    M = temp("m", [P, 2, 4, P])
    X = temp("x", [P, 2, 4, 2, P])
    PX = temp("px", [P, 2, 4, P])
    TW = temp("tw", [P, 2, 4, P])
    pe_done = [K.sem(f"rwc_pe{s}") for s in range(2)]
    dve_done = [K.sem(f"rwc_dve{s}") for s in range(2)]
    act_done = [K.sem(f"rwc_act{s}") for s in range(2)]
    d_own = K.sem("rwc_dve_own")
    masked, turned_x = K.sem("rwc_masked"), [K.sem(f"rwc_x{s}") for s in range(2)]
    LV = 5
    M_STAGE, LEVEL0 = 3, 4
    TW_STAGE = LEVEL0 + 3 * LV - 1
    OUT_STAGE = TW_STAGE + 1
    STAGES = OUT_STAGE + 1

    def unit(t, d, hp):
        return slice(64 * hp, 64 * hp + 64), slice(t * P, (t + 1) * P)

    def eye_over(n):
        return K.eye[:, :].rearrange("p (o c) -> p o c", o=1).to_broadcast([P, n, P])

    def over_heads(m):
        return m.rearrange("p d (o c) -> p d o c", o=1).to_broadcast([P, 2, 2, P])

    def flip_d(m):
        return m[:, ::-1, :]

    def by_unit(x):
        return x.rearrange("p (d h) c -> p d h c", d=2)

    def pe_stage(pe, n, t, s):
        ps = K.ps[:, s]
        if n == 0:
            for d in range(2):
                pe.transpose(ps[:, 0, d * P:(d + 1) * P], R.ar[:, d, t, 0, :], K.eye[:, :])
                pe.transpose(ps[:, 0, (2 + d) * P:(3 + d) * P], R.beta[:, d, t * P:(t + 1) * P], K.eye[:, :])
                pe.transpose(ps[:, 1, d * P:(d + 1) * P], R.kappa[:, d, t * P:(t + 1) * P], K.eye[:, :])
            return pe.transpose(ps[:, 1, 2 * P:3 * P], R.v[:, t * P:(t + 1) * P], K.eye[:, :])
        if n in (1, 2):
            for d, hp in UNITS:
                q, tok = unit(t, d, hp)
                mm = pe.matmul(ps[:, 2 * (n - 1) + hp, d * 256:(d + 1) * 256], (R.beta, R.kappa)[n - 1][q, d, tok],
                               R.ar[q, d, t, :, :], start=True, stop=True)
            return mm
        if n == M_STAGE:
            for d, hp in UNITS:
                q, tok = unit(t, d, hp)
                pe.matmul(ps[:, hp, d * P:(d + 1) * P], R.ar[q, d, t, 0, :], R.beta[q, d, tok],
                          start=True, stop=True)
            for d, hp in UNITS:
                u = 2 * d + hp
                mm = pe.matmul(ps[:, 2, u * 64:(u + 1) * 64], SK[:, s, hp, d, 0, :],
                               TM[:, s, 4, 64 * hp:64 * hp + 64], start=True, stop=True)
            return mm
        if n < TW_STAGE:
            for u in range(4):
                lhsT, rhs = ((M[:, s, u, :], X[:, s, u, 1, :]), (X[:, s, u, 0, :], PX[:, s, u, :]),
                             (PX[:, s, u, :], X[:, s, u, 0, :]))[(n - LEVEL0) % 3]
                mm = pe.matmul(ps[:, (n - LEVEL0) % 3, u * P:(u + 1) * P], lhsT, rhs, start=True, stop=True)
            return mm
        if n == TW_STAGE:
            for u in range(4):
                mm = pe.matmul(ps[:, 3, u * P:(u + 1) * P], X[:, s, u, 1, :], AZ[:, s, u, :],
                               start=True, stop=True)
            return mm
        for d, hp in UNITS:
            u = 2 * d + hp
            hq = slice(64 * hp, 64 * hp + 64)
            for c in range(2):
                cq = slice(64 * c, 64 * c + 64)
                pe.matmul(ps[hq, c, d * P:d * P + 64], TW[cq, s, u, 0:64], TM[cq, s, d, hq],
                          start=True, stop=True)
                pe.matmul(ps[hq, c, d * P + 64:(d + 1) * P], TM[cq, s, 2 + d, hq], TM[cq, s, 4, hq],
                          start=True, stop=False)
                mm = pe.matmul(ps[hq, c, d * P + 64:(d + 1) * P], TM[cq, s, d, hq], TW[cq, s, u, 64:128],
                               start=False, stop=True)
            if t < SEQ // P:
                mm = pe.matmul(ps[hq, 2, d * P:(d + 1) * P], TW[:, s, u, 0:64], SB[:, s, hp, d, 1, :],
                               start=True, stop=True)
        if t < SEQ // P:
            for hp in range(2):
                hq = slice(64 * hp, 64 * hp + 64)
                for d in range(2):
                    pe.matmul(ps[hq, 3, 0:P], TM[:, s, 4, hq], SK[:, s, hp, d, 1, :], start=d == 0, stop=False)
                    mm = pe.matmul(ps[hq, 3, 0:P], TW[:, s, 2 * d + hp, 64:128], SB[:, s, hp, d, 1, :],
                                   start=False, stop=d == 1)
        return mm

    def act_stage(act, n, t, s):
        ps = K.ps[:, s]
        if n == 0:
            act.copy(AZ[:, s, :, 0:64], ps[:, 0, 0:256].rearrange("p (u c) -> p u c", u=4))
            act.copy(TM[:, s, 0:2, :], ps[:, 0, 256:512].rearrange("p (u c) -> p u c", u=2))
            return act.copy(TM[:, s, 2:5, :], ps[:, 1, 0:384].rearrange("p (u c) -> p u c", u=3))
        if n == M_STAGE:
            return act.copy(AZ[:, s, :, 64:128], ps[:, 2, 0:256].rearrange("p (u c) -> p u c", u=4))
        if n == TW_STAGE:
            return act.copy(TW[:, s, :, :], ps[:, 3, :].rearrange("p (u c) -> p u c", u=4))
        if n == OUT_STAGE and t < SEQ // P:
            return act.copy(R.Y[:, t * P:(t + 1) * P], ps[:, 3, 0:P])
        return None

    def dve_stage(dve, own, n, t, s):
        ps = K.ps[:, s]
        if n in (1, 2):
            for hp in range(2):
                ins = dve.tensor_tensor((SB, SK)[n - 1][:, s, hp, :, :, :],
                                        ps[:, 2 * (n - 1) + hp, :].rearrange("p (d m c) -> p d m c", d=2, m=2),
                                        R.mask[:, :, :, :], ALU.mult)
            return ins
        if n == M_STAGE:
            own.link(dve.tensor_tensor(by_unit(M[:, s]), ps[:, 0:2, 0:256].rearrange("p h (d c) -> p d h c", d=2),
                                       over_heads(flip_d(R.mask[:, :, 0, :])), ALU.mult))
            own.link(dve.tensor_tensor(by_unit(X[:, s, :, 0, :]), by_unit(M[:, s]),
                                       over_heads(flip_d(R.level[:, 0, :, :])), ALU.mult))
            return dve.tensor_tensor(X[:, s, :, 0, :], X[:, s, :, 0, :], eye_over(4), ALU.add)
        if LEVEL0 <= n < TW_STAGE:
            j, part = (n - LEVEL0) // 3, (n - LEVEL0) % 3
            got = ps[:, part, :].rearrange("p (u c) -> p u c", u=4)
            if part == 0:
                return dve.tensor_tensor(by_unit(PX[:, s]), by_unit(got), over_heads(R.level[:, 1 + j, :, :]),
                                         ALU.mult)
            x = X[:, s, :, 2 - part, :]
            return dve.tensor_tensor(x, x, got, ALU.add)
        if n == OUT_STAGE:
            c0 = 2 * t
            for d in range(2):
                gh = ps[:, 0:2, d * P:(d + 1) * P]
                dve.tensor_tensor(R.G[:, d, c0:c0 + 2, :], gh[:, :, 0:64],
                                  K.eye2[:, :].rearrange("p (o c) -> p o c", o=1).to_broadcast([P, 2, 64]), ALU.add)
                ins = dve.tensor_tensor(R.HP[:, d, c0:c0 + 2, :], gh[:, :, 64:128],
                                        R.pend[:, d, c0:c0 + 2].rearrange("p (c o) -> p c o", o=1)
                                        .to_broadcast([P, 2, 64]), ALU.mult)
            if t < SEQ // P:
                ins = dve.tensor_tensor(R.Q[:, :, t * P:(t + 1) * P],
                                        ps[:, 2, 0:256].rearrange("p (d c) -> p d c", d=2),
                                        R.ar[:, :, t, 1, :], ALU.add)
            return ins
        return None

    on_act = lambda n, t: n in (0, M_STAGE, TW_STAGE) or (n == OUT_STAGE and t < SEQ // P)
    on_dve = lambda n, t: n in (1, 2, M_STAGE, OUT_STAGE) or LEVEL0 <= n < TW_STAGE
    groups, n = [], 0
    while n < STAGES:
        size = 2 if n == 1 or (LEVEL0 <= n < TW_STAGE - 1 and (n - LEVEL0) % 3 == 1) else 1
        groups.append(range(n, n + size))
        n += size
    steps = [(n, t, s) for pair in range(TOK // 2) for group in groups
             for s, t in ((0, 2 * pair), (1, 2 * pair + 1)) for n in group]

    def before(n, t, s):
        past = [(m, u) for m, u, q in steps if q == s]
        past = past[:past.index((n, t))]
        return sum(on_act(*x) for x in past), sum(on_dve(*x) for x in past)

    def runs_ahead(n):
        return n == 2 or LEVEL0 < n < TW_STAGE and (n - LEVEL0) % 3 in (0, 2)

    with nc.Block() as block:
        @block.gpsimd
        def _(pool):
            for t in range(TOK):
                s = t % 2
                x = X[:, s, :, 1, :]
                sb = SB[:, s, :, :, 0, :].rearrange("p h d c -> p d h c")
                pool.wait_ge(dve_done[s], before(2, t, s)[1])
                pool.tensor_tensor(by_unit(x), sb, over_heads(R.level[:, 0, :, :]), ALU.mult).then_inc(masked, 1)
                pool.wait_ge(masked, t + 1)
                pool.tensor_tensor(x, x, eye_over(4), ALU.add).then_inc(turned_x[s], 1)

        @block.tensor
        def _(pe):
            for n, t, s in steps:
                na, nd = before(n, t, s)
                nd -= runs_ahead(n)
                if na:
                    pe.wait_ge(act_done[s], na)
                if nd:
                    pe.wait_ge(dve_done[s], nd)
                if n == LEVEL0:
                    pe.wait_ge(turned_x[s], t // 2 + 1)
                pe_stage(pe, n, t, s).then_inc(pe_done[s], 1)

        @block.scalar
        def _(act):
            for n, t, s in steps:
                if on_act(n, t):
                    act.wait_ge(pe_done[s], STAGES * (t // 2) + n + 1)
                    act_stage(act, n, t, s).then_inc(act_done[s], 1)

        @block.vector
        def _(dve):
            own = Chain(dve, d_own)
            for n, t, s in steps:
                if on_dve(n, t):
                    nd = before(n, t, s)[1]
                    dve.wait_ge(pe_done[s], STAGES * (t // 2) + n + 1)
                    if nd:
                        dve.wait_ge(dve_done[s], nd)
                    dve_stage(dve, own, n, t, s).then_inc(dve_done[s], 1)


def rwkv_scan(K, p):
    nc = K.nc
    R = K.R
    at = [R.temp_at]

    def temp(name, shape):
        t = K.place("rws_" + name, shape, F32, at=at[0])
        at[0] += -(-4 * int(np.prod(shape[1:])) // 32) * 32
        assert at[0] <= K.s_end
        return t
    S = temp("s", [P, 2, NC, CL])
    sq = temp("sq", [P, SEQ])
    fac = temp("fac", [P, 8, 2, 64])
    dev = temp("dev", [P, 8, 2])
    eps = temp("gn_eps", [P, 1])
    order = [list(range(NL, NC)) + list(range(NL)), list(range(NC - 1, NL - 1, -1)) + list(range(NL - 1, -1, -1))]
    stepped = [K.sem("rws_step0"), K.sem("rws_step1")]
    moved = [K.sem("rws_move0"), K.sem("rws_move1")]
    (y_done, added, mean_done, centred, sq_done, var_done, root, inverted, fac_done, spread, own_s, fin, stored,
     eps_set) = [K.sem(f"rws_{n}") for n in ("y", "added", "mean", "centred", "sq", "var", "root", "inverted", "fac",
                                            "spread", "dve_own", "fin", "stored", "eps")]
    half = lambda i: slice(512 * i, 512 * (i + 1))
    with nc.Block() as block:
        @block.gpsimd
        def _(pool):
            pool.memset(eps[:, :], 64e-5).then_inc(eps_set, 1)

        @block.tensor
        def _(pe):
            def y_part(n, d):
                c = order[d][n]
                for hp in range(2):
                    q = slice(64 * hp, 64 * hp + 64)
                    mm = pe.matmul(K.ps[q, 1, 2 * d + c // 8, (c % 8) * 64:(c % 8) * 64 + 64], S[q, d, n, :],
                                   R.Q[q, d, c * 64:(c + 1) * 64], start=True, stop=True)
                return mm
            for n in range(1, NC):
                for d in range(2):
                    c = order[d][n]
                    pe.wait_ge(moved[d], n)
                    if n < NC - 1:
                        for hp in range(2):
                            q = slice(64 * hp, 64 * hp + 64)
                            mm = pe.matmul(K.ps[q, 0, d, 0:64], R.G[q, d, c, :], S[q, d, n, :], start=True,
                                           stop=True)
                        mm.then_inc(stepped[d], 1)
                if n > NC - NL - 1:
                    for d in range(2):
                        mm = y_part(n, d)
            mm.then_inc(y_done, 1)
            for i in range(2):
                pe.wait_ge(added, i + 1)
                pe.matmul(K.ps[:, 0, 2 + i, :], R.hones[:, :], R.Y[:, half(i)], start=True,
                          stop=True).then_inc(mean_done, 1)
            for i in range(2):
                pe.wait_ge(sq_done, i + 1)
                for m in range(4 * i, 4 * i + 4):
                    mm = pe.matmul(K.ps[:, 0, i, 2 * m:2 * m + 2], sq[:, m * P:(m + 1) * P], R.hones[:, 0::64],
                                   start=True, stop=True)
                mm.then_inc(var_done, 1)
            for i in range(2):
                pe.wait_ge(fac_done, i + 1)
                for m in range(4 * i, 4 * i + 4):
                    mm = pe.matmul(K.ps[:, 1, 2 + i, (m % 4) * P:(m % 4 + 1) * P],
                                   fac[:, m, :, :].rearrange("p h d -> p (h d)"), K.eye[:, :], start=True, stop=True)
                mm.then_inc(spread, 1)

        @block.vector
        def _(dve):
            own = Chain(dve, own_s)
            for d in range(2):
                dve.tensor_copy(S[:, d, 1, :], R.HP[:, d, order[d][0], :]).then_inc(moved[d], 1)
            for n in range(1, NC - 1):
                for d in range(2):
                    c = order[d][n]
                    dve.wait_ge(stepped[d], n)
                    dve.scalar_tensor_tensor(S[:, d, n + 1, :], K.ps[:, 0, d, 0:64], R.pend[:, d, c:c + 1],
                                             R.HP[:, d, c, :], ALU.mult, ALU.add).then_inc(moved[d], 1)
            dve.wait_ge(y_done, 1)
            for i in range(2):
                own.link(dve.tensor_tensor(R.Y[:, half(i)], R.Y[:, half(i)], K.ps[:, 1, i, :], ALU.add))
                dve.tensor_tensor(R.Y[:, half(i)], R.Y[:, half(i)], K.ps[:, 1, 2 + i, :], ALU.add).then_inc(added, 1)
            dve.wait_ge(added, 2)
            for i in range(2):
                dve.wait_ge(mean_done, i + 1)
                dve.scalar_tensor_tensor(R.Y[:, half(i)], K.ps[:, 0, 2 + i, :], -1.0 / 64, R.Y[:, half(i)],
                                         ALU.mult, ALU.add).then_inc(centred, 1)
            dve.wait_ge(centred, 2)
            for i in range(2):
                dve.wait_ge(root, i + 1)
                v = dev[:, 4 * i:4 * i + 4, :]
                dve.reciprocal(v, v).then_inc(inverted, 1)
                dve.wait_ge(inverted, i + 1)
                dve.tensor_copy(fac[:, 4 * i:4 * i + 4, :, :], v.rearrange("p t (h o) -> p t h o", o=1).to_broadcast(
                    [P, 4, 2, 64])).then_inc(fac_done, 1)
            for i in range(2):
                y = R.Y[:, half(i)]
                dve.wait_ge(spread, i + 1)
                own.link(dve.scalar_tensor_tensor(y, y, R.vec[:, 7:8], K.ps[:, 1, 2 + i, :], ALU.mult, ALU.mult))
                own.link(dve.scalar_tensor_tensor(y, y, R.vec[:, 8:9], R.bonus[:, half(i)], ALU.add, ALU.add))
                dve.tensor_tensor(y, y, R.gate[:, half(i)], ALU.mult).then_inc(fin, 1)

        @block.scalar
        def _(act):
            act.wait_ge(eps_set, 1)
            for i in range(2):
                act.wait_ge(centred, i + 1)
                act.activation(sq[:, half(i)], R.Y[:, half(i)], ACT.Square).then_inc(sq_done, 1)
            for i in range(2):
                act.wait_ge(var_done, i + 1)
                act.activation(dev[:, 4 * i:4 * i + 4, :],
                               K.ps[:, 0, i, 8 * i:8 * i + 8].rearrange("p (t h) -> p t h", h=2), ACT.Sqrt,
                               bias=eps[:, 0:1], scale=1.0 / 64).then_inc(root, 1)

        @block.sync
        def _(sp):
            for i in range(2):
                sp.wait_ge(fin, i + 1)
                sp.dma_start(K.y[4 + p][:, half(i)], R.Y[:, half(i)]).then_inc(stored, 16)
            sp.wait_ge(stored, 32)


def store_phase(K):
    nc = K.nc
    stored = K.sem("stored")
    with nc.Block() as block:
        @block.sync
        def _(sp):
            for k in range(KT):
                sp.dma_start(K.out[k], K.h[:, k, 0:K.out.shape[2]]).then_inc(stored, 16)
            sp.wait_ge(stored, 16 * KT)


LAT_COLS, LAT_SEGS = COLS[:2], SEGS[:1]


def build(nc, a, out):
    K = Kernel(nc, a, out)
    K.z = nc.dram_tensor("z_scratch", (ZT, P, NT), F32, kind="Internal").ap()
    K.y = nc.dram_tensor("y_scratch", (KT, P, SEQ), F32, kind="Internal").ap()

    def per(n, phase):
        def run():
            with nc.Fori(0, n) as i:
                phase(i)
                K.phase_over()
        return run

    phases = [lambda: setup_phase(K),
              lambda: ab_in_phase(K),
              lambda: pool_fourier_phase(K),
              lambda: out_phase(K, "about", a["ab_out"], 0, COLS, SEGS),
              lambda: ffn_phase(K, 0, COLS, SEGS),
              lambda: cd_in_phase(K),
              per(2, lambda g: attention_phase(K, g)),
              ] + rwkv_phases(K, per) + [
              lambda: out_phase(K, "cdout", a["cd_out"], 1, LAT_COLS, LAT_SEGS, y_dram=K.y),
              lambda: ffn_phase(K, 1, LAT_COLS, LAT_SEGS, out)]
    for f in phases[:STOP]:
        f()
        if K.sems:
            K.phase_over()
    if STOP is not None:
        store_phase(K)


def rwkv_phases(K, per):
    def pair(p):
        rwkv_prepare(K, p)
        K.phase_over()
        rwkv_chunks(K, p)
        K.phase_over()
        rwkv_scan(K, p)
    return [per(4, pair)]


def _tiles(v):
    return np.ascontiguousarray(v.reshape(-1, P).T)


def _blocks(w):
    k, m = w.shape
    return w.reshape(k // P, P, m // P, P).transpose(2, 1, 0, 3).reshape(m // P, P, k)


def _layout(i):
    f = {n: np.asarray(v) for n, v in i.items()}
    arr = {}
    x = np.concatenate([f["x"][0].T, f["ctx"][0].T], axis=1)
    arr["x"] = x.reshape(KT, P, NT)
    arr["ada"] = np.concatenate([
        f["ada_w"][l].reshape(KT, P, 12, 512).transpose(2, 1, 0, 3).reshape(12, P, KT * 512) for l in range(2)])
    cond = np.stack([_tiles(f["c"][0]), _tiles(f["c_ctx"])], axis=2).reshape(P, 16)
    ada_b = np.concatenate([_tiles(f["ada_b"][l]) for l in range(2)], axis=1)
    norm = np.concatenate([_tiles(f[n][l]) for l in range(2) for n in ("norm1", "norm2")], axis=1)
    conv = np.concatenate([_tiles(f["ffn_conv"][l, t]) for l in range(2) for t in range(3)], axis=1)
    edge = np.ones((4, 2, 8), np.float32)
    for wi, w in enumerate((2, 4, 8, 16)):
        for e in range(8):
            edge[wi, 0, e] = w / (min(e, w // 2) + w - w // 2)
            edge[wi, 1, e] = w / (w // 2 + min(w - w // 2, 8 - e))
    two = lambda v: np.concatenate([v, v])[:, None]
    rconv = np.concatenate([_tiles(f["rwkv_conv"][0, t]) for t in range(3)], axis=1)
    cols = {"cond": cond, "ada_b": ada_b, "norm": norm, "conv": conv, "pool_scale": _tiles(f["pool_scale"][0]),
            "edge": np.broadcast_to(edge.reshape(1, -1), (P, 64)), "qn": two(f["q_norm"][0]),
            "kn": two(f["k_norm"][0]), "rconv": rconv,
            "sink": np.broadcast_to(f["attn_sink"][0], (P, 8))}
    arr["small"] = np.concatenate([cols[n] for n, _ in _SMALL], axis=1)
    arr["ab_in"] = _blocks(f["ab_w_in"][0])
    arr["ab_out"] = _blocks(f["ab_w_out"][0])
    big = []
    for half in range(2):
        w = np.zeros((384, 384), np.float32)
        w[:192, :192] = f["pool_w"][0, 2 * half]
        w[192:, 192:] = f["pool_w"][0, 2 * half + 1]
        for m, ks in ((0, (0, 1)), (1, (0, 1, 2)), (2, (1, 2))):
            big += [w[k * P:(k + 1) * P, m * P:(m + 1) * P] for k in ks]
    arr["pool_w"] = np.stack(big, axis=1)
    ch = 2 * np.pi * (np.outer(np.arange(256), np.arange(256)) % 256) / 256
    as_k = lambda w: w.reshape(2, P, 256).transpose(1, 0, 2)
    arr["dft_ch"] = np.stack([as_k(np.cos(ch).astype(np.float32)), as_k(-np.sin(ch).astype(np.float32)),
                              as_k(f["fourier_w"][0])], axis=1)
    for name, n in (("dft_tok", SEQ), ("dft_ctx", CTX)):
        ang = 2 * np.pi * (np.outer(np.arange(n), np.arange(n)) % n) / n
        s = 1 / np.sqrt(n * 256)
        t = np.stack([np.cos(ang) * s, np.sin(ang) * s]).astype(np.float32)
        t = t.reshape(2, n // P, P, n).transpose(1, 2, 0, 3)
        arr[name] = t if n == SEQ else t.transpose(1, 0, 2, 3)
    ffn = []
    for l in range(2):
        up, down = _blocks(f["ffn_up"][l]), f["ffn_down"][l].reshape(FT, P, D)
        ups = [[up[2 * g], up[FT + 2 * g], up[2 * g + 1], up[FT + 2 * g + 1]] for g in range(GROUPS)]
        seq = ups[0] + ups[1] + [down[0], down[1]]
        for g in range(2, GROUPS):
            seq += ups[g] + [down[2 * g - 2], down[2 * g - 1]]
        seq += [down[FT - 2], down[FT - 1]]
        ffn.append(np.stack(seq))
    arr["ffn"] = np.stack(ffn)
    arr["cd_in"] = _blocks(f["cd_w_in"][0])
    arr["cd_out"] = _blocks(f["cd_w_out"][0])
    _constants(arr, f)
    return {n: np.ascontiguousarray(v, dtype=np.float32) for n, v in arr.items()}


OUT_COLS = SEQ
STOP = None


def _constants(arr, f):
    half = 32
    inv = (np.float32(10000.0) ** (-np.arange(0, half, 2, dtype=np.float32) / half)).astype(np.float32)
    t = np.arange(SEQ)
    pos = np.stack([t // GRID_W, t % GRID_W]).astype(np.float32)
    ang = np.concatenate([np.concatenate([pos[s][None, :] * inv[:, None]] * 2) for s in range(2)])
    ang = np.concatenate([ang, ang]).astype(np.float32)
    arr["rope"] = np.stack([np.cos(ang), np.sin(ang)], axis=1)
    d = np.arange(P)
    head = (d[:, None] // 64 == d[None, :] // 64).astype(np.float32)
    rot = np.zeros((P, P), np.float32)
    for m in range(P):
        if m % 32 < 16:
            rot[m + 16, m] = -1.0
        else:
            rot[m - 16, m] = 1.0
    j, r = np.arange(384)[None, :], np.arange(P)[:, None]
    band = np.where((j >= r) & (j <= r + 256), 0.0, -1e30).astype(np.float32)
    row = np.zeros((P, P), np.float32)
    row[:8, :4] = np.concatenate([np.eye(4), np.eye(4)])
    arr["att_aux"] = np.concatenate([head, rot, row, band], axis=1)
    ch, sub = d // CL, np.arange(P)
    mask = np.zeros((P, 2, 2, P), np.float32)
    level = np.zeros((P, 6, 2, P), np.float32)
    src, dst = sub[:, None], sub[None, :]
    same = (src // CL) == (dst // CL)
    for way in range(2):
        before = src < dst if way == 0 else src > dst
        mask[:, way, 0] = same & before
        mask[:, way, 1] = same & (before | (src == dst))
        for i in range(6):
            b = 1 << i
            near = (src // (2 * b)) == (dst // (2 * b))
            level[:, i, way] = near & ((src // b) != (dst // b)) & before
    arr["rw_mask"], arr["rw_level"] = mask, level
    col = lambda v: v.reshape(4, P)
    zero = np.zeros(512, np.float32)
    arr["rw_vec"] = np.stack([col(v) for v in (
        f["rwkv_w0"][0, 0], f["rwkv_w0"][0, 1], f["rwkv_a0"][0, 0], f["rwkv_a0"][0, 1], f["rwkv_k_k"][0],
        f["rwkv_k_a"][0], f["rwkv_r_k"][0].reshape(-1), f["rwkv_lnx_w"][0], f["rwkv_lnx_b"][0], zero)], axis=2)
    lora = [np.concatenate([f["rwkv_w2"][0, way], f["rwkv_a2"][0, way]]) for way in range(2)]
    lora.append(f["rwkv_g_up"][0])
    arr["rw_mats"] = np.stack([m.reshape(P, 4, P) for m in lora]).transpose(2, 1, 0, 3).reshape(4, P, 3 * P)
    arr["sink"] = np.broadcast_to(f["attn_sink"][0].reshape(2, 1, 4), (2, P, 4))


def kernel(**inputs):
    import concourse.bacc as bacc
    from concourse.bass_utils import run_bass_kernel_spmd

    arrays = _layout(inputs)
    nc = bacc.Bacc("TRN2", target_bir_lowering=False, num_devices=1)
    a = {n: nc.dram_tensor(f"in_{n}", v.shape, F32, kind="ExternalInput").ap() for n, v in arrays.items()}
    out = nc.dram_tensor("out", (KT, P, OUT_COLS), F32, kind="ExternalOutput").ap()
    build(nc, a, out)
    r = run_bass_kernel_spmd(nc, [{f"in_{n}": v for n, v in arrays.items()}], core_ids=[0])
    return r.results[0]["out"].reshape(D, OUT_COLS).T[None]
```
